# Optimizing a Trainium2 kernel written in Bass

```python
import jax
import jax.numpy as jnp
from jax import lax
import numpy as np
import math
import jax, jax.numpy as jnp

D_MODEL = 1024
BATCH = 1
SEQ = 256
DEPTH = 2

N_A_LAYERS = DEPTH // 2
N_B_LAYERS = DEPTH - N_A_LAYERS
Q_BLOCK = 128
NEG_INF = -1e30
NORM_EPS = 1e-6

NSA_HEADS = 16
NSA_GROUPS = 4
NSA_HPG = NSA_HEADS // NSA_GROUPS
NSA_DH = 64
CMP_BLOCK = 32
CMP_STRIDE = 16
CMP_HIDDEN = 256
SLC_BLOCK = 64
SLC_TOP = 16
WINDOW = 512
FORCE_SCORE = 1e4
NSA_IN_WIDTH = NSA_HEADS * NSA_DH + 6 * NSA_GROUPS * NSA_DH + 3 * NSA_HEADS

MLA_HEADS = 8
QK_NOPE = 128
QK_ROPE = 64
MLA_V = 128
Q_LORA = 384
KV_LORA = 256
ROPE_THETA = 10000.0

FFN_HIDDEN = -(-8 * D_MODEL // (3 * 256)) * 256


def rms_norm(x, g):
    xf = x.astype(jnp.float32)
    y = xf * lax.rsqrt(jnp.mean(xf * xf, axis=-1, keepdims=True) + NORM_EPS)
    return (y * g.astype(jnp.float32)).astype(x.dtype)

def masked_softmax(s, mask):
    p = jax.nn.softmax(jnp.where(mask, s, NEG_INF), axis=-1)
    return jnp.where(mask, p, 0.0)

def alibi_slopes(n):
    return 2.0 ** (-8.0 * jnp.arange(1, n + 1, dtype=jnp.float32) / n)

def rope_tables(T):
    inv = ROPE_THETA ** (-jnp.arange(0, QK_ROPE, 2, dtype=jnp.float32) / QK_ROPE)
    ang = jnp.arange(T, dtype=jnp.float32)[:, None] * inv[None, :]
    return jnp.cos(ang), jnp.sin(ang)

def apply_rope(x, cos, sin):
    c = cos[None, :, None, :].astype(x.dtype)
    s = sin[None, :, None, :].astype(x.dtype)
    x1, x2 = jnp.split(x, 2, axis=-1)
    return jnp.concatenate([x1 * c - x2 * s, x1 * s + x2 * c], axis=-1)

def swiglu(h, w_gate_up, w_down):
    gate, up = jnp.split(h @ w_gate_up, 2, axis=-1)
    return (jax.nn.silu(gate) * up) @ w_down

_gather_bg = jax.vmap(jax.vmap(lambda src, idx: src[idx]))

def nsa_mixer(h, w_in, q_norm, kcmp_norm, kslc_norm, kwin_norm, pos_k, pos_v,
              k_w1, k_b1, k_w2, v_w1, v_b1, v_w2, w_out):
    B, T, _ = h.shape
    G, HG, DH = NSA_GROUPS, NSA_HPG, NSA_DH
    f32 = jnp.float32
    qw, kvw = NSA_HEADS * DH, G * DH
    cuts = [qw + i * kvw for i in range(7)]
    parts = jnp.split(h @ w_in, cuts, axis=-1)
    q = rms_norm(parts[0].reshape(B, T, G, HG, DH), q_norm)
    kc, vc, ksl, vsl, kw, vw = [a.reshape(B, T, G, DH) for a in parts[1:7]]
    gates = jax.nn.sigmoid(parts[7].astype(f32)).astype(h.dtype).reshape(B, T, G, HG, 3)

    n_cmp = (T - CMP_BLOCK) // CMP_STRIDE + 1
    cmp_j = jnp.arange(n_cmp)
    cmp_idx = cmp_j[:, None] * CMP_STRIDE + jnp.arange(CMP_BLOCK)[None, :]

    def compress(a, pe, w1, b1, w2):
        blk = a[:, cmp_idx] + pe[:, None, :].astype(a.dtype)
        blk = jnp.swapaxes(blk, 2, 3).reshape(B, n_cmp, G, CMP_BLOCK * DH)
        return jax.nn.gelu(blk @ w1 + b1) @ w2

    k_cmp = rms_norm(compress(kc, pos_k, k_w1, k_b1, k_w2), kcmp_norm)
    v_cmp = compress(vc, pos_v, v_w1, v_b1, v_w2)
    k_sel_src = jnp.swapaxes(rms_norm(ksl, kslc_norm), 1, 2)
    v_sel_src = jnp.swapaxes(vsl, 1, 2)
    pad = ((0, 0), (WINDOW, 0), (0, 0), (0, 0))
    kw_pad = jnp.pad(rms_norm(kw, kwin_norm), pad)
    vw_pad = jnp.pad(vw, pad)

    slopes = alibi_slopes(NSA_HEADS).reshape(G, HG)[:, :, None, None]
    scale = DH ** -0.5
    n_slc = T // SLC_BLOCK
    n_top = min(SLC_TOP, n_slc)
    n_sel = n_top * SLC_BLOCK
    cmp_end = cmp_j * CMP_STRIDE + CMP_BLOCK - 1
    cmp_mid = (cmp_j * CMP_STRIDE).astype(f32) + 0.5 * (CMP_BLOCK - 1)
    slc_i = jnp.arange(n_slc)
    overlap = ((cmp_j[:, None] * CMP_STRIDE <= slc_i[None, :] * SLC_BLOCK + SLC_BLOCK - 1)
               & (cmp_end[:, None] >= slc_i[None, :] * SLC_BLOCK)).astype(f32)
    win_off = jnp.arange(WINDOW + Q_BLOCK)
    in_blk = jnp.arange(SLC_BLOCK)

    def block(s0):
        t = s0 + jnp.arange(Q_BLOCK)
        tf = t.astype(f32)
        qb = lax.dynamic_slice_in_dim(q, s0, Q_BLOCK, axis=1)
        gb = lax.dynamic_slice_in_dim(gates, s0, Q_BLOCK, axis=1)
        s_c = (jnp.einsum('bqghd,bjgd->bghqj', qb, k_cmp).astype(f32) * scale
               - slopes * (tf[:, None] - cmp_mid[None, :]))
        p_c = masked_softmax(s_c, cmp_end[None, :] <= t[:, None])
        o_c = jnp.einsum('bghqj,bjgd->bqghd', p_c.astype(v_cmp.dtype), v_cmp)
        imp = jnp.einsum('bghqj,ji->bgqi', p_c, overlap)
        cur = (t // SLC_BLOCK)[:, None]
        valid = slc_i[None, :] * SLC_BLOCK <= t[:, None]
        forced = (slc_i[None, :] == 0) | (slc_i[None, :] == cur) | (slc_i[None, :] == cur - 1)
        score = jnp.where(valid, imp + jnp.where(forced, FORCE_SCORE, 0.0), -1.0)
        _, top = lax.top_k(score, n_top)
        sel_pos = (top[..., None] * SLC_BLOCK + in_blk).reshape(B, G, Q_BLOCK * n_sel)
        k_s = _gather_bg(k_sel_src, sel_pos).reshape(B, G, Q_BLOCK, n_sel, DH)
        v_s = _gather_bg(v_sel_src, sel_pos).reshape(B, G, Q_BLOCK, n_sel, DH)
        sel_pos = sel_pos.reshape(B, G, 1, Q_BLOCK, n_sel)
        s_s = (jnp.einsum('bqghd,bgqnd->bghqn', qb, k_s).astype(f32) * scale
               - slopes * (tf[:, None] - sel_pos.astype(f32)))
        p_s = masked_softmax(s_s, sel_pos <= t[:, None])
        o_s = jnp.einsum('bghqn,bgqnd->bqghd', p_s.astype(v_s.dtype), v_s)
        k_w = lax.dynamic_slice_in_dim(kw_pad, s0, WINDOW + Q_BLOCK, axis=1)
        v_w = lax.dynamic_slice_in_dim(vw_pad, s0, WINDOW + Q_BLOCK, axis=1)
        kpos = s0 - WINDOW + win_off
        dist = t[:, None] - kpos[None, :]
        s_w = (jnp.einsum('bqghd,bkgd->bghqk', qb, k_w).astype(f32) * scale
               - slopes * dist.astype(f32))
        p_w = masked_softmax(s_w, (dist >= 0) & (dist < WINDOW) & (kpos[None, :] >= 0))
        o_w = jnp.einsum('bghqk,bkgd->bqghd', p_w.astype(v_w.dtype), v_w)
        o = gb[..., 0:1] * o_c + gb[..., 1:2] * o_s + gb[..., 2:3] * o_w
        return o.reshape(B, Q_BLOCK, NSA_HEADS * DH)

    starts = jnp.arange(T // Q_BLOCK, dtype=jnp.int32) * Q_BLOCK
    o = jnp.swapaxes(lax.map(block, starts), 0, 1).reshape(B, T, NSA_HEADS * DH)
    return o @ w_out

def shared_mla_kv(x, kv_norm, kv_w_a, kv_c_norm, kv_w_b, kv_k_norm, cos, sin):
    B, T, _ = x.shape
    kv_a = rms_norm(x, kv_norm) @ kv_w_a
    c_kv = rms_norm(kv_a[..., :KV_LORA], kv_c_norm)
    k_pe = kv_a[..., KV_LORA:]
    kv = (c_kv @ kv_w_b).reshape(B, T, MLA_HEADS, QK_NOPE + MLA_V)
    k = jnp.concatenate([kv[..., :QK_NOPE],
                         jnp.broadcast_to(k_pe[:, :, None, :], (B, T, MLA_HEADS, QK_ROPE))], axis=-1)
    k = rms_norm(k, kv_k_norm)
    k = jnp.concatenate([k[..., :QK_NOPE], apply_rope(k[..., QK_NOPE:], cos, sin)], axis=-1)
    return k, kv[..., QK_NOPE:]

def mla_mixer(h, k, v, w_q_a, q_a_norm, w_q_b, q_norm, w_out, cos, sin):
    B, T, _ = h.shape
    q = (rms_norm(h @ w_q_a, q_a_norm) @ w_q_b).reshape(B, T, MLA_HEADS, QK_NOPE + QK_ROPE)
    q = rms_norm(q, q_norm)
    q = jnp.concatenate([q[..., :QK_NOPE], apply_rope(q[..., QK_NOPE:], cos, sin)], axis=-1)
    scale = (QK_NOPE + QK_ROPE) ** -0.5
    kpos = jnp.arange(T)

    def block(s0):
        t = s0 + jnp.arange(Q_BLOCK)
        qb = lax.dynamic_slice_in_dim(q, s0, Q_BLOCK, axis=1)
        s = jnp.einsum('bqhd,bkhd->bhqk', qb, k).astype(jnp.float32) * scale
        p = masked_softmax(s, kpos[None, :] <= t[:, None])
        o = jnp.einsum('bhqk,bkhd->bqhd', p.astype(v.dtype), v)
        return o.reshape(B, Q_BLOCK, MLA_HEADS * MLA_V)

    starts = jnp.arange(T // Q_BLOCK, dtype=jnp.int32) * Q_BLOCK
    o = jnp.swapaxes(lax.map(block, starts), 0, 1).reshape(B, T, MLA_HEADS * MLA_V)
    return o @ w_out

def first_inputs(seed: int = 0) -> dict:
    key = jax.random.key(seed)
    ks = iter(jax.random.split(key, 32))
    f32 = jnp.float32

    def w(shape, fan_in):
        return jax.random.normal(next(ks), shape, f32) * (fan_in ** -0.5)

    def gain(shape):
        return 1.0 + 0.02 * jax.random.normal(next(ks), shape, f32)

    def small(shape, s):
        return s * jax.random.normal(next(ks), shape, f32)

    NA, NB, D = N_A_LAYERS, N_B_LAYERS, D_MODEL
    flat = CMP_BLOCK * NSA_DH
    return {
        'x': jax.random.normal(next(ks), (BATCH, SEQ, D), f32),
        'a_attn_norm': gain((NA, D)),
        'a_w_in': w((NA, D, NSA_IN_WIDTH), D),
        'a_q_norm': gain((NA, NSA_DH)),
        'a_kcmp_norm': gain((NA, NSA_DH)),
        'a_kslc_norm': gain((NA, NSA_DH)),
        'a_kwin_norm': gain((NA, NSA_DH)),
        'a_cmp_pos_k': small((NA, CMP_BLOCK, NSA_DH), 0.02),
        'a_cmp_pos_v': small((NA, CMP_BLOCK, NSA_DH), 0.02),
        'a_cmp_k_w1': w((NA, flat, CMP_HIDDEN), flat),
        'a_cmp_k_b1': small((NA, CMP_HIDDEN), 0.01),
        'a_cmp_k_w2': w((NA, CMP_HIDDEN, NSA_DH), CMP_HIDDEN),
        'a_cmp_v_w1': w((NA, flat, CMP_HIDDEN), flat),
        'a_cmp_v_b1': small((NA, CMP_HIDDEN), 0.01),
        'a_cmp_v_w2': w((NA, CMP_HIDDEN, NSA_DH), CMP_HIDDEN),
        'a_w_out': w((NA, NSA_HEADS * NSA_DH, D), NSA_HEADS * NSA_DH),
        'kv_norm': gain((D,)),
        'kv_w_a': w((D, KV_LORA + QK_ROPE), D),
        'kv_c_norm': gain((KV_LORA,)),
        'kv_w_b': w((KV_LORA, MLA_HEADS * (QK_NOPE + MLA_V)), KV_LORA),
        'kv_k_norm': gain((QK_NOPE + QK_ROPE,)),
        'b_attn_norm': gain((NB, D)),
        'b_w_q_a': w((NB, D, Q_LORA), D),
        'b_q_a_norm': gain((NB, Q_LORA)),
        'b_w_q_b': w((NB, Q_LORA, MLA_HEADS * (QK_NOPE + QK_ROPE)), Q_LORA),
        'b_q_norm': gain((NB, QK_NOPE + QK_ROPE)),
        'b_w_out': w((NB, MLA_HEADS * MLA_V, D), MLA_HEADS * MLA_V),
        'ffn_norm': gain((DEPTH, D)),
        'ffn_w_gate_up': w((DEPTH, D, 2 * FFN_HIDDEN), D),
        'ffn_w_down': w((DEPTH, FFN_HIDDEN, D), FFN_HIDDEN),
    }

def first_block(x, a_attn_norm, a_w_in, a_q_norm, a_kcmp_norm, a_kslc_norm, a_kwin_norm,
              a_cmp_pos_k, a_cmp_pos_v, a_cmp_k_w1, a_cmp_k_b1, a_cmp_k_w2,
              a_cmp_v_w1, a_cmp_v_b1, a_cmp_v_w2, a_w_out,
              kv_norm, kv_w_a, kv_c_norm, kv_w_b, kv_k_norm,
              b_attn_norm, b_w_q_a, b_q_a_norm, b_w_q_b, b_q_norm, b_w_out,
              ffn_norm, ffn_w_gate_up, ffn_w_down):
    T = x.shape[1]
    cos, sin = rope_tables(T)
    shared_k = None
    shared_v = None
    for layer in range(DEPTH):
        if layer < N_A_LAYERS:
            i = layer
            x = x + nsa_mixer(rms_norm(x, a_attn_norm[i]), a_w_in[i], a_q_norm[i],
                              a_kcmp_norm[i], a_kslc_norm[i], a_kwin_norm[i],
                              a_cmp_pos_k[i], a_cmp_pos_v[i],
                              a_cmp_k_w1[i], a_cmp_k_b1[i], a_cmp_k_w2[i],
                              a_cmp_v_w1[i], a_cmp_v_b1[i], a_cmp_v_w2[i], a_w_out[i])
        else:
            j = layer - N_A_LAYERS
            x = x + mla_mixer(rms_norm(x, b_attn_norm[j]), shared_k, shared_v,
                              b_w_q_a[j], b_q_a_norm[j], b_w_q_b[j], b_q_norm[j],
                              b_w_out[j], cos, sin)
        x = x + swiglu(rms_norm(x, ffn_norm[layer]), ffn_w_gate_up[layer], ffn_w_down[layer])
        if layer == N_A_LAYERS - 1:
            shared_k, shared_v = shared_mla_kv(x, kv_norm, kv_w_a, kv_c_norm, kv_w_b,
                                               kv_k_norm, cos, sin)
    return x


N_MIXERS = 2
D_FF = 2816
CONV_WIDTH = 31
N_HEADS = 8
HEAD_DIM = 64
QK_WIDTH = N_HEADS * 2 * HEAD_DIM
V_WIDTH = N_HEADS * 2 * HEAD_DIM
RMS_EPS = 1e-6
SUBLN_EPS = 1e-5
LN_EPS = 1e-5
N_CONV_LAYERS = (DEPTH + 1) // 2
N_ATTN_LAYERS = DEPTH // 2


def _rmsnorm(x, g, eps=RMS_EPS):
    xf = x.astype(jnp.float32)
    y = xf * lax.rsqrt(jnp.mean(xf * xf, axis=-1, keepdims=True) + eps)
    return (y * g.astype(jnp.float32)).astype(x.dtype)

def _layernorm(x, g, b, eps=LN_EPS):
    xf = x.astype(jnp.float32)
    mu = jnp.mean(xf, axis=-1, keepdims=True)
    var = jnp.mean(jnp.square(xf - mu), axis=-1, keepdims=True)
    y = (xf - mu) * lax.rsqrt(var + eps)
    return (y * g.astype(jnp.float32) + b.astype(jnp.float32)).astype(x.dtype)

def _half_ffn(x, g_pre, g_post, w_gate, w_up, w_down):
    h = _rmsnorm(x, g_pre)
    f = (jax.nn.silu(h @ w_gate) * (h @ w_up)) @ w_down
    return x + 0.5 * _rmsnorm(f, g_post)

def _conformer_conv(h, w_pw1, b_pw1, w_dw, b_dw, ln_g, ln_b, w_pw2, b_pw2):
    u = h @ w_pw1 + b_pw1
    u = u[..., :D_MODEL] * jax.nn.sigmoid(u[..., D_MODEL:])
    pad = (CONV_WIDTH - 1) // 2
    c = lax.conv_general_dilated(
        u, w_dw[:, None, :].astype(u.dtype),
        window_strides=(1,), padding=[(pad, pad)],
        dimension_numbers=("NWC", "WIO", "NWC"),
        feature_group_count=D_MODEL) + b_dw
    c = jax.nn.silu(_layernorm(c, ln_g, ln_b))
    return c @ w_pw2 + b_pw2

def _lambda_init(layer_idx):
    return 0.8 - 0.6 * math.exp(-0.3 * layer_idx)

def _diff_attention(h, w_qkv, w_o, lq1, lk1, lq2, lk2, subln_g, lambda_init):
    B, S, _ = h.shape
    qkv = h @ w_qkv
    q, k, v = jnp.split(qkv, [QK_WIDTH, 2 * QK_WIDTH], axis=-1)
    q = q.reshape(B, S, N_HEADS, 2, HEAD_DIM)
    k = k.reshape(B, S, N_HEADS, 2, HEAD_DIM)
    v = v.reshape(B, S, N_HEADS, 2 * HEAD_DIM)
    f32 = jnp.float32
    lam = (jnp.exp(jnp.sum(lq1.astype(f32) * lk1.astype(f32)))
           - jnp.exp(jnp.sum(lq2.astype(f32) * lk2.astype(f32))) + lambda_init)
    slopes = 2.0 ** (-8.0 * (jnp.arange(N_HEADS, dtype=f32) + 1.0) / N_HEADS)
    scale = HEAD_DIM ** -0.5
    kpos = jnp.arange(S, dtype=f32)
    nblk = S // Q_BLOCK
    q_blocks = q.reshape(B, nblk, Q_BLOCK, N_HEADS, 2, HEAD_DIM).transpose(1, 0, 2, 3, 4, 5)
    starts = jnp.arange(nblk, dtype=jnp.int32) * Q_BLOCK

    def one_block(args):
        qb, start = args
        s = jnp.einsum("bqhmd,bkhmd->bhmqk", qb, k).astype(f32) * scale
        qpos = start.astype(f32) + jnp.arange(Q_BLOCK, dtype=f32)
        dist = jnp.abs(qpos[:, None] - kpos[None, :])
        s = s - slopes[:, None, None, None] * dist
        p = jax.nn.softmax(s, axis=-1)
        a = p[:, :, 0] - lam * p[:, :, 1]
        return jnp.einsum("bhqk,bkhe->bqhe", a.astype(v.dtype), v)

    o = lax.map(one_block, (q_blocks, starts))
    o = o.transpose(1, 0, 2, 3, 4).reshape(B, S, N_HEADS, 2 * HEAD_DIM)
    o = _rmsnorm(o, subln_g, SUBLN_EPS) * (1.0 - lambda_init)
    return o.reshape(B, S, V_WIDTH) @ w_o

def second_inputs(seed: int = 0) -> dict:
    key = jax.random.key(seed)
    ks = jax.random.split(key, 24)
    D, F, K = D_MODEL, D_FF, CONV_WIDTH
    NC, NA = N_CONV_LAYERS, N_ATTN_LAYERS
    nrm = jax.random.normal
    f32 = jnp.float32

    def gain(k, shape):
        return 1.0 + 0.05 * nrm(k, shape, f32)

    def small(k, shape):
        return 0.02 * nrm(k, shape, f32)

    return {
        "x": nrm(ks[0], (BATCH, SEQ, D), f32),
        "ffn_norm_pre": gain(ks[1], (DEPTH, 2, D)),
        "ffn_norm_post": gain(ks[2], (DEPTH, 2, D)),
        "ffn_w_gate": nrm(ks[3], (DEPTH, 2, D, F), f32) * D ** -0.5,
        "ffn_w_up": nrm(ks[4], (DEPTH, 2, D, F), f32) * D ** -0.5,
        "ffn_w_down": nrm(ks[5], (DEPTH, 2, F, D), f32) * F ** -0.5,
        "mix_norm_pre": gain(ks[6], (DEPTH, D)),
        "mix_norm_post": gain(ks[7], (DEPTH, D)),
        "conv_w_pw1": nrm(ks[8], (NC, D, 2 * D), f32) * D ** -0.5,
        "conv_b_pw1": small(ks[9], (NC, 2 * D)),
        "conv_w_dw": nrm(ks[10], (NC, K, D), f32) * K ** -0.5,
        "conv_b_dw": small(ks[11], (NC, D)),
        "conv_ln_g": gain(ks[12], (NC, D)),
        "conv_ln_b": small(ks[13], (NC, D)),
        "conv_w_pw2": nrm(ks[14], (NC, D, D), f32) * D ** -0.5,
        "conv_b_pw2": small(ks[15], (NC, D)),
        "attn_w_qkv": nrm(ks[16], (NA, D, 2 * QK_WIDTH + V_WIDTH), f32) * D ** -0.5,
        "attn_w_o": nrm(ks[17], (NA, V_WIDTH, D), f32) * V_WIDTH ** -0.5,
        "attn_lambda_q1": 0.1 * nrm(ks[18], (NA, HEAD_DIM), f32),
        "attn_lambda_k1": 0.1 * nrm(ks[19], (NA, HEAD_DIM), f32),
        "attn_lambda_q2": 0.1 * nrm(ks[20], (NA, HEAD_DIM), f32),
        "attn_lambda_k2": 0.1 * nrm(ks[21], (NA, HEAD_DIM), f32),
        "attn_subln_g": gain(ks[22], (NA, 2 * HEAD_DIM)),
    }

def second_block(x, ffn_norm_pre, ffn_norm_post, ffn_w_gate, ffn_w_up, ffn_w_down,
              mix_norm_pre, mix_norm_post,
              conv_w_pw1, conv_b_pw1, conv_w_dw, conv_b_dw, conv_ln_g, conv_ln_b,
              conv_w_pw2, conv_b_pw2,
              attn_w_qkv, attn_w_o, attn_lambda_q1, attn_lambda_k1,
              attn_lambda_q2, attn_lambda_k2, attn_subln_g):
    ic = 0
    ia = 0
    for i in range(DEPTH):
        x = _half_ffn(x, ffn_norm_pre[i, 0], ffn_norm_post[i, 0],
                      ffn_w_gate[i, 0], ffn_w_up[i, 0], ffn_w_down[i, 0])
        h = _rmsnorm(x, mix_norm_pre[i])
        if i % N_MIXERS == 0:
            m = _conformer_conv(h, conv_w_pw1[ic], conv_b_pw1[ic], conv_w_dw[ic],
                                conv_b_dw[ic], conv_ln_g[ic], conv_ln_b[ic],
                                conv_w_pw2[ic], conv_b_pw2[ic])
            ic += 1
        else:
            m = _diff_attention(h, attn_w_qkv[ia], attn_w_o[ia],
                                attn_lambda_q1[ia], attn_lambda_k1[ia],
                                attn_lambda_q2[ia], attn_lambda_k2[ia],
                                attn_subln_g[ia], _lambda_init(i))
            ia += 1
        x = x + _rmsnorm(m, mix_norm_post[i])
        x = _half_ffn(x, ffn_norm_pre[i, 1], ffn_norm_post[i, 1],
                      ffn_w_gate[i, 1], ffn_w_up[i, 1], ffn_w_down[i, 1])
    return x


def setup_inputs(seed=0):
    out = dict(first_inputs(seed))
    for name, value in second_inputs(seed + 1).items():
        if name != "x":
            out[name + "_2"] = value
    return out


def reference(
    x, a_attn_norm, a_w_in, a_q_norm, a_kcmp_norm, a_kslc_norm, a_kwin_norm, a_cmp_pos_k,
    a_cmp_pos_v, a_cmp_k_w1, a_cmp_k_b1, a_cmp_k_w2, a_cmp_v_w1, a_cmp_v_b1, a_cmp_v_w2,
    a_w_out, kv_norm, kv_w_a, kv_c_norm, kv_w_b, kv_k_norm, b_attn_norm, b_w_q_a, b_q_a_norm,
    b_w_q_b, b_q_norm, b_w_out, ffn_norm, ffn_w_gate_up, ffn_w_down, ffn_norm_pre_2,
    ffn_norm_post_2, ffn_w_gate_2, ffn_w_up_2, ffn_w_down_2, mix_norm_pre_2, mix_norm_post_2,
    conv_w_pw1_2, conv_b_pw1_2, conv_w_dw_2, conv_b_dw_2, conv_ln_g_2, conv_ln_b_2,
    conv_w_pw2_2, conv_b_pw2_2, attn_w_qkv_2, attn_w_o_2, attn_lambda_q1_2, attn_lambda_k1_2,
    attn_lambda_q2_2, attn_lambda_k2_2, attn_subln_g_2,
):
    x = first_block(
        x, a_attn_norm, a_w_in, a_q_norm, a_kcmp_norm, a_kslc_norm, a_kwin_norm, a_cmp_pos_k,
        a_cmp_pos_v, a_cmp_k_w1, a_cmp_k_b1, a_cmp_k_w2, a_cmp_v_w1, a_cmp_v_b1, a_cmp_v_w2,
        a_w_out, kv_norm, kv_w_a, kv_c_norm, kv_w_b, kv_k_norm, b_attn_norm, b_w_q_a,
        b_q_a_norm, b_w_q_b, b_q_norm, b_w_out, ffn_norm, ffn_w_gate_up, ffn_w_down,
    )
    return second_block(
        x, ffn_norm_pre_2, ffn_norm_post_2, ffn_w_gate_2, ffn_w_up_2, ffn_w_down_2,
        mix_norm_pre_2, mix_norm_post_2, conv_w_pw1_2, conv_b_pw1_2, conv_w_dw_2, conv_b_dw_2,
        conv_ln_g_2, conv_ln_b_2, conv_w_pw2_2, conv_b_pw2_2, attn_w_qkv_2, attn_w_o_2,
        attn_lambda_q1_2, attn_lambda_k1_2, attn_lambda_q2_2, attn_lambda_k2_2, attn_subln_g_2,
    )


_drawn_inputs = setup_inputs


def setup_inputs(seed=0):
    import zlib

    import numpy as np

    out = dict(_drawn_inputs(seed))
    spreads = {}
    factors = {'a_attn_norm': 3.271,
     'a_q_norm': 7.081,
     'a_kcmp_norm': 8.0,
     'a_kslc_norm': 8.0,
     'a_kwin_norm': 8.0,
     'a_cmp_pos_k': 8.0,
     'a_cmp_pos_v': 4.598,
     'a_cmp_k_b1': 8.0,
     'a_cmp_v_b1': 8.0,
     'kv_norm': 7.716,
     'kv_c_norm': 7.987,
     'kv_k_norm': 8.0,
     'b_attn_norm': 8.0,
     'b_q_a_norm': 8.0,
     'b_q_norm': 8.0,
     'conv_b_pw1_2': 21.299,
     'conv_ln_b_2': 22.686,
     'attn_lambda_q1_2': 30.94,
     'attn_subln_g_2': 21.968,
     'ffn_norm_pre_2': 6.706,
     'ffn_norm_post_2': 8.0,
     'mix_norm_pre_2': 4.996,
     'mix_norm_post_2': 6.871,
     'conv_b_dw_2': 8.0,
     'conv_ln_g_2': 8.0,
     'conv_b_pw2_2': 8.0,
     'attn_lambda_q2_2': 8.0,
     'attn_lambda_k2_2': 8.0}
    for name, (base, spread) in spreads.items():
        noise = np.random.default_rng([zlib.crc32(name.encode()), seed]).standard_normal(out[name].shape)
        drawn = base * np.exp(spread * noise) if base else spread * noise
        out[name] = jnp.asarray(drawn.astype(out[name].dtype))
    for name, factor in factors.items():
        out[name] = (out[name] * factor).astype(out[name].dtype)
    return out
```

```python
from contextlib import ExitStack

import numpy as np

import concourse.bass as bass
from concourse import mybir

ALU = mybir.AluOpType
ACT = mybir.ActivationFunctionType
F32 = mybir.dt.float32
F32R = mybir.dt.float32r
AX = mybir.AxisListType.X

P = 128
T = 256
NT = T // P
D = 1024
DC = D // P
EPS = 1e-6
LN_EPS = 1e-5
SUBLN_EPS = 1e-5

H1, G1, DH = 16, 4, 64
CMP_BLOCK, CMP_STRIDE, CMP_HIDDEN = 32, 16, 256
NCMP = (T - CMP_BLOCK) // CMP_STRIDE + 1
GJ = G1 * NCMP
IN_W = H1 * DH + 6 * G1 * DH + 3 * H1
COL_KC, COL_VC, COL_KS, COL_VS, COL_KW, COL_VW, COL_G = (H1 * DH + i * G1 * DH for i in range(7))
H2, NOPE, ROPE, VD = 8, 128, 64, 128
QL, KVL = 384, 256
QK = NOPE + ROPE
FF = 2816
FC = FF // P
TAPS = 31
PAD = (TAPS - 1) // 2
CONV_DVE = 5
CONV_PE = D // P - CONV_DVE
EARLY = 3
H3 = 8
LAMBDA_INIT = 0.8 - 0.6 * float(np.exp(-0.3))

UNIT, UA = 3072, 2048
PITCH = UNIT // DC

U_IN, U_CMP, U_OUT, U_F1 = 0, 7, 10, 13
U_KVA, U_QA, U_KVB, U_QB, U_MO, U_F2 = 35, 36, 37, 39, 41, 44
U_F3, U_PW1, U_PW2, U_F4, U_F5 = 66, 88, 94, 97, 119
U_QKV, U_WO, U_F6, U_END = 141, 149, 152, 174
UNITS = U_END + 2

COLS = [("attn_norm", 8), ("kv_norm", 8), ("b_attn_norm", 8), ("ffn_norm", 16), ("ffn_pre", 32),
        ("mix_pre", 16), ("q_norm", 1), ("kcmp_norm", 1), ("kslc_norm", 1), ("kwin_norm", 1),
        ("b1", 4), ("pos", 32), ("w2", 256), ("kv_c_norm", 2), ("q_a_norm", 3), ("knope", 1),
        ("qnope", 1), ("b_pw1", 16), ("ln_g", 8), ("ln_b", 8), ("b_dw", 8), ("w_dw", TAPS * 8),
        ("subln", 1)]
CO, _at = {}, 0
for _n, _w in COLS:
    CO[_n] = _at
    _at += _w
NCOLS = _at
RO = {"kpe": 0, "qpe": 64, "lambda": 128}
NROWS = 128 + 4 * 64
KO, _at = {}, 0
for _n, _w in (("ident", 128), ("ones", 128), ("causal", 512), ("mask", 512), ("dist", 512),
               ("valid", 2), ("cos", 64), ("sin", 64), ("biasc", 2 * H1 * GJ)):
    KO[_n] = _at
    _at += _w
NCONST = _at
NKEEP = KO["biasc"]
SLOPES1 = [float(np.float32(2.0) ** np.float32(-8.0 * (h + 1) / H1)) for h in range(H1)]
SLOPES3 = [float(np.float32(2.0) ** np.float32(-8.0 * (h + 1) / H3)) for h in range(H3)]

STEPS = {}
for _u in range(7):
    STEPS[U_IN + _u] = (8, PITCH, [(0, min(PITCH, IN_W - _u * PITCH))])
for _b in (U_OUT, U_MO, U_PW2, U_WO):
    for _u in range(3):
        STEPS[_b + _u] = (8, PITCH, [(0, min(PITCH, D - _u * PITCH))])
STEPS[U_KVA] = (8, PITCH, [(0, KVL + ROPE)])
STEPS[U_QA] = (8, PITCH, [(0, QL)])
for _u in range(2):
    STEPS[U_KVB + _u] = (2, 2048, [(0, 512), (512, 512)])
    STEPS[U_QB + _u] = (3, 1024, [(0, 384), (384, 384)])
for _u in range(8):
    STEPS[U_QKV + _u] = (8, PITCH, [(0, PITCH)])


UPDATES = 10
ADDED = (U_OUT, U_MO)


def projection_plan():
    plan, last, flip, eva, evd = {}, {}, 0, 0, 0
    for u in sorted(STEPS):
        pieces = STEPS[u][2]
        if len(pieces) == 1:
            banks = [[2 * (flip % 2) + t] for t in range(NT)]
            flip += 1
        else:
            banks = [[2 * t, 2 * t + 1] for t in range(NT)]
        before = max([last.get(b, -1) for row in banks for b in row])
        added = any(b <= u < b + 3 for b in ADDED)
        eva += not added
        evd += not (added and any(u == b + 2 for b in ADDED))
        plan[u] = (banks, before, eva, evd)
        for row in banks:
            for b in row:
                last[b] = u
    return plan


ROUNDS = [("op_attn", 4), ("kcvc", 2), ("q1", 4), ("k1", 4), ("kcmp", 1), ("pc0", 4), ("pc1", 4), ("nsa", 2 * H1),
          ("op_f1", 4), ("op_kv", 4), ("op_bq", 4), ("op_ckv", 1), ("op_qa", 2), ("k2", 4), ("q2", 4),
          ("kpe", 2), ("qpe", 2), ("mla", H2), ("op_f2", 4), ("op_f3", 4), ("op_conv", 4), ("op_f4", 4),
          ("op_f5", 4), ("op_qkv", 4), ("q3", 4), ("k3", 4), ("diff", 2 * H3), ("op_wo", 4), ("op_f6", 4)]
RD, _at = {}, 0
for _n, _w in ROUNDS:
    RD[_n] = _at
    _at += _w
RSTD = {n: i for i, n in enumerate(
    ["n0", "qk1", "kcmp", "n1", "n2", "ckv", "qan", "qk2", "n3", "n4", "post0", "n5", "post1", "n6", "post2",
     "n7", "post3", "n8", "subln", "post4", "n9", "post5"])}
ITEM0 = {"nsa": 0, "mla": 2 * H1, "diff": 2 * H1 + H2}
NITEM = {"nsa": 2 * H1, "mla": H2, "diff": 2 * H3}
PW1 = [[0, 1, 2], [3, 4, 5], [6, 7, 8], [9, 10, 11], [12, 13], [14, 15]]


OPN, _at = {}, 0
for _n, _w in ROUNDS:
    if _n.startswith("op_"):
        OPN[_n] = _at
        _at += _w
FUNITS = [U_F1, U_F2, U_F3, U_F4, U_F5, U_F6]


def item_blocks(kind, i):
    if kind == "nsa":
        return [(b, k) for b in range(2) for k in range(i % 2 + 1)]
    if kind == "mla":
        return [(0, 0), (1, 0), (1, 1)]
    return [(0, 0), (0, 1)]


def build(nc, stream, cols_d, rows_d, wide_d, x_d, const_d, out_d):
    ctx = ExitStack()
    with ctx:
        def sb(name, shape, dt=F32):
            return ctx.enter_context(nc.sbuf_tensor(name, shape, dt))

        def sem(name):
            return ctx.enter_context(nc.semaphore(name))

        raw = sb("raw", [P, 2, UNIT])
        whi = sb("whi", [P, 2, UNIT], F32R)
        wlo = sb("wlo", [P, 2, UNIT], F32R)
        x = sb("x", [P, NT, D])
        xn = sb("xn", [P, NT, D])
        hthi = sb("hthi", [P, DC, T], F32R)
        htlo = sb("htlo", [P, DC, T], F32R)
        proj = sb("proj", [P, 7168])
        tr = sb("tr", [P, 8192])
        att = sb("att", [P, 3072])
        hidhi = sb("hidhi", [P, 2, T], F32R)
        hidlo = sb("hidlo", [P, 2, T], F32R)
        wide = sb("wide", [P, 2, D])
        cols = sb("cols", [P, NCOLS])
        rows = sb("rows", [P, NROWS])
        const = sb("const", [P, NKEEP])
        gates = sb("gates", [P, NT, 48])
        ss = sb("ss", [P, 64])
        std = sb("std", [P, 64])
        rs = sb("rs", [P, 64])
        nmax = sb("nmax", [P, 2, 16])
        lsum = sb("lsum", [P, 2, 16])
        pw = sb("pw", [P, 2, 16])
        vcmp = sb("vcmp", [GJ, DH])
        kcd = sb("kcd", [GJ, 2, DH])
        kcz = sb("kcz", [P, 2, GJ])
        cst = sb("cst", [P, 4, H1])
        lam = sb("lam", [P, 8])
        lamt = sb("lamt", [P, 128])
        sgain = sb("sgain", [P, 1])

        bank = [ctx.enter_context(nc.psum_tensor(f"bank{i}", [P, 512], F32)) for i in range(8)]
        acc, tp, gub = bank[0:4], bank[4:6], bank[6:8]

        ident = const[:, KO["ident"]:KO["ident"] + P]
        ones = const[:, KO["ones"]:KO["ones"] + P]

        def col(name, i=0):
            return cols[:, CO[name] + i:CO[name] + i + 1]

        biasc = wide[:, :, :].rearrange("p a n -> p (a n)")[:, 0:NCONST - NKEEP]
        p1 = proj[:, 0:NT * IN_W].rearrange("p (t n) -> p t n", t=NT)
        kv = proj[:, 0:4096].rearrange("p (t h n) -> p t h n", t=NT, h=H2)
        q2 = proj[:, 4096:7168].rearrange("p (t h n) -> p t h n", t=NT, h=H2)
        p3 = proj[:, 0:6144].rearrange("p (t n) -> p t n", t=NT)
        m_out = proj[:, 0:NT * D].rearrange("p (t n) -> p t n", t=NT)
        conv_u = proj[:, 0:8 * (T + 2 * PAD)].rearrange("p (c n) -> p c n", c=8)
        conv_c = proj[:, 2304:4352].rearrange("p (c n) -> p c n", c=8)
        conv_s = proj[:, 4352:6400].rearrange("p (c n) -> p c n", c=8)
        conv_r = proj[:, 6400:6912].rearrange("p (c n) -> p c n", c=2)
        diag = [v.rearrange("p (k n) -> p k n", n=P) for v in (tr[:, 1024:8192], att[:, :], proj[:, 4352:6400])]
        diag_runs, left = [], [v.shape[1] for v in diag]
        for c in range(CONV_DVE, 8):
            k = 0
            while k < TAPS:
                part = [room > 0 for room in left].index(True)
                cnt = min(TAPS - k, left[part])
                diag_runs.append((c, k, cnt, part, diag[part].shape[1] - left[part]))
                left[part] -= cnt
                k += cnt
        diff_o = proj[:, 0:NT * D].rearrange("p (t n) -> p t n", t=NT)

        qT = tr[:, 0:2048].rearrange("p (c n) -> p c n", c=8)
        kz = tr[:, 2048:6144].rearrange("p (m g n) -> p m g n", m=2, g=8)
        sq1 = tr[:, 2048:2048 + NT * 24 * 64].rearrange("p (t n) -> p t n", t=NT)
        blk = tr[:, 6144:6144 + 1920]
        kd = tr[:, 6144:8192].rearrange("p (t g d n) -> p t g d n", t=NT, g=8, d=2)
        pct = [xn[0:GJ, :, :].rearrange("p t n -> p (t n)").rearrange("p (h n) -> p h n", h=H1),
               tr[0:GJ, 6144:8192].rearrange("p (h n) -> p h n", h=H1)]
        kc2 = xn[:, :, :].rearrange("p t n -> p (t n)").rearrange("p (v a b n) -> p v a b n", v=2, a=2, b=2)
        xflat = xn[:, :, :].rearrange("p t n -> p (t n)")
        blkhi = hthi[:, :, :].rearrange("p c n -> p (c n)")[:, 0:1920]
        blklo = htlo[:, :, :].rearrange("p c n -> p (c n)")[:, 0:1920]
        kT2 = tr[:, 2048:4096].rearrange("p (c n) -> p c n", c=8)
        qpe = att[:, 0:1024].rearrange("p (t h n) -> p t h n", t=NT, h=H2)
        qpT = tr[:, 4096:5120].rearrange("p (c n) -> p c n", c=4)
        kpT = tr[:, 5120:6144].rearrange("p (c n) -> p c n", c=4)
        kva = att[:, 0:640].rearrange("p (t n) -> p t n", t=NT)
        qa = att[:, 640:1408].rearrange("p (t n) -> p t n", t=NT)
        kpe = att[:, 1408:2432].rearrange("p (t h n) -> p t h n", t=NT, h=H2)
        sg = tr[:, 0:512].rearrange("p (c n) -> p c n", c=2)
        hidf = tr[:, 512:1024].rearrange("p (c n) -> p c n", c=2)

        s_sc = att[:, 0:1024].rearrange("p (i b n) -> p i b n", i=2, b=2)
        s_pr = att[:, 1024:2048].rearrange("p (i b n) -> p i b n", i=2, b=2)
        s_pt = att[:, 2048:3072].rearrange("p (i n) -> p i n", i=2)

        s_ldx, s_ldc, s_ldk, s_ldr = sem("x_loaded"), sem("cols_loaded"), sem("const_loaded"), sem("rows_loaded")
        s_ldbc = sem("compressed_bias_loaded")
        s_lda = [sem("piece_a_loaded_0"), sem("piece_a_loaded_1")]
        s_ldb = [sem("piece_b_loaded_0"), sem("piece_b_loaded_1")]
        s_ldw = [sem("wide_loaded_0"), sem("wide_loaded_1")]
        s_hia, s_hib = sem("hi_a_done"), sem("hi_b_done")
        s_loa, s_lob = sem("lo_a_done"), sem("lo_b_done")
        s_usea, s_useb = sem("piece_a_used"), sem("piece_b_used")
        s_act, s_dve = sem("act_own"), sem("dve_own")
        s_x = sem("x_updated")
        s_std, s_rs = sem("std_done"), sem("rstd_done")
        s_xn = sem("normalised")
        s_tr = sem("transposed")
        s_tf = [sem("transpose_bank_taken_0"), sem("transpose_bank_taken_1")]
        s_thi = sem("operand_hi_done")
        s_eva, s_evd = sem("step_taken_by_act"), sem("step_taken_by_dve")
        s_silu, s_hf, s_hh, s_hid = sem("silu_done"), sem("hidden_full"), sem("hidden_hi"), sem("hidden_done")
        s_wu = sem("wide_used")
        s_sco, s_bia, s_exp, s_prob = sem("scores_done"), sem("scores_biased"), sem("exp_done"), sem("probs_done")
        s_pv = sem("values_summed")
        s_oh, s_ol, s_od = sem("output_hi_done"), sem("output_lo_done"), sem("output_taken")
        s_pss, s_phs = sem("post_squares_summed"), sem("post_halves_added")
        s_pw, s_sig, s_glu = sem("pw1_gate_done"), sem("sigmoid_done"), sem("glu_done")
        s_out = sem("stored")
        ev = {name: sem(name) for name in (
            "kc2_ready", "blk_ready", "sq1_ready", "ss1_ready", "qn_ready", "kd_ready", "q1_ready", "k1_ready",
            "hx_ready", "gelu_in", "gelu_sig", "gelu_ready", "w2_done", "kcmp_sq", "kcd_ready", "kcz_ready",
            "gates_ready", "cs0", "cs1", "cm0", "cm1", "ce0", "ce1", "cp0", "cp1", "kz_zeroed", "v2_sq",
            "ckv_ready", "qa_ready", "ckv_sq", "qa_sq", "qk2_sq", "qk2_ss", "k2n_ready", "q2n_ready", "kpe_ready",
            "diagonals_ready", "conv_summed", "conv_early", "sum_ready",
            "qpe_ready", "k2_done", "q2_done", "conv_ready", "mean_done", "centred", "sq_ready", "var_done",
            "conv_std", "lny_ready", "silu_ready", "conv_hi", "conv_lo", "q3_done", "k3_done",
            "lam_sum", "lam_exp", "sub_sq", "sub_ss", "sub_ready")}

        plan = projection_plan()
        block = ctx.enter_context(nc.Block())

        def pw1_ready(eng, u, m, c):
            if m == 0:
                eng.wait_ge(s_pw, sum(1 for w in PW1 for mm, q in enumerate(w) if mm == 0 and q % 2 and q <= 2 * c + 1))
            elif m == 1:
                eng.wait_ge(s_usea, u + 1)
            else:
                eng.wait_ge(s_useb, u + 1)

        @block.sync
        def _(sp):
            sp.dma_start(x[:, :, :], x_d.rearrange("(t p) n -> p t n", p=P)).then_inc(s_ldx, 16)
            sp.dma_start(raw[:, 0, 0:UA], stream[0, :, 0:UA]).then_inc(s_lda[0], 16)
            sp.dma_start(cols[:, :], cols_d).then_inc(s_ldc, 16)
            sp.dma_start(const[:, :], const_d[:, 0:NKEEP]).then_inc(s_ldk, 16)
            sp.dma_start(raw[:, 0, UA:UNIT], stream[0, :, UA:UNIT]).then_inc(s_ldb[0], 16)
            sp.dma_start(raw[:, 1, 0:UA], stream[1, :, 0:UA]).then_inc(s_lda[1], 16)
            sp.dma_start(raw[:, 1, UA:UNIT], stream[1, :, UA:UNIT]).then_inc(s_ldb[1], 16)
            sp.dma_start(rows[:, :], rows_d[0].partition_broadcast(P)).then_inc(s_ldr, 16)
            sp.dma_start(biasc, const_d[:, NKEEP:NCONST]).then_inc(s_ldbc, 16)
            with sp.Fori(1, UNITS // 2) as i:
                for j in range(2):
                    sp.wait_ge(s_loa, i * 2 + (j - 1))
                    sp.dma_start(raw[:, j, 0:UA], stream[i * 2 + j, :, 0:UA]).then_inc(s_lda[j], 16)
                    sp.wait_ge(s_lob, i * 2 + (j - 1))
                    sp.dma_start(raw[:, j, UA:UNIT], stream[i * 2 + j, :, UA:UNIT]).then_inc(s_ldb[j], 16)
            for j in range(2):
                sp.wait_ge(s_lda[j], 16 * (UNITS // 2))
                sp.wait_ge(s_ldb[j], 16 * (UNITS // 2))
            sp.wait_ge(s_x, 2 * UPDATES)
            sp.dma_start(out_d.rearrange("(t p) n -> p t n", p=P), x[:, :, :]).then_inc(s_out, 16)
            sp.wait_ge(s_out, 16)

        @block.gpsimd
        def _(pool):
            for n in range(7):
                if n == 0:
                    pool.wait_ge(ev["cm1"], 1)
                if n == 2:
                    pool.wait_ge(s_ldk, 16)
                    pool.wait_ge(s_ldc, 16)
                    pool.wait_ge(s_ol, 16)
                    pool.wait_ge(s_x, 6)
                    dw = cols[:, CO["w_dw"]:CO["w_dw"] + 8 * TAPS].rearrange("p (k c) -> p c k", c=8)
                    for c, k, cnt, part, at in diag_runs:
                        ins = nc.gpsimd.tensor_tensor(
                            diag[part][:, at:at + cnt, :], ident.unsqueeze(1).to_broadcast([P, cnt, P]),
                            dw[:, c, k:k + cnt].unsqueeze(2).to_broadcast([P, cnt, P]), ALU.mult)
                    ins.then_inc(ev["diagonals_ready"], 1)
                if n >= 2:
                    pool.wait_ge(s_wu, n - 1)
                pool.dma_start(wide[:, n % 2, :], wide_d[n].partition_broadcast(P)).then_inc(s_ldw[n % 2], 16)

        @block.scalar
        def _(act):
            n = dict(own=0, thi=0)

            def own(ins):
                n["own"] += 1
                ins.then_inc(s_act, 1)
                act.wait_ge(s_act, n["own"])

            def hi_a(u, i=0):
                s = u % 2
                act.wait_ge(s_lda[s], i * 16 + 16 * (u // 2 + 1))
                if u >= 2:
                    act.wait_ge(s_usea, i * 2 + (u - 1))
                nc.scalar.activation(whi[:, s, 0:UA], raw[:, s, 0:UA], ACT.Copy).then_inc(s_hia, 1)

            def hi_b(u, i=0):
                s = u % 2
                act.wait_ge(s_ldb[s], i * 16 + 16 * (u // 2 + 1))
                if u >= 2:
                    act.wait_ge(s_useb, i * 2 + (u - 1))
                nc.scalar.activation(whi[:, s, UA:UNIT], raw[:, s, UA:UNIT], ACT.Copy).then_inc(s_hib, 1)

            def step(u, dst=None):
                hi_b(u)
                hi_a(u + 1)
                if dst is not None:
                    banks = plan[u][0]
                    act.wait_ge(s_useb, u + 1)
                    for j, (c, w) in enumerate(STEPS[u][2]):
                        ins = nc.scalar.activation(dst(0, u, c, w), acc[banks[0][j]][:, 0:w], ACT.Copy)
                    ins.then_inc(s_eva, 1)

            def sqrt(name, cnt, dim, eps, src=None):
                if RSTD[name] >= 1:
                    act.wait_ge(s_rs, RSTD[name])
                r = vcmp.shape[0] if name == "kcmp" else P
                nc.scalar.activation(std[0:r, 0:cnt], (ss if src is None else src)[0:r, 0:cnt], ACT.Sqrt,
                                     scale=1.0 / dim, bias=eps).then_inc(s_std, 1)

            def norm(m):
                for t in range(NT):
                    if m == 0:
                        act.wait_ge(s_ldx, 16)
                    else:
                        act.wait_ge(s_x, 2 * m + t - 1)
                    ins = nc.scalar.activation(xn[:, t, :], x[:, t, :], ACT.Square, accum_out=ss[:, t:t + 1])
                own(ins)
                sqrt(f"n{m}", 2, D, EPS)

            def operand(name, chunks, free):
                if free:
                    act.wait_ge(s_useb, free)
                for a in range(0, len(chunks), 2):
                    r = RD[name] + a // 2
                    act.wait_ge(s_tr, r + 1)
                    for j, (dst, gain) in enumerate(chunks[a:a + 2]):
                        ins = nc.scalar.activation(hthi[:, dst, :], tp[r % 2][:, j * T:(j + 1) * T], ACT.Copy,
                                                   scale=1.0 if gain is None else gain)
                    ins.then_inc(s_thi, 1)

            def ffn(f):
                with act.Fori(0, FC // 2) as i:
                    for j in range(2):
                        hi_a(f + j + 1, i)
                        act.wait_ge(s_usea, i * 2 + (f + j + 1))
                        nc.scalar.activation(sg[:, j, :], gub[j][:, 0:T], ACT.Silu).then_inc(s_silu, 1)
                        hi_b(f + j, i)

            def post_ffn(k, f):
                act.wait_ge(s_useb, f + FC)
                for q in range(4):
                    ins = nc.scalar.activation(xn[:, q // 2, (q % 2) * 512:(q % 2 + 1) * 512], acc[q][:, :],
                                               ACT.Square, accum_out=ss[:, 8 + q:9 + q])
                ins.then_inc(s_pss, 1)
                act.wait_ge(s_phs, [0, None, 1, 2, None, 3][k] + 1)
                sqrt(f"post{k}", 2, D, EPS)

            def post_mixer(k, ready):
                ready()
                for t in range(NT):
                    ins = nc.scalar.activation(xn[:, t, :], m_out[:, t, :], ACT.Square, accum_out=ss[:, t:t + 1])
                own(ins)
                sqrt(f"post{k}", 2, D, EPS)

            def attention(kind):
                base, cnt = ITEM0[kind], NITEM[kind]

                def post(i):
                    g = base + i
                    if kind == "nsa" and i % 4 == 3:
                        act.wait_ge(s_pv, g + 1)
                        nc.scalar.activation(hthi[:, i // 4, :], gub[(i // 4) % 2][:, 0:T], ACT.Copy).then_inc(s_oh, 1)
                    if kind == "mla":
                        act.wait_ge(s_pv, g + 1)
                        nc.scalar.activation(hthi[:, i, :], gub[i % 2][:, 0:T], ACT.Copy).then_inc(s_oh, 1)
                    if kind == "diff":
                        act.wait_ge(s_pv, g + 1)
                        nc.scalar.activation(diff_o[:, i % 2, (i // 2) * P:(i // 2 + 1) * P], gub[g % 2][:, 0:P],
                                             ACT.Copy).then_inc(s_od, 1)

                for i in range(cnt + 2):
                    g = base + i
                    if i < cnt:
                        act.wait_ge(s_bia, g + 1)
                        act.wait_ge(s_tr, RD[kind] + max(i - 1, 0))
                        nk = P * (i % 2 + 1) if kind == "nsa" else T
                        for b in range(2):
                            ins = nc.scalar.activation(s_pr[:, g % 2, b, 0:nk], s_sc[:, g % 2, b, 0:nk], ACT.Exp,
                                                       bias=nmax[:, g % 2, b:b + 1],
                                                       accum_out=lsum[:, g % 2, b:b + 1])
                        ins.then_inc(s_exp, 1)
                    if 1 <= i <= cnt:
                        g, r = base + i - 1, RD[kind] + i - 1
                        w = P * len(item_blocks(kind, i - 1))
                        act.wait_ge(s_tr, r + 1)
                        if g >= 2:
                            act.wait_ge(s_pv, g - 1)
                        nc.scalar.activation(s_pt[:, g % 2, 0:w], tp[r % 2][:, 0:w], ACT.Copy).then_inc(s_tf[r % 2], 1)
                    if i >= 2:
                        post(i - 2)

            hi_a(0)
            act.wait_ge(s_ldc, 16)
            act.wait_ge(s_ldk, 16)
            norm(0)
            operand("op_attn", [(c, col("attn_norm", c)) for c in range(DC)], 0)
            for u in range(U_IN, U_IN + 7):
                step(u, lambda t, u, c, w: p1[:, t, (u - U_IN) * PITCH + c:(u - U_IN) * PITCH + c + w])
            act.wait_ge(s_evd, plan[U_IN + 6][3])
            act.wait_ge(s_eva, plan[U_IN + 6][2])
            for t in range(NT):
                nc.scalar.activation(sq1[:, t, 0:1024], p1[:, t, 0:1024], ACT.Square)
                ins = nc.scalar.activation(
                    sq1[:, t, 1024:1536].rearrange("p (a n) -> p a n", a=2),
                    p1[:, t, COL_KS:COL_KS + 1024].rearrange("p (a n) -> p a n", a=2)[:, :, 0:256], ACT.Square)
            ins.then_inc(ev["sq1_ready"], 1)
            nc.scalar.activation(gates[:, :, :], p1[:, :, COL_G:COL_G + 48], ACT.Sigmoid).then_inc(ev["gates_ready"], 1)
            hi_b(U_CMP)
            hi_a(U_CMP + 1)
            act.wait_ge(ev["ss1_ready"], 1)
            sqrt("qk1", 48, DH, EPS)
            for u in (U_CMP + 1, U_CMP + 2):
                hi_b(u)
                hi_a(u + 1)
            act.wait_ge(s_usea, U_CMP + 3)
            for q in range(4):
                ins = nc.scalar.activation(att[:, q * GJ:(q + 1) * GJ], acc[q][:, 0:GJ], ACT.Identity,
                                           bias=col("b1", q))
            ins.then_inc(ev["hx_ready"], 1)
            for r in range(4):
                rr = RD["k1"] + r
                act.wait_ge(s_tr, rr + 1)
                if r == 0:
                    act.wait_ge(ev["kz_zeroed"], 1)
                g0 = 2 * r
                name = "kslc_norm" if r < 2 else "kwin_norm"
                for m in range(2):
                    ins = nc.scalar.activation(
                        kz[m * 64:(m + 1) * 64, m, g0:g0 + 2, :],
                        tp[rr % 2][m * 64:(m + 1) * 64, :].rearrange("p (a n) -> p a n", a=2), ACT.Copy,
                        scale=cols[m * 64:(m + 1) * 64, CO[name]:CO[name] + 1])
                ins.then_inc(s_tf[rr % 2], 1)
            act.wait_ge(ev["gelu_in"], 1)
            nc.scalar.activation(att[:, 480:720], att[:, 240:480], ACT.Sigmoid, scale=2 * 0.7978845608028654)\
                .then_inc(ev["gelu_sig"], 1)
            act.wait_ge(ev["w2_done"], 1)
            own(nc.scalar.activation(att[0:GJ, 960:1024], gub[0][0:GJ, 0:DH], ACT.Square, accum_out=ss[0:GJ, 0:1]))
            sqrt("kcmp", 1, DH, EPS)
            r = RD["kcmp"]
            act.wait_ge(s_tr, r + 1)
            for m in range(2):
                ins = nc.scalar.activation(kcz[m * 64:(m + 1) * 64, m, :], tp[r % 2][m * 64:(m + 1) * 64, 0:GJ], ACT.Copy,
                                           scale=cols[m * 64:(m + 1) * 64, CO["kcmp_norm"]:CO["kcmp_norm"] + 1])
            ins.then_inc(s_tf[r % 2], 1)
            for t in range(NT):
                act.wait_ge(ev[f"cm{t}"], 1)
                if t == 1:
                    act.wait_ge(s_tr, RD["pc0"] + 4)
                nc.scalar.activation(att[:, 1024:1024 + H1 * GJ], att[:, 0:H1 * GJ], ACT.Exp).then_inc(ev[f"ce{t}"], 1)
                for q in range(4):
                    r = RD[f"pc{t}"] + q
                    act.wait_ge(s_tr, r + 1)
                    nc.scalar.activation(pct[t][:, 4 * q:4 * q + 4, :],
                                         tp[r % 2][0:GJ, :].rearrange("p (h n) -> p h n", h=4), ACT.Copy)\
                        .then_inc(s_tf[r % 2], 1)
            attention("nsa")
            for u in range(U_OUT, U_OUT + 3):
                step(u)
            norm(1)
            operand("op_f1", [(c, col("ffn_norm", c)) for c in range(DC)], U_F1)
            ffn(U_F1)
            norm(2)
            operand("op_kv", [(c, col("kv_norm", c)) for c in range(DC)], U_KVA)
            step(U_KVA, lambda t, u, c, w: kva[:, t, c:c + w])
            operand("op_bq", [(c, col("b_attn_norm", c)) for c in range(DC)], U_KVA + 1)
            act.wait_ge(s_evd, plan[U_KVA][3])
            act.wait_ge(s_eva, plan[U_KVA][2])
            for t in range(NT):
                nc.scalar.activation(xn[:, t, 0:KVL], kva[:, t, 0:KVL], ACT.Square, accum_out=ss[:, t:t + 1])
                ins = nc.scalar.activation(xn[:, t, KVL:KVL + ROPE], kva[:, t, KVL:KVL + ROPE], ACT.Square,
                                           accum_out=ss[:, 40 + t:41 + t])
            own(ins)
            sqrt("ckv", 2, KVL, EPS)
            step(U_QA, lambda t, u, c, w: qa[:, t, c:c + w])
            act.wait_ge(s_evd, plan[U_QA][3])
            act.wait_ge(s_eva, plan[U_QA][2])
            for t in range(NT):
                ins = nc.scalar.activation(xn[:, t, 0:QL], qa[:, t, :], ACT.Square, accum_out=ss[:, t:t + 1])
            own(ins)
            sqrt("qan", 2, QL, EPS)
            operand("op_ckv", [(c, col("kv_c_norm", c)) for c in range(2)], U_QA + 1)
            operand("op_qa", [(2 + c, col("q_a_norm", c)) for c in range(3)], U_QA + 1)
            for u in (U_KVB, U_KVB + 1):
                step(u, lambda t, u, c, w: kv[:, t, 4 * (u - U_KVB) + c // 256:4 * (u - U_KVB) + (c + w) // 256, :])
            for u in (U_QB, U_QB + 1):
                step(u, lambda t, u, c, w: q2[:, t, 4 * (u - U_QB) + c // QK:4 * (u - U_QB) + (c + w) // QK, :])
            act.wait_ge(s_evd, plan[U_QB + 1][3])
            act.wait_ge(s_eva, plan[U_QB + 1][2])
            for t in range(NT):
                nc.scalar.activation(tr[:, 3072 + t * 1024:3072 + (t + 1) * 1024].rearrange("p (h n) -> p h n", h=H2),
                                     kv[:, t, :, 0:NOPE], ACT.Square)
                ins = nc.scalar.activation(tr[:, t * 1536:(t + 1) * 1536].rearrange("p (h n) -> p h n", h=H2),
                                           q2[:, t, :, :], ACT.Square)
            ins.then_inc(ev["qk2_sq"], 1)
            act.wait_ge(ev["qk2_ss"], 1)
            sqrt("qk2", 32, QK, EPS)
            for r in range(4):
                rr = RD["k2"] + r
                act.wait_ge(s_tr, rr + 1)
                nc.scalar.activation(kT2[:, 2 * r:2 * r + 2, :], tp[rr % 2][:, :].rearrange("p (a n) -> p a n", a=2),
                                     ACT.Copy, scale=col("knope")).then_inc(s_tf[rr % 2], 1)
            for r in range(2):
                rr = RD["kpe"] + r
                act.wait_ge(s_tr, rr + 1)
                nc.scalar.activation(kpT[:, 2 * r:2 * r + 2, :], tp[rr % 2][:, :].rearrange("p (a n) -> p a n", a=2),
                                     ACT.Copy).then_inc(s_tf[rr % 2], 1)
            attention("mla")
            for u in range(U_MO, U_MO + 3):
                step(u)
            norm(3)
            operand("op_f2", [(c, col("ffn_norm", 8 + c)) for c in range(DC)], U_F2)
            ffn(U_F2)
            norm(4)
            operand("op_f3", [(c, col("ffn_pre", c)) for c in range(DC)], U_F3)
            ffn(U_F3)
            post_ffn(0, U_F3)
            norm(5)
            operand("op_conv", [(c, col("mix_pre", c)) for c in range(DC)], U_PW1)
            for w, chunks in enumerate(PW1):
                u = U_PW1 + w
                hi_b(u)
                hi_a(u + 1)
                for m, q in enumerate(chunks):
                    if q % 2:
                        c = q // 2
                        pw1_ready(act, u, m, c)
                        if c >= 2:
                            act.wait_ge(s_glu, c - 1)
                        nc.scalar.activation(sg[:, c % 2, :], gub[c % 2][:, T:2 * T], ACT.Sigmoid,
                                             bias=col("b_pw1", 8 + c)).then_inc(s_sig, 1)
            act.wait_ge(ev["conv_summed"], 1)
            for c in range(CONV_PE):
                ins = nc.scalar.activation(conv_c[:, CONV_DVE + c, :], acc[2 + c // 2][:, (c % 2) * T:(c % 2 + 1) * T],
                                           ACT.Identity, bias=col("b_dw", CONV_DVE + c))
            ins.then_inc(ev["sum_ready"], 1)
            for q in range(2):
                act.wait_ge(ev["centred"], q + 1)
                h = slice(4 * q, 4 * q + 4)
                nc.scalar.activation(conv_s[:, h, :], conv_c[:, h, :], ACT.Square).then_inc(ev["sq_ready"], 1)
            act.wait_ge(ev["var_done"], 1)
            nc.scalar.activation(conv_r[:, 0, :], acc[1][:, 0:T], ACT.Sqrt, bias=LN_EPS)\
                .then_inc(ev["conv_std"], 1)
            act.wait_ge(s_useb, U_PW2)
            for q in range(4):
                act.wait_ge(ev["lny_ready"], q + 1)
                for c in (2 * q, 2 * q + 1):
                    ins = nc.scalar.activation(conv_s[:, c, :], conv_c[:, c, :], ACT.Silu, scale=col("ln_g", c),
                                               bias=col("ln_b", c))
                own(ins)
                h = slice(2 * q, 2 * q + 2)
                nc.scalar.activation(hthi[:, h, :], conv_s[:, h, :], ACT.Copy).then_inc(ev["conv_hi"], 1)
            for u in range(U_PW2, U_PW2 + 3):
                step(u, lambda t, u, c, w: m_out[:, t, (u - U_PW2) * PITCH + c:(u - U_PW2) * PITCH + c + w])
            post_mixer(1, lambda: act.wait_ge(s_wu, 2))
            norm(6)
            operand("op_f4", [(c, col("ffn_pre", 8 + c)) for c in range(DC)], U_F4)
            ffn(U_F4)
            post_ffn(2, U_F4)
            norm(7)
            operand("op_f5", [(c, col("ffn_pre", 16 + c)) for c in range(DC)], U_F5)
            ffn(U_F5)
            post_ffn(3, U_F5)
            norm(8)
            operand("op_qkv", [(c, col("mix_pre", 8 + c)) for c in range(DC)], U_QKV)
            for u in range(U_QKV, U_QKV + 8):
                step(u, lambda t, u, c, w: p3[:, t, (u - U_QKV) * PITCH + c:(u - U_QKV) * PITCH + c + w])
            act.wait_ge(ev["kz_zeroed"], 2)
            for r in range(4):
                rr = RD["k3"] + r
                act.wait_ge(s_tr, rr + 1)
                for m in range(2):
                    ins = nc.scalar.activation(
                        kz[m * 64:(m + 1) * 64, m, 2 * r:2 * r + 2, :],
                        tp[rr % 2][m * 64:(m + 1) * 64, :].rearrange("p (a n) -> p a n", a=2), ACT.Copy)
                ins.then_inc(s_tf[rr % 2], 1)
            act.wait_ge(ev["lam_sum"], 1)
            nc.scalar.activation(lam[:, 2:4], lam[:, 0:2], ACT.Exp).then_inc(ev["lam_exp"], 1)
            attention("diff")
            act.wait_ge(s_od, 2 * H3)
            nc.scalar.activation(xflat, proj[:, 0:2048], ACT.Square).then_inc(ev["sub_sq"], 1)
            act.wait_ge(ev["sub_ss"], 1)
            sqrt("subln", 16, 2 * DH, SUBLN_EPS)
            operand("op_wo", [(c, sgain[:, 0:1]) for c in range(DC)], U_WO)
            for u in range(U_WO, U_WO + 3):
                step(u, lambda t, u, c, w: m_out[:, t, (u - U_WO) * PITCH + c:(u - U_WO) * PITCH + c + w])
            act.wait_ge(s_eva, plan[U_WO + 2][2])
            post_mixer(4, lambda: act.wait_ge(s_evd, plan[U_WO + 2][3]))
            norm(9)
            operand("op_f6", [(c, col("ffn_pre", 24 + c)) for c in range(DC)], U_F6)
            ffn(U_F6)
            post_ffn(5, U_F6)

        @block.tensor
        def _(pe):
            def mm3(out, whi_, wlo_, mhi, mlo, start, stop):
                nc.tensor.matmul(out, whi_, mhi, start=start, stop=False)
                nc.tensor.matmul(out, whi_, mlo, start=False, stop=False)
                return nc.tensor.matmul(out, wlo_, mhi, start=False, stop=stop)

            def bank_free(r):
                if r >= 2:
                    pe.wait_ge(s_tf[r % 2], r // 2)

            def rounds(name, cnt, per, blocks):
                for q in range(cnt):
                    r = RD[name] + q
                    bank_free(r)
                    for j, (rows_out, width, src) in enumerate(blocks(q)):
                        ins = nc.tensor.transpose(tp[r % 2][0:rows_out, j * per:j * per + width], src,
                                                  const[0:width, KO["ident"]:KO["ident"] + width])
                    ins.then_inc(s_tr, 1)

            def operand(name, src, nchunks):
                rounds(name, (nchunks + 1) // 2, P,
                       lambda q: [(P, P, src(t, 2 * q + j)) for j in range(min(2, nchunks - 2 * q)) for t in range(NT)])

            def taken(name, cnt):
                last = RD[name] + cnt - 1
                for r in (last - 1, last):
                    pe.wait_ge(s_tf[r % 2], r // 2 + 1)

            def step(u, k0=0, ready=None):
                kk, pitch, pieces = STEPS[u]
                s, end = u % 2, pieces[-1][0] + pieces[-1][1]
                banks, before, _, _ = plan[u]
                if before >= 0:
                    pe.wait_ge(s_eva, plan[before][2])
                    pe.wait_ge(s_evd, plan[before][3])
                pe.wait_ge(s_loa, u + 1)
                used_a = b_ready = False
                for k in range(kk):
                    if ready is not None:
                        ready(k)
                    if k * pitch + end > UA and not b_ready:
                        pe.wait_ge(s_lob, u + 1)
                        b_ready = True
                    for t in range(NT):
                        for j, (c, w) in enumerate(pieces):
                            sl = slice(k * pitch + c, k * pitch + c + w)
                            lhs = slice(t * P, (t + 1) * P)
                            ins = mm3(acc[banks[t][j]][:, 0:w], hthi[:, k0 + k, lhs], htlo[:, k0 + k, lhs],
                                      whi[:, s, sl], wlo[:, s, sl], k == 0, k == kk - 1)
                    if (k + 1) * pitch >= UA and not used_a:
                        ins.then_inc(s_usea, 1)
                        used_a = True
                ins.then_inc(s_useb, 1)

            def gate_up(f, c, i=0, op=None):
                s, b = (f + c) % 2, c % 2
                pe.wait_ge(s_loa, i * 2 + (f + c + 1))
                for half in range(2):
                    for k in range(DC):
                        if op is not None and half == 0 and k % 2 == 0:
                            r = RD[op] + k // 2
                            pe.wait_ge(s_tf[r % 2], r // 2 + 1)
                        at = half * 1024 + k * P
                        ins = mm3(gub[b][:, half * T:(half + 1) * T], whi[:, s, at:at + P], wlo[:, s, at:at + P],
                                  hthi[:, k, :], htlo[:, k, :], k == 0, k == DC - 1)
                ins.then_inc(s_usea, 1)

            def down(f, fi, c, i=0, start=False, stop=False):
                s, b = (f + c) % 2, c % 2
                pe.wait_ge(s_lob, i * 2 + (f + c + 1))
                pe.wait_ge(s_hid, i * 2 + (FC * fi + c + 1))
                for t in range(NT):
                    for j in range(2):
                        lhs, sl = slice(t * P, (t + 1) * P), slice(UA + j * 512, UA + (j + 1) * 512)
                        nc.tensor.matmul(acc[2 * t + j][:, :], hidhi[:, b, lhs], whi[:, s, sl], start=start, stop=False,
                                         skip_group_check=True)
                        nc.tensor.matmul(acc[2 * t + j][:, :], hidhi[:, b, lhs], wlo[:, s, sl], start=False, stop=False,
                                         skip_group_check=True)
                        ins = nc.tensor.matmul(acc[2 * t + j][:, :], hidlo[:, b, lhs], whi[:, s, sl], start=False,
                                               stop=stop, skip_group_check=True)
                ins.then_inc(s_useb, 1)

            def ffn(fi, op):
                f = FUNITS[fi]
                gate_up(f, 0, op=op)
                gate_up(f, 1)
                down(f, fi, 0, start=True)
                with pe.Fori(1, FC // 2) as i:
                    for j in range(2):
                        pe.wait_ge(s_hid, i * 2 + (FC * fi + j - 1))
                        gate_up(f, j, i)
                        down(f, fi, j - 1, i) if j else down_prev(f, fi, i)
                down(f, fi, FC - 1, stop=True)

            def down_prev(f, fi, i):
                s = (f + 1) % 2
                pe.wait_ge(s_lob, i * 2 + f)
                pe.wait_ge(s_hid, i * 2 + FC * fi)
                for t in range(NT):
                    for j in range(2):
                        lhs, sl = slice(t * P, (t + 1) * P), slice(UA + j * 512, UA + (j + 1) * 512)
                        for a, w in ((hidhi, whi), (hidhi, wlo), (hidlo, whi)):
                            ins = nc.tensor.matmul(acc[2 * t + j][:, :], a[:, 1, lhs], w[:, s, sl], start=False, stop=False,
                                                   skip_group_check=True)
                ins.then_inc(s_useb, 1)

            def attention(kind):
                base, cnt = ITEM0[kind], NITEM[kind]

                def scores(i):
                    g = base + i
                    if g >= 4:
                        pe.wait_ge(s_bia, g - 3)
                    b = acc[g % 4]
                    if kind == "nsa":
                        h, t = i // 2, i % 2
                        nk = P * (t + 1)
                        for br in range(2):
                            ins = nc.tensor.matmul(b[:, br * T:br * T + nk], qT[:, h // 2, t * P:(t + 1) * P],
                                                   kz[:, h % 2, br * G1 + h // 4, 0:nk], start=True, stop=True)
                    elif kind == "mla":
                        o = (i % 2) * ROPE
                        for t in range(NT):
                            nc.tensor.matmul(b[:, t * T:(t + 1) * T], qT[:, i, t * P:(t + 1) * P], kT2[:, i, :],
                                             start=True, stop=False)
                            ins = nc.tensor.matmul(b[:, t * T:(t + 1) * T], qpT[o:o + ROPE, i // 2, t * P:(t + 1) * P],
                                                   kpT[o:o + ROPE, i // 2, :], start=False, stop=True)
                    else:
                        h, t = i // 2, i % 2
                        for m in range(2):
                            ins = nc.tensor.matmul(b[:, m * T:(m + 1) * T], qT[:, h, t * P:(t + 1) * P], kz[:, m, h, :],
                                                   start=True, stop=True)
                    ins.then_inc(s_sco, 1)

                def transposes(i):
                    g, r = base + i, RD[kind] + i
                    pe.wait_ge(s_prob, g + 1)
                    bank_free(r)
                    for j, (br, k) in enumerate(item_blocks(kind, i)):
                        ins = nc.tensor.transpose(tp[r % 2][:, j * P:(j + 1) * P], s_pr[:, g % 2, br, k * P:(k + 1) * P],
                                                  ident)
                    ins.then_inc(s_tr, 1)

                def values(i):
                    g, r = base + i, RD[kind] + i
                    pe.wait_ge(s_tf[r % 2], r // 2 + 1)
                    blocks = item_blocks(kind, i)

                    def pt(j):
                        return s_pt[:, g % 2, j * P:(j + 1) * P]

                    if kind == "nsa":
                        h, t = i // 2, i % 2
                        if i % 4 == 0 and i >= 8:
                            pe.wait_ge(s_ol, i // 4 - 1)
                        out = gub[(h // 2) % 2][(h % 2) * 64:(h % 2 + 1) * 64, t * P:(t + 1) * P]
                        nc.tensor.matmul(out, vcmp[:, :], pct[t][:, h, :], start=True, stop=False)
                        for j, (br, k) in enumerate(blocks):
                            c = (COL_VS, COL_VW)[br] + (h // 4) * DH
                            ins = nc.tensor.matmul(out, p1[:, k, c:c + DH], pt(j), start=False, stop=j == len(blocks) - 1)
                    elif kind == "mla":
                        pe.wait_ge(s_ol, 8 + i - 1)
                        out = gub[i % 2]
                        nc.tensor.matmul(out[:, 0:P], kv[:, 0, i, NOPE:], pt(0), start=True, stop=True)
                        nc.tensor.matmul(out[:, P:T], kv[:, 0, i, NOPE:], pt(1), start=True, stop=False)
                        ins = nc.tensor.matmul(out[:, P:T], kv[:, 1, i, NOPE:], pt(2), start=False, stop=True)
                    else:
                        h = i // 2
                        if i >= 2:
                            pe.wait_ge(s_od, i - 1)
                        for k in range(NT):
                            ins = nc.tensor.matmul(gub[g % 2][:, 0:P], pt(k), p3[:, k, 2048 + h * P:2048 + (h + 1) * P],
                                                   start=k == 0, stop=k == NT - 1)
                    ins.then_inc(s_pv, 1)

                scores(0)
                for i in range(cnt + 2):
                    if i + 1 < cnt:
                        scores(i + 1)
                    if 1 <= i <= cnt:
                        transposes(i - 1)
                    if i >= 2:
                        values(i - 2)

            def xn_chunk(t, c):
                return xn[:, t, c * P:(c + 1) * P]

            pe.wait_ge(s_ldk, 16)
            pe.wait_ge(s_xn, 2)
            operand("op_attn", xn_chunk, DC)
            taken("op_attn", 4)
            for u in range(U_IN, U_IN + 7):
                step(u)
            pe.wait_ge(s_eva, 7)
            pe.wait_ge(s_evd, 7)
            rounds("kcvc", 2, P, lambda q: [(P, P, p1[:, t, COL_KC + q * T + a * P:COL_KC + q * T + (a + 1) * P])
                                            for a in range(2) for t in range(NT)])
            pe.wait_ge(ev["blk_ready"], 1)
            for w in range(3):
                u = U_CMP + w
                s = u % 2
                for m in range(12 if w < 2 else 8):
                    if m == 0:
                        pe.wait_ge(s_loa, u + 1)
                    if m == 8:
                        pe.wait_ge(s_lob, u + 1)
                    e = 12 * w + m
                    for half in range(2):
                        at = m * CMP_HIDDEN + half * P
                        mv = slice(e * GJ, (e + 1) * GJ)
                        ins = mm3(acc[(e // 16) * 2 + half][:, 0:GJ], whi[:, s, at:at + P], wlo[:, s, at:at + P],
                                  blkhi[:, mv], blklo[:, mv], e % 16 == 0, e % 16 == 15)
                        if w == 2 and m == 7 and half == 0:
                            pe.wait_ge(s_lob, u + 1)
                            ins.then_inc(s_useb, 1)
                    if m == 7:
                        ins.then_inc(s_usea, 1)
                if w < 2:
                    ins.then_inc(s_useb, 1)
            pe.wait_ge(ev["qn_ready"], 1)
            rounds("q1", 4, P, lambda q: [(P, P, p1[:, t, c * P:(c + 1) * P]) for c in (2 * q, 2 * q + 1) for t in range(NT)])
            pe.wait_ge(ev["kd_ready"], 1)
            rounds("k1", 4, P, lambda q: [(P, P, kd[:, t, g, :, :].rearrange("p d n -> p (d n)"))
                                          for g in (2 * q, 2 * q + 1) for t in range(NT)])
            pe.wait_ge(ev["gelu_ready"], 1)
            for v in range(2):
                for half in range(2):
                    ins = nc.tensor.matmul(gub[0][0:GJ, v * DH:(v + 1) * DH], att[:, 720 + (2 * v + half) * GJ:720 + (2 * v + half + 1) * GJ],
                                           cols[:, CO["w2"] + (2 * v + half) * DH:CO["w2"] + (2 * v + half + 1) * DH],
                                           start=half == 0, stop=half == 1)
            ins.then_inc(ev["w2_done"], 1)
            pe.wait_ge(ev["kcd_ready"], 1)
            rounds("kcmp", 1, P, lambda q: [(P, GJ, kcd[:, :, :].rearrange("p d n -> p (d n)"))])
            taken("kcmp", 1)
            for t in range(NT):
                if t == 1:
                    pe.wait_ge(ev["cm0"], 1)
                for h in range(H1):
                    ins = nc.tensor.matmul(acc[2 + h // 8][:, (h % 8) * GJ:(h % 8 + 1) * GJ], qT[:, h // 2, t * P:(t + 1) * P],
                                           kcz[:, h % 2, :], start=True, stop=True)
                ins.then_inc(ev[f"cs{t}"], 1)
            for t in range(NT):
                pe.wait_ge(ev[f"cp{t}"], 1)
                rounds(f"pc{t}", 4, P, lambda q: [(GJ, P, att[:, 1024 + (4 * q + j) * GJ:1024 + (4 * q + j + 1) * GJ])
                                                  for j in range(4)])
            taken("pc1", 4)
            attention("nsa")
            pe.wait_ge(s_ol, 8)
            for u in range(U_OUT, U_OUT + 3):
                step(u)
            pe.wait_ge(s_xn, 4)
            operand("op_f1", xn_chunk, DC)
            ffn(0, "op_f1")
            pe.wait_ge(s_xn, 6)
            operand("op_kv", xn_chunk, DC)
            taken("op_kv", 4)
            step(U_KVA)
            operand("op_bq", xn_chunk, DC)
            taken("op_bq", 4)
            step(U_QA)
            pe.wait_ge(ev["ckv_ready"], 1)
            operand("op_ckv", lambda t, c: kva[:, t, c * P:(c + 1) * P], 2)
            pe.wait_ge(ev["qa_ready"], 1)
            operand("op_qa", lambda t, c: qa[:, t, c * P:(c + 1) * P], 3)
            taken("op_qa", 2)
            for u in (U_KVB, U_KVB + 1):
                step(u)
            for u in (U_QB, U_QB + 1):
                step(u, 2)
            pe.wait_ge(ev["k2n_ready"], 1)
            rounds("k2", 4, P, lambda q: [(P, P, kv[:, t, h, 0:NOPE]) for h in (2 * q, 2 * q + 1) for t in range(NT)])
            pe.wait_ge(ev["q2n_ready"], 1)
            rounds("q2", 4, P, lambda q: [(P, P, q2[:, t, h, 0:NOPE]) for h in (2 * q, 2 * q + 1) for t in range(NT)])
            pe.wait_ge(ev["kpe_ready"], 1)
            rounds("kpe", 2, P, lambda q: [(P, P, kpe[:, t, 2 * c:2 * c + 2, :].rearrange("p a n -> p (a n)"))
                                           for c in (2 * q, 2 * q + 1) for t in range(NT)])
            pe.wait_ge(ev["qpe_ready"], 1)
            rounds("qpe", 2, P, lambda q: [(P, P, qpe[:, t, 2 * c:2 * c + 2, :].rearrange("p a n -> p (a n)"))
                                           for c in (2 * q, 2 * q + 1) for t in range(NT)])
            taken("qpe", 2)
            attention("mla")
            pe.wait_ge(s_ol, 16)
            for u in range(U_MO, U_MO + 3):
                step(u)
            pe.wait_ge(s_xn, 8)
            operand("op_f2", xn_chunk, DC)
            ffn(1, "op_f2")
            pe.wait_ge(s_xn, 10)
            operand("op_f3", xn_chunk, DC)
            ffn(2, "op_f3")
            pe.wait_ge(s_xn, 12)
            operand("op_conv", xn_chunk, DC)
            taken("op_conv", 4)
            for w, chunks in enumerate(PW1):
                u = U_PW1 + w
                s = u % 2
                pe.wait_ge(s_loa, u + 1)
                for m, q in enumerate(chunks):
                    if m == 2:
                        pe.wait_ge(s_lob, u + 1)
                    if q % 2 == 0 and q >= 4:
                        pe.wait_ge(s_glu, q // 2 - 1)
                    for k in range(DC):
                        at = m * 1024 + k * P
                        ins = mm3(gub[(q // 2) % 2][:, (q % 2) * T:(q % 2 + 1) * T], whi[:, s, at:at + P],
                                  wlo[:, s, at:at + P], hthi[:, k, :], htlo[:, k, :], k == 0, k == DC - 1)
                        if len(chunks) == 2 and m == 1 and k == 0:
                            pe.wait_ge(s_lob, u + 1)
                            ins.then_inc(s_useb, 1)
                    if m == 0 and q % 2:
                        ins.then_inc(s_pw, 1)
                    if m == 1:
                        ins.then_inc(s_usea, 1)
                    if m == 2:
                        ins.then_inc(s_useb, 1)
            pe.wait_ge(ev["diagonals_ready"], 1)
            pe.wait_ge(s_glu, 8)
            for c, k0, cnt, part, at in diag_runs:
                b = c - CONV_DVE
                for k in range(k0, k0 + cnt):
                    ins = nc.tensor.matmul(acc[2 + b // 2][:, (b % 2) * T:(b % 2 + 1) * T], diag[part][:, at + k - k0, :],
                                           conv_u[:, c, k:k + T], start=k == 0, stop=k == TAPS - 1)
            ins.then_inc(ev["conv_summed"], 1)
            pe.wait_ge(ev["conv_early"], 1)
            for c in (0, 1):
                nc.tensor.matmul(acc[0][:, 0:T], ones, conv_c[:, c, :], start=c == 0, stop=False)
            pe.wait_ge(ev["sum_ready"], 1)
            for c in range(CONV_DVE, 8):
                nc.tensor.matmul(acc[0][:, 0:T], ones, conv_c[:, c, :], start=False, stop=False)
            pe.wait_ge(ev["conv_ready"], 1)
            for c in range(2, CONV_DVE):
                ins = nc.tensor.matmul(acc[0][:, 0:T], ones, conv_c[:, c, :], start=False, stop=c == CONV_DVE - 1)
            ins.then_inc(ev["mean_done"], 1)
            for c in range(8):
                if c % 4 == 0:
                    pe.wait_ge(ev["sq_ready"], c // 4 + 1)
                ins = nc.tensor.matmul(acc[1][:, 0:T], ones, conv_s[:, c, :], start=c == 0, stop=c == 7)
            ins.then_inc(ev["var_done"], 1)
            step(U_PW2, ready=lambda k: pe.wait_ge(ev["conv_lo"], k // 2 + 1) if k % 2 == 0 else None)
            for u in range(U_PW2 + 1, U_PW2 + 3):
                step(u)
            pe.wait_ge(s_xn, 14)
            operand("op_f4", xn_chunk, DC)
            ffn(3, "op_f4")
            pe.wait_ge(s_xn, 16)
            operand("op_f5", xn_chunk, DC)
            ffn(4, "op_f5")
            pe.wait_ge(s_xn, 18)
            operand("op_qkv", xn_chunk, DC)
            taken("op_qkv", 4)
            for u in range(U_QKV, U_QKV + 8):
                step(u)
            pe.wait_ge(s_eva, plan[U_QKV + 7][2])
            pe.wait_ge(s_evd, plan[U_QKV + 7][3])
            for name, at in (("q3", 0), ("k3", 1024)):
                rounds(name, 4, P, lambda q, at=at: [(P, P, p3[:, t, at + c * P:at + (c + 1) * P])
                                                     for c in (2 * q, 2 * q + 1) for t in range(NT)])
            taken("k3", 4)
            attention("diff")
            pe.wait_ge(ev["sub_ready"], 1)
            operand("op_wo", lambda t, c: diff_o[:, t, c * P:(c + 1) * P], DC)
            taken("op_wo", 4)
            for u in range(U_WO, U_WO + 3):
                step(u)
            pe.wait_ge(s_xn, 20)
            operand("op_f6", xn_chunk, DC)
            ffn(5, "op_f6")

        @block.vector
        def _(dve):
            n = dict(own=0)
            V = nc.vector

            def own(ins):
                n["own"] += 1
                ins.then_inc(s_dve, 1)
                dve.wait_ge(s_dve, n["own"])

            def lo_a(u, i=0):
                s = u % 2
                dve.wait_ge(s_hia, i * 2 + (u + 1))
                V.tensor_tensor(wlo[:, s, 0:UA], raw[:, s, 0:UA], whi[:, s, 0:UA].bitcast(F32), ALU.subtract)\
                    .then_inc(s_loa, 1)

            def lo_b(u, i=0):
                s = u % 2
                dve.wait_ge(s_hib, i * 2 + (u + 1))
                V.tensor_tensor(wlo[:, s, UA:UNIT], raw[:, s, UA:UNIT], whi[:, s, UA:UNIT].bitcast(F32), ALU.subtract)\
                    .then_inc(s_lob, 1)

            def step(u, dst=None):
                lo_b(u)
                lo_a(u + 1)
                banks = plan[u][0]
                dve.wait_ge(s_useb, u + 1)
                if dst is not None:
                    for j, (c, w) in enumerate(STEPS[u][2]):
                        src = acc[banks[1][j]][:, 0:w]
                        out = dst(1, u, c, w)
                        ins = V.tensor_copy(out, src)
                    ins.then_inc(s_evd, 1)

            def add_steps(first):
                for u in range(first, first + 3):
                    step(u)
                    a, w = (u - first) * PITCH, STEPS[u][2][0][1]
                    for t in range(NT):
                        ins = V.tensor_tensor(x[:, t, a:a + w], x[:, t, a:a + w], acc[plan[u][0][t][0]][:, 0:w], ALU.add)
                        if u == first + 2:
                            ins.then_inc(s_x, 1)
                    if u < first + 2:
                        ins.then_inc(s_evd, 1)

            def rstd(name, cnt, r=P):
                dve.wait_ge(s_std, RSTD[name] + 1)
                V.reciprocal(rs[0:r, 0:cnt], std[0:r, 0:cnt]).then_inc(s_rs, 1)
                dve.wait_ge(s_rs, RSTD[name] + 1)

            def norm(m):
                rstd(f"n{m}", 2)
                for t in range(NT):
                    V.tensor_scalar(xn[:, t, :], x[:, t, :], rs[:, t:t + 1], None, ALU.mult).then_inc(s_xn, 1)

            def operand(name, chunks):
                for a in range(0, len(chunks), 2):
                    r = RD[name] + a // 2
                    dve.wait_ge(s_thi, OPN[name] + a // 2 + 1)
                    for j, (dst, gain) in enumerate(chunks[a:a + 2]):
                        ins = V.scalar_tensor_tensor(out=htlo[:, dst, :], in0=tp[r % 2][:, j * T:(j + 1) * T],
                                                     scalar=gain, in1=hthi[:, dst, :].bitcast(F32),
                                                     op0=ALU.mult, op1=ALU.subtract)
                    ins.then_inc(s_tf[r % 2], 1)

            def ffn(fi):
                f = FUNITS[fi]
                with dve.Fori(0, FC // 2) as i:
                    for j in range(2):
                        lo_a(f + j + 1, i)
                        dve.wait_ge(s_silu, i * 2 + (FC * fi + j + 1))
                        V.tensor_tensor(hidf[:, j, :], sg[:, j, :], gub[j][:, T:2 * T], ALU.mult).then_inc(s_hf, 1)
                        dve.wait_ge(s_hf, i * 2 + (FC * fi + j + 1))
                        dve.wait_ge(s_useb, i * 2 + (f + j - 1))
                        V.tensor_copy(hidhi[:, j, :], hidf[:, j, :]).then_inc(s_hh, 1)
                        dve.wait_ge(s_hh, i * 2 + (FC * fi + j + 1))
                        V.tensor_tensor(hidlo[:, j, :], hidf[:, j, :], hidhi[:, j, :].bitcast(F32), ALU.subtract)\
                            .then_inc(s_hid, 1)
                        lo_b(f + j, i)

            def add_ffn(f):
                dve.wait_ge(s_useb, f + FC)
                for t in range(NT):
                    for j in range(2):
                        sl = slice(j * 512, (j + 1) * 512)
                        ins = V.tensor_tensor(x[:, t, sl], x[:, t, sl], acc[2 * t + j][:, :], ALU.add)
                    ins.then_inc(s_x, 1)

            def post_ffn(k, row):
                dve.wait_ge(s_pss, [0, None, 1, 2, None, 3][k] + 1)
                V.tensor_tensor(ss[:, 0:2], ss[:, 8:12].rearrange("p (t j) -> p t j", j=2)[:, :, 0],
                                ss[:, 8:12].rearrange("p (t j) -> p t j", j=2)[:, :, 1], ALU.add).then_inc(s_phs, 1)
                rstd(f"post{k}", 2)
                dve.wait_ge(s_ldw[row % 2], 16 * (row // 2 + 1))
                for t in range(NT):
                    for j in range(2):
                        sl = slice(j * 512, (j + 1) * 512)
                        ins = V.scalar_tensor_tensor(out=xn[:, t, sl], in0=acc[2 * t + j][:, :], scalar=rs[:, t:t + 1],
                                                     in1=wide[:, row % 2, sl], op0=ALU.mult, op1=ALU.mult)
                ins.then_inc(s_wu, 1)
                dve.wait_ge(s_wu, row + 1)
                for t in range(NT):
                    V.scalar_tensor_tensor(out=x[:, t, :], in0=xn[:, t, :], scalar=0.5, in1=x[:, t, :],
                                           op0=ALU.mult, op1=ALU.add).then_inc(s_x, 1)

            def post_mixer(k, row):
                rstd(f"post{k}", 2)
                dve.wait_ge(s_ldw[row % 2], 16 * (row // 2 + 1))
                for t in range(NT):
                    ins = V.scalar_tensor_tensor(out=xn[:, t, :], in0=m_out[:, t, :], scalar=rs[:, t:t + 1],
                                                 in1=wide[:, row % 2, :], op0=ALU.mult, op1=ALU.mult)
                ins.then_inc(s_wu, 1)
                dve.wait_ge(s_wu, row + 1)
                for t in range(NT):
                    V.tensor_tensor(x[:, t, :], x[:, t, :], xn[:, t, :], ALU.add).then_inc(s_x, 1)

            def attention(kind):
                base, cnt = ITEM0[kind], NITEM[kind]

                def bias(i):
                    g, t = base + i, i % 2
                    dve.wait_ge(s_sco, g + 1)
                    if g >= 2:
                        dve.wait_ge(s_exp, g - 1)
                    nk = P * (t + 1) if kind == "nsa" else T
                    src = acc[g % 4][:, :].rearrange("p (b n) -> p b n", b=2)[:, :, 0:nk]
                    out = s_sc[:, g % 2, :, 0:nk]
                    if kind == "mla":
                        own(V.scalar_tensor_tensor(out=out, in0=src, scalar=float(QK) ** -0.5,
                                                   in1=const[:, KO["mask"]:KO["mask"] + 512].rearrange("p (t n) -> p t n", t=2),
                                                   op0=ALU.mult, op1=ALU.add))
                    else:
                        k = KO["causal" if kind == "nsa" else "dist"] + t * T
                        slope = SLOPES1[i // 2] if kind == "nsa" else -SLOPES3[i // 2]
                        own(V.scalar_tensor_tensor(out=out, in0=const[:, k:k + nk].unsqueeze(1).to_broadcast([P, 2, nk]),
                                                   scalar=slope, in1=src, op0=ALU.mult, op1=ALU.add))
                    V.tensor_reduce(nmax[:, g % 2, 0:2], out, AX, ALU.max, negate=True).then_inc(s_bia, 1)

                def probs(i):
                    g, t = base + i, i % 2
                    s = g % 2
                    nk = P * (t + 1) if kind == "nsa" else T
                    dve.wait_ge(s_exp, g + 1)
                    own(V.reciprocal(pw[:, s, 0:2], lsum[:, s, 0:2]))
                    if kind == "nsa":
                        h = i // 2
                        own(V.tensor_tensor(pw[:, s, 2:4], pw[:, s, 0:2], gates[:, t, 3 * h + 1:3 * h + 3], ALU.mult))
                        for b in range(2):
                            ins = V.tensor_scalar(s_pr[:, s, b, 0:nk], s_pr[:, s, b, 0:nk], pw[:, s, 2 + b:3 + b], None, ALU.mult)
                    elif kind == "mla":
                        for b in range(2):
                            ins = V.tensor_scalar(s_pr[:, s, b, :], s_pr[:, s, b, :], pw[:, s, b:b + 1], None, ALU.mult)
                    else:
                        V.tensor_scalar(pw[:, s, 2:3], pw[:, s, 1:2], lam[:, 4:5], None, ALU.mult)
                        own(V.tensor_scalar(s_pr[:, s, 0, :], s_pr[:, s, 0, :], pw[:, s, 0:1], None, ALU.mult))
                        ins = V.scalar_tensor_tensor(out=s_pr[:, s, 0, :], in0=s_pr[:, s, 1, :], scalar=pw[:, s, 2:3],
                                                     in1=s_pr[:, s, 0, :], op0=ALU.mult, op1=ALU.add)
                    ins.then_inc(s_prob, 1)

                def post(i):
                    if kind == "nsa" and i % 4 == 3:
                        c = i // 4
                        dve.wait_ge(s_oh, c + 1)
                        V.tensor_tensor(htlo[:, c, :], gub[c % 2][:, 0:T], hthi[:, c, :].bitcast(F32), ALU.subtract)\
                            .then_inc(s_ol, 1)
                    if kind == "mla":
                        dve.wait_ge(s_oh, 8 + i + 1)
                        V.tensor_tensor(htlo[:, i, :], gub[i % 2][:, 0:T], hthi[:, i, :].bitcast(F32), ALU.subtract)\
                            .then_inc(s_ol, 1)

                for i in range(cnt + 2):
                    if i < cnt:
                        bias(i)
                    if 1 <= i <= cnt:
                        probs(i - 1)
                    if i >= 2:
                        post(i - 2)

            lo_a(0)
            dve.wait_ge(s_ldc, 16)
            dve.wait_ge(s_ldk, 16)
            dve.wait_ge(s_ldr, 16)
            norm(0)
            operand("op_attn", [(c, col("attn_norm", c)) for c in range(DC)])
            for u in range(U_IN, U_IN + 7):
                step(u, lambda t, u, c, w: p1[:, t, (u - U_IN) * PITCH + c:(u - U_IN) * PITCH + c + w])
            for v in range(2):
                r = RD["kcvc"] + v
                dve.wait_ge(s_tr, r + 1)
                for b in range(2):
                    src = tp[r % 2][64 * b:64 * b + 64, :].rearrange("p (a n) -> p a n", a=2)
                    V.tensor_copy(kc2[0:64, v, :, b, :], src)
                    ins = V.tensor_copy(kc2[64:128, v, :, b, 0:T - 1], src[:, :, 1:T])
                ins.then_inc(s_tf[r % 2], 1)
                dve.wait_ge(s_tf[r % 2], r // 2 + 1)
            for v in range(2):
                for half in range(2):
                    src = kc2[:, v, :, :, :].rearrange("p a b n -> p (a b) n").rearrange("p g (j c r) -> p g j c r", c=8, r=2)
                    src = src[:, :, half:half + NCMP, :, 0].rearrange("p g j c -> p c g j")
                    at = (v * 16 + half * 8) * GJ
                    pos = cols[:, CO["pos"] + v * 16 + half * 8:CO["pos"] + v * 16 + half * 8 + 8]
                    for c in range(8):
                        ins = V.tensor_scalar(blk[:, at + c * GJ:at + (c + 1) * GJ].rearrange("p (g j) -> p g j", g=G1),
                                              src[:, c, :, :], pos[:, c:c + 1], None, ALU.add)
            own(ins)
            own(V.tensor_copy(blkhi, blk))
            V.tensor_tensor(blklo, blk, blkhi.bitcast(F32), ALU.subtract).then_inc(ev["blk_ready"], 1)
            lo_b(U_CMP)
            lo_a(U_CMP + 1)
            dve.wait_ge(ev["sq1_ready"], 1)
            V.tensor_reduce(ss[:, 0:48], tr[:, 2048:2048 + 3072].rearrange("p (a n) -> p a n", n=DH), AX, ALU.add)\
                .then_inc(ev["ss1_ready"], 1)
            dve.wait_ge(ev["ss1_ready"], 1)
            V.memset(kz[64:128, 0, :, :], 0.0)
            V.memset(kz[0:64, 1, :, :], 0.0).then_inc(ev["kz_zeroed"], 1)
            V.memset(kcz[64:128, 0, :], 0.0)
            V.memset(kcz[0:64, 1, :], 0.0)
            rstd("qk1", 48)
            dve.wait_ge(ev["blk_ready"], 1)
            for t in range(NT):
                qv = p1[:, t, 0:1024].rearrange("p (h n) -> p h n", h=H1)
                ins = V.tensor_tensor(qv, qv, rs[:, 24 * t:24 * t + 16].unsqueeze(2).to_broadcast([P, H1, DH]), ALU.mult)
            ins.then_inc(ev["qn_ready"], 1)
            for t in range(NT):
                for b in range(2):
                    c = (COL_KS, COL_KW)[b]
                    src = p1[:, t, c:c + 256].rearrange("p (g n) -> p g n", g=G1)
                    r = rs[:, 24 * t + 16 + 4 * b:24 * t + 20 + 4 * b].unsqueeze(2).to_broadcast([P, G1, DH])
                    for d in range(2):
                        ins = V.tensor_tensor(kd[:, t, 4 * b:4 * b + 4, d, :], src, r, ALU.mult)
            ins.then_inc(ev["kd_ready"], 1)
            for u in (U_CMP + 1, U_CMP + 2):
                lo_b(u)
                lo_a(u + 1)
            for r in range(4):
                rr = RD["q1"] + r
                dve.wait_ge(s_tr, rr + 1)
                V.tensor_scalar(qT[:, 2 * r:2 * r + 2, :], tp[rr % 2][:, :].rearrange("p (a n) -> p a n", a=2),
                                col("q_norm"), DH ** -0.5, ALU.mult, ALU.mult).then_inc(s_tf[rr % 2], 1)
            dve.wait_ge(ev["hx_ready"], 1)
            own(V.tensor_tensor(att[:, 240:480], att[:, 0:240], att[:, 0:240], ALU.mult))
            own(V.tensor_scalar(att[:, 240:480], att[:, 240:480], 0.044715, 1.0, ALU.mult, ALU.add))
            V.tensor_tensor(att[:, 240:480], att[:, 240:480], att[:, 0:240], ALU.mult).then_inc(ev["gelu_in"], 1)
            dve.wait_ge(ev["gelu_sig"], 1)
            V.tensor_tensor(att[:, 720:960], att[:, 480:720], att[:, 0:240], ALU.mult).then_inc(ev["gelu_ready"], 1)
            rstd("kcmp", 1, GJ)
            V.tensor_copy(vcmp[:, :], gub[0][0:GJ, DH:2 * DH])
            for d in range(2):
                ins = V.tensor_scalar(kcd[:, d, :], gub[0][0:GJ, 0:DH], rs[0:GJ, 0:1], None, ALU.mult)
            ins.then_inc(ev["kcd_ready"], 1)
            dve.wait_ge(ev["gates_ready"], 1)
            dve.wait_ge(s_ldbc, 16)
            for t in range(NT):
                sc = att[:, 0:H1 * GJ]
                pc = att[:, 1024:1024 + H1 * GJ]
                dve.wait_ge(ev[f"cs{t}"], 1)
                for b in range(2):
                    w = 8 * GJ
                    k = (2 * t + b) * w
                    ins = V.tensor_tensor(sc[:, b * w:(b + 1) * w], biasc[:, k:k + w], acc[2 + b][:, 0:w], ALU.add)
                own(ins)
                sv, pv = sc.rearrange("p (h n) -> p h n", h=H1), pc.rearrange("p (h n) -> p h n", h=H1)
                own(V.tensor_reduce(cst[:, 0, :], sv, AX, ALU.max))
                V.tensor_tensor(sv, sv, cst[:, 0, :].unsqueeze(2).to_broadcast([P, H1, GJ]), ALU.subtract)\
                    .then_inc(ev[f"cm{t}"], 1)
                dve.wait_ge(ev[f"ce{t}"], 1)
                own(V.tensor_reduce(cst[:, 1, :], pv, AX, ALU.add))
                own(V.reciprocal(cst[:, 2, :], cst[:, 1, :]))
                own(V.scalar_tensor_tensor(out=cst[:, 3, :], in0=cst[:, 2, :],
                                           scalar=const[:, KO["valid"] + t:KO["valid"] + t + 1],
                                           in1=gates[:, t, :].rearrange("p (h n) -> p h n", n=3)[:, :, 0],
                                           op0=ALU.mult, op1=ALU.mult))
                V.tensor_tensor(pv, pv, cst[:, 3, :].unsqueeze(2).to_broadcast([P, H1, GJ]), ALU.mult)\
                    .then_inc(ev[f"cp{t}"], 1)
            attention("nsa")
            add_steps(U_OUT)
            norm(1)
            operand("op_f1", [(c, col("ffn_norm", c)) for c in range(DC)])
            ffn(0)
            add_ffn(U_F1)
            norm(2)
            operand("op_kv", [(c, col("kv_norm", c)) for c in range(DC)])
            step(U_KVA, lambda t, u, c, w: kva[:, t, c:c + w])
            operand("op_bq", [(c, col("b_attn_norm", c)) for c in range(DC)])
            rstd("ckv", 2)
            for t in range(NT):
                ins = V.tensor_scalar(kva[:, t, 0:KVL], kva[:, t, 0:KVL], rs[:, t:t + 1], None, ALU.mult)
            ins.then_inc(ev["ckv_ready"], 1)
            step(U_QA, lambda t, u, c, w: qa[:, t, c:c + w])
            rstd("qan", 2)
            for t in range(NT):
                ins = V.tensor_scalar(qa[:, t, :], qa[:, t, :], rs[:, t:t + 1], None, ALU.mult)
            ins.then_inc(ev["qa_ready"], 1)
            operand("op_ckv", [(c, col("kv_c_norm", c)) for c in range(2)])
            operand("op_qa", [(2 + c, col("q_a_norm", c)) for c in range(3)])
            for u in (U_KVB, U_KVB + 1):
                step(u, lambda t, u, c, w: kv[:, t, 4 * (u - U_KVB) + c // 256:4 * (u - U_KVB) + (c + w) // 256, :])
            for u in (U_QB, U_QB + 1):
                step(u, lambda t, u, c, w: q2[:, t, 4 * (u - U_QB) + c // QK:4 * (u - U_QB) + (c + w) // QK, :])
            dve.wait_ge(ev["qk2_sq"], 1)
            own(V.tensor_reduce(ss[:, 0:16], tr[:, 3072:5120].rearrange("p (a n) -> p a n", n=NOPE), AX, ALU.add))
            V.tensor_reduce(ss[:, 16:32], tr[:, 0:3072].rearrange("p (a n) -> p a n", n=QK), AX, ALU.add)
            for t in range(NT):
                ins = V.tensor_scalar(ss[:, 8 * t:8 * t + 8], ss[:, 8 * t:8 * t + 8], ss[:, 40 + t:41 + t], None, ALU.add)
            ins.then_inc(ev["qk2_ss"], 1)
            rstd("qk2", 32)

            def per_head(r0, w):
                return rs[:, r0:r0 + H2].unsqueeze(2).to_broadcast([P, H2, w])

            def on_heads(k, w):
                return k.unsqueeze(1).to_broadcast([P, H2, w])

            for t in range(NT):
                ins = V.tensor_tensor(kv[:, t, :, 0:NOPE], kv[:, t, :, 0:NOPE], per_head(8 * t, NOPE), ALU.mult)
            ins.then_inc(ev["k2n_ready"], 1)
            for t in range(NT):
                ins = V.tensor_tensor(q2[:, t, :, :], q2[:, t, :, :], per_head(16 + 8 * t, QK), ALU.mult)
            ins.then_inc(ev["q2n_ready"], 1)
            dve.wait_ge(ev["q2n_ready"], 1)
            for t in range(NT):
                ins = V.tensor_tensor(kpe[:, t, :, :], on_heads(kva[:, t, KVL:KVL + ROPE], ROPE), per_head(8 * t, ROPE), ALU.mult)
            own(ins)
            for t in range(NT):
                V.tensor_tensor(kpe[:, t, :, :], kpe[:, t, :, :], on_heads(rows[:, RO["kpe"]:RO["kpe"] + ROPE], ROPE), ALU.mult)
                ins = V.tensor_tensor(q2[:, t, :, NOPE:], q2[:, t, :, NOPE:], on_heads(rows[:, RO["qpe"]:RO["qpe"] + ROPE], ROPE), ALU.mult)
            own(ins)
            hr = ROPE // 2
            for name, src, dst in (("kpe_ready", [kpe[:, t, :, :] for t in range(NT)], kpe),
                                   ("qpe_ready", [q2[:, t, :, NOPE:] for t in range(NT)], qpe)):
                pr = [[xflat[:, (4 * t + q) * 256:(4 * t + q + 1) * 256].rearrange("p (h n) -> p h n", h=H2)
                       for q in range(4)] for t in range(NT)]
                for t in range(NT):
                    cos = on_heads(const[:, KO["cos"] + t * hr:KO["cos"] + (t + 1) * hr], hr)
                    sin = on_heads(const[:, KO["sin"] + t * hr:KO["sin"] + (t + 1) * hr], hr)
                    x1, x2 = src[t][:, :, 0:hr], src[t][:, :, hr:ROPE]
                    for q, (a, b) in enumerate(((x1, cos), (x2, sin), (x1, sin), (x2, cos))):
                        ins = V.tensor_tensor(pr[t][q], a, b, ALU.mult)
                own(ins)
                for t in range(NT):
                    V.tensor_tensor(dst[:, t, :, 0:hr], pr[t][0], pr[t][1], ALU.subtract)
                    ins = V.tensor_tensor(dst[:, t, :, hr:ROPE], pr[t][2], pr[t][3], ALU.add)
                ins.then_inc(ev[name], 1)
                dve.wait_ge(ev[name], 1)
            for r in range(4):
                rr = RD["q2"] + r
                dve.wait_ge(s_tr, rr + 1)
                V.tensor_scalar(qT[:, 2 * r:2 * r + 2, :], tp[rr % 2][:, :].rearrange("p (a n) -> p a n", a=2),
                                col("qnope"), None, ALU.mult).then_inc(s_tf[rr % 2], 1)
            for r in range(2):
                rr = RD["qpe"] + r
                dve.wait_ge(s_tr, rr + 1)
                V.tensor_copy(qpT[:, 2 * r:2 * r + 2, :], tp[rr % 2][:, :].rearrange("p (a n) -> p a n", a=2))\
                    .then_inc(s_tf[rr % 2], 1)
            attention("mla")
            add_steps(U_MO)
            norm(3)
            operand("op_f2", [(c, col("ffn_norm", 8 + c)) for c in range(DC)])
            ffn(1)
            add_ffn(U_F2)
            norm(4)
            operand("op_f3", [(c, col("ffn_pre", c)) for c in range(DC)])
            ffn(2)
            post_ffn(0, 0)
            norm(5)
            V.memset(conv_u[:, :, 0:PAD], 0.0)
            V.memset(conv_u[:, :, PAD + T:], 0.0)
            operand("op_conv", [(c, col("mix_pre", c)) for c in range(DC)])
            def conv_taps(chunks_, k0, k1, ready=None):
                for k in range(k0, k1):
                    for c in chunks_:
                        w = col("w_dw", k * 8 + c)
                        if k == 0:
                            ins = V.tensor_scalar(conv_c[:, c, :], conv_u[:, c, 0:T], w, col("b_dw", c), ALU.mult, ALU.add)
                        else:
                            ins = V.scalar_tensor_tensor(out=conv_c[:, c, :], in0=conv_u[:, c, k:k + T], scalar=w,
                                                         in1=conv_c[:, c, :], op0=ALU.mult, op1=ALU.add)
                    if k < k1 - 1 or ready is None:
                        own(ins)
                if ready is not None:
                    ins.then_inc(ready, 1)

            for w, chunks in enumerate(PW1):
                u = U_PW1 + w
                lo_b(u)
                lo_a(u + 1)
                for q in chunks:
                    if q % 2:
                        c = q // 2
                        dve.wait_ge(s_sig, c + 1)
                        V.scalar_tensor_tensor(out=conv_u[:, c, PAD:PAD + T], in0=gub[c % 2][:, 0:T], scalar=col("b_pw1", c),
                                               in1=sg[:, c % 2, :], op0=ALU.add, op1=ALU.mult).then_inc(s_glu, 1)
                        if 1 <= c < 7:
                            dve.wait_ge(s_glu, 2)
                            conv_taps((0, 1), EARLY * (c - 1), EARLY * c)
            dve.wait_ge(s_glu, 8)
            conv_taps((0, 1), 6 * EARLY, TAPS, ready=ev["conv_early"])
            conv_taps(range(2, CONV_DVE), 0, TAPS, ready=ev["conv_ready"])
            dve.wait_ge(ev["mean_done"], 1)
            mean = acc[0][:, 0:T].unsqueeze(1).to_broadcast([P, 4, T])
            for q in range(2):
                h = slice(4 * q, 4 * q + 4)
                V.tensor_tensor(conv_c[:, h, :], conv_c[:, h, :], mean, ALU.subtract).then_inc(ev["centred"], 1)
            dve.wait_ge(ev["conv_std"], 1)
            own(V.reciprocal(conv_r[:, 1, :], conv_r[:, 0, :]))
            dve.wait_ge(ev["centred"], 2)
            for q in range(5):
                if q < 4:
                    h = slice(2 * q, 2 * q + 2)
                    V.tensor_tensor(conv_c[:, h, :], conv_c[:, h, :], conv_r[:, 1, :].unsqueeze(1).to_broadcast([P, 2, T]),
                                    ALU.mult).then_inc(ev["lny_ready"], 1)
                if q >= 1:
                    h = slice(2 * q - 2, 2 * q)
                    dve.wait_ge(ev["conv_hi"], q)
                    V.tensor_tensor(htlo[:, h, :], conv_s[:, h, :], hthi[:, h, :].bitcast(F32), ALU.subtract)\
                        .then_inc(ev["conv_lo"], 1)
            for u in range(U_PW2, U_PW2 + 3):
                step(u, lambda t, u, c, w: m_out[:, t, (u - U_PW2) * PITCH + c:(u - U_PW2) * PITCH + c + w])
            dve.wait_ge(s_eva, plan[U_PW2 + 2][2])
            dve.wait_ge(s_evd, plan[U_PW2 + 2][3])
            dve.wait_ge(s_ldw[1], 16)
            V.tensor_tensor(m_out, m_out, wide[:, 1, :].unsqueeze(1).to_broadcast([P, NT, D]), ALU.add).then_inc(s_wu, 1)
            post_mixer(1, 2)
            norm(6)
            operand("op_f4", [(c, col("ffn_pre", 8 + c)) for c in range(DC)])
            ffn(3)
            post_ffn(2, 3)
            norm(7)
            operand("op_f5", [(c, col("ffn_pre", 16 + c)) for c in range(DC)])
            ffn(4)
            post_ffn(3, 4)
            norm(8)
            V.memset(kz[64:128, 0, :, :], 0.0)
            V.memset(kz[0:64, 1, :, :], 0.0).then_inc(ev["kz_zeroed"], 1)
            lv = rows[:, RO["lambda"]:RO["lambda"] + 256].rearrange("p (a b n) -> p a b n", a=2, b=2)
            own(V.tensor_tensor(lamt[:, :].rearrange("p (a n) -> p a n", a=2), lv[:, :, 0, :], lv[:, :, 1, :], ALU.mult))
            V.tensor_reduce(lam[:, 0:2], lamt[:, :].rearrange("p (a n) -> p a n", a=2), AX, ALU.add).then_inc(ev["lam_sum"], 1)
            operand("op_qkv", [(c, col("mix_pre", 8 + c)) for c in range(DC)])
            for u in range(U_QKV, U_QKV + 8):
                step(u, lambda t, u, c, w: p3[:, t, (u - U_QKV) * PITCH + c:(u - U_QKV) * PITCH + c + w])
            for r in range(4):
                rr = RD["q3"] + r
                dve.wait_ge(s_tr, rr + 1)
                V.tensor_scalar(qT[:, 2 * r:2 * r + 2, :], tp[rr % 2][:, :].rearrange("p (a n) -> p a n", a=2),
                                DH ** -0.5, None, ALU.mult).then_inc(s_tf[rr % 2], 1)
            dve.wait_ge(ev["lam_exp"], 1)
            own(V.tensor_tensor(lam[:, 5:6], lam[:, 3:4], lam[:, 2:3], ALU.subtract))
            own(V.tensor_scalar(lam[:, 4:5], lam[:, 5:6], -LAMBDA_INIT, None, ALU.add))
            V.tensor_scalar(sgain[:, :], col("subln"), 1.0 - LAMBDA_INIT, None, ALU.mult)
            attention("diff")
            dve.wait_ge(ev["sub_sq"], 1)
            V.tensor_reduce(ss[:, 0:16], xflat.rearrange("p (a n) -> p a n", n=P), AX, ALU.add).then_inc(ev["sub_ss"], 1)
            rstd("subln", 16)
            ov = proj[:, 0:2048].rearrange("p (a n) -> p a n", n=P)
            V.tensor_tensor(ov, ov, rs[:, 0:16].unsqueeze(2).to_broadcast([P, 16, P]), ALU.mult).then_inc(ev["sub_ready"], 1)
            operand("op_wo", [(c, sgain[:, 0:1]) for c in range(DC)])
            for u in range(U_WO, U_WO + 3):
                step(u, lambda t, u, c, w: m_out[:, t, (u - U_WO) * PITCH + c:(u - U_WO) * PITCH + c + w])
            dve.wait_ge(s_eva, plan[U_WO + 2][2])
            post_mixer(4, 5)
            norm(9)
            operand("op_f6", [(c, col("ffn_pre", 24 + c)) for c in range(DC)])
            ffn(5)
            post_ffn(5, 6)


def chunks(w, pitch=None):
    k, n = w.shape
    pitch = pitch or n
    out = np.zeros((P, k // P, pitch), w.dtype)
    out[:, :, :n] = w.reshape(k // P, P, n).transpose(1, 0, 2)
    return out


def lay_stream(a):
    s = np.zeros((UNITS, P, UNIT), np.float32)

    def projection(u0, w, width=PITCH):
        for i in range(-(-w.shape[1] // width)):
            part = w[:, i * width:(i + 1) * width]
            pitch = STEPS[u0 + i][1]
            rows_ = part.shape[0] // P
            for k in range(rows_):
                s[u0 + i, :, k * pitch:k * pitch + part.shape[1]] = part[k * P:(k + 1) * P]

    def ffn(u0, gate, up, down):
        for c in range(FC):
            sl = slice(c * P, (c + 1) * P)
            s[u0 + c, :, 0:1024] = chunks(gate[:, sl]).reshape(P, 1024)
            s[u0 + c, :, 1024:2048] = chunks(up[:, sl]).reshape(P, 1024)
            s[u0 + c, :, 2048:] = down[sl]

    projection(U_IN, a["a_w_in"][0])
    w1 = np.concatenate([chunks(a["a_cmp_k_w1"][0]), chunks(a["a_cmp_v_w1"][0])], 1).reshape(P, -1)
    for i in range(3):
        part = w1[:, i * UNIT:(i + 1) * UNIT]
        s[U_CMP + i, :, :part.shape[1]] = part
    projection(U_OUT, a["a_w_out"][0])
    for i in range(2):
        ffn((U_F1, U_F2)[i], a["ffn_w_gate_up"][i][:, :FF], a["ffn_w_gate_up"][i][:, FF:], a["ffn_w_down"][i])
    projection(U_KVA, a["kv_w_a"])
    projection(U_QA, a["b_w_q_a"][0])
    projection(U_KVB, a["kv_w_b"], 1024)
    projection(U_QB, a["b_w_q_b"][0], 768)
    projection(U_MO, a["b_w_out"][0])
    for i, u in enumerate((U_F3, U_F4, U_F5, U_F6)):
        ffn(u, a["ffn_w_gate_2"][i // 2, i % 2], a["ffn_w_up_2"][i // 2, i % 2], a["ffn_w_down_2"][i // 2, i % 2])
    pw1 = a["conv_w_pw1_2"][0]
    for w, qs in enumerate(PW1):
        for m, q in enumerate(qs):
            c0 = (q % 2) * D + (q // 2) * P
            s[U_PW1 + w, :, m * 1024:(m + 1) * 1024] = chunks(pw1[:, c0:c0 + P]).reshape(P, 1024)
    projection(U_PW2, a["conv_w_pw2_2"][0])
    projection(U_QKV, a["attn_w_qkv_2"][0])
    projection(U_WO, a["attn_w_o_2"][0])
    return s


def lay_cols(a):
    def v(x):
        return x.reshape(-1, P).T

    def twice(x):
        return np.concatenate([x, x])[:, None]

    parts = {
        "attn_norm": v(a["a_attn_norm"]), "kv_norm": v(a["kv_norm"]), "b_attn_norm": v(a["b_attn_norm"]),
        "ffn_norm": v(a["ffn_norm"]), "ffn_pre": v(a["ffn_norm_pre_2"]), "mix_pre": v(a["mix_norm_pre_2"]),
        "q_norm": twice(a["a_q_norm"][0]), "kcmp_norm": twice(a["a_kcmp_norm"][0]),
        "kslc_norm": twice(a["a_kslc_norm"][0]), "kwin_norm": twice(a["a_kwin_norm"][0]),
        "b1": np.concatenate([v(a["a_cmp_k_b1"]), v(a["a_cmp_v_b1"])], 1),
        "pos": np.concatenate([v(a["a_cmp_pos_k"]), v(a["a_cmp_pos_v"])], 1),
        "w2": np.concatenate([chunks(a["a_cmp_k_w2"][0]).reshape(P, -1), chunks(a["a_cmp_v_w2"][0]).reshape(P, -1)], 1),
        "kv_c_norm": v(a["kv_c_norm"]), "q_a_norm": v(a["b_q_a_norm"]),
        "knope": a["kv_k_norm"][:NOPE, None], "qnope": a["b_q_norm"][0, :NOPE, None],
        "b_pw1": v(a["conv_b_pw1_2"]), "ln_g": v(a["conv_ln_g_2"]), "ln_b": v(a["conv_ln_b_2"]),
        "b_dw": v(a["conv_b_dw_2"]), "w_dw": v(a["conv_w_dw_2"]), "subln": v(a["attn_subln_g_2"]),
    }
    return np.ascontiguousarray(np.concatenate([parts[n] for n, _ in COLS], 1))


def lay_rows(a):
    return np.concatenate([a["kv_k_norm"][NOPE:], a["b_q_norm"][0, NOPE:], a["attn_lambda_q1_2"][0], a["attn_lambda_k1_2"][0],
                           a["attn_lambda_q2_2"][0], a["attn_lambda_k2_2"][0]])[None]


def lay_wide(a):
    post, mix = a["ffn_norm_post_2"], a["mix_norm_post_2"]
    return np.stack([post[0, 0], a["conv_b_pw2_2"][0], mix[0], post[0, 1], post[1, 0], mix[1], post[1, 1]])


def shape_constants():
    f = np.float32
    tok, key = np.arange(T), np.arange(T)
    allowed = key[None, :] <= tok[:, None]
    dist = (key[None, :] - tok[:, None]).astype(f)

    def tiles(m):
        return m.reshape(NT, P, -1).transpose(1, 0, 2).reshape(P, -1).astype(f)

    j = np.arange(NCMP)
    end, mid = j * CMP_STRIDE + CMP_BLOCK - 1, (j * CMP_STRIDE).astype(f) + f(0.5 * (CMP_BLOCK - 1))
    biasc = np.full((T, H1, G1, NCMP), f(-1e30))
    for h in range(H1):
        b = -f(SLOPES1[h]) * (tok.astype(f)[:, None] - mid[None, :])
        biasc[:, h, h // (H1 // G1)] = np.where(end[None, :] <= tok[:, None], b, f(-1e30))
    inv = f(10000.0) ** (-np.arange(0, ROPE, 2, dtype=f) / f(ROPE))
    ang = tok.astype(f)[:, None] * inv[None, :]
    parts = {
        "ident": np.eye(P, dtype=f), "ones": np.full((P, P), f(1.0 / D)),
        "causal": tiles(np.where(allowed, dist, f(-1e32))), "mask": tiles(np.where(allowed, f(0), f(-1e30))),
        "dist": tiles(np.abs(dist)), "biasc": tiles(biasc.reshape(T, -1)),
        "valid": tiles((tok >= CMP_BLOCK - 1).astype(f)[:, None]), "cos": tiles(np.cos(ang)), "sin": tiles(np.sin(ang)),
    }
    out = np.zeros((P, NCONST), f)
    for name, m in parts.items():
        out[:, KO[name]:KO[name] + m.shape[1]] = m
    return out


def kernel(**inputs):
    import concourse.bacc as bacc
    from concourse.bass_utils import run_bass_kernel_spmd

    a = {k: np.asarray(v) for k, v in inputs.items()}
    arrays = {
        "in_stream": lay_stream(a), "in_cols": lay_cols(a), "in_rows": lay_rows(a), "in_wide": lay_wide(a),
        "in_x": np.ascontiguousarray(a["x"][0]), "in_const": shape_constants(),
    }
    nc = bacc.Bacc("TRN2", target_bir_lowering=False, num_devices=1)
    args = [nc.dram_tensor(k, v.shape, mybir.dt.from_np(v.dtype), kind="ExternalInput").ap() for k, v in arrays.items()]
    args.append(nc.dram_tensor("out_0", (T, D), F32, kind="ExternalOutput").ap())
    build(nc, *args)
    r = run_bass_kernel_spmd(nc, [arrays], core_ids=[0])
    return r.results[0]["out_0"].reshape(1, T, D)
```

```python
from contextlib import ExitStack

import numpy as np

import concourse.bass as bass
from concourse import mybir

ALU = mybir.AluOpType
ACT = mybir.ActivationFunctionType
F32 = mybir.dt.float32
F32R = mybir.dt.float32r
AX = mybir.AxisListType.X

P = 128
T = 256
NT = T // P
D = 1024
DC = D // P
EPS = 1e-6
LN_EPS = 1e-5
SUBLN_EPS = 1e-5

H1, G1, DH = 16, 4, 64
CMP_BLOCK, CMP_STRIDE, CMP_HIDDEN = 32, 16, 256
NCMP = (T - CMP_BLOCK) // CMP_STRIDE + 1
GJ = G1 * NCMP
IN_W = H1 * DH + 6 * G1 * DH + 3 * H1
COL_KC, COL_VC, COL_KS, COL_VS, COL_KW, COL_VW, COL_G = (H1 * DH + i * G1 * DH for i in range(7))
H2, NOPE, ROPE, VD = 8, 128, 64, 128
QL, KVL = 384, 256
QK = NOPE + ROPE
FF = 2816
FC = FF // P
TAPS = 31
PAD = (TAPS - 1) // 2
CONV_DVE = 5
CONV_PE = D // P - CONV_DVE
SHARED = CONV_DVE - 1
SPLIT = 15
EARLY = 2
H3 = 8
LAMBDA_INIT = 0.8 - 0.6 * float(np.exp(-0.3))

UNIT, UA = 3072, 2048
PITCH = UNIT // DC

U_IN, U_CMP, U_OUT, U_F1 = 0, 7, 10, 13
U_KVA, U_QA, U_KVB, U_QB, U_MO, U_F2 = 35, 36, 37, 39, 41, 44
U_F3, U_PW1, U_PW2, U_F4, U_F5 = 66, 88, 94, 97, 119
U_QKV, U_WO, U_F6, U_END = 141, 149, 152, 174
UNITS = U_END + 2

COLS = [("attn_norm", 8), ("kv_norm", 8), ("b_attn_norm", 8), ("ffn_norm", 16), ("ffn_pre", 32),
        ("mix_pre", 16), ("q_norm", 1), ("kcmp_norm", 1), ("kslc_norm", 1), ("kwin_norm", 1),
        ("b1", 4), ("pos", 32), ("w2", 256), ("kv_c_norm", 2), ("q_a_norm", 3), ("knope", 1),
        ("qnope", 1), ("b_pw1", 16), ("ln_g", 8), ("ln_b", 8), ("b_dw", 8), ("w_dw", TAPS * 8),
        ("subln", 1)]
CO, _at = {}, 0
for _n, _w in COLS:
    CO[_n] = _at
    _at += _w
NCOLS = _at
RO = {"kpe": 0, "qpe": 64, "lambda": 128}
NROWS = 128 + 4 * 64
KO, _at = {}, 0
for _n, _w in (("ident", 128), ("ones", 128), ("causal", 512), ("mask", 512), ("dist", 512),
               ("valid", 2), ("cos", 64), ("sin", 64), ("biasc", 2 * H1 * GJ)):
    KO[_n] = _at
    _at += _w
NCONST = _at
NORM = 62
NKEEP = KO["biasc"]
SLOPES1 = [float(np.float32(2.0) ** np.float32(-8.0 * (h + 1) / H1)) for h in range(H1)]
SLOPES3 = [float(np.float32(2.0) ** np.float32(-8.0 * (h + 1) / H3)) for h in range(H3)]

STEPS = {}
for _u in range(7):
    STEPS[U_IN + _u] = (8, PITCH, [(0, min(PITCH, IN_W - _u * PITCH))])
for _b in (U_OUT, U_MO, U_PW2, U_WO):
    for _u in range(3):
        STEPS[_b + _u] = (8, PITCH, [(0, min(PITCH, D - _u * PITCH))])
STEPS[U_KVA] = (8, PITCH, [(0, KVL + ROPE)])
STEPS[U_QA] = (8, PITCH, [(0, QL)])
for _u in range(2):
    STEPS[U_KVB + _u] = (2, 2048, [(0, 512), (512, 512)])
    STEPS[U_QB + _u] = (3, 1024, [(0, 384), (384, 384)])
for _u in range(8):
    STEPS[U_QKV + _u] = (8, PITCH, [(0, PITCH)])


UPDATES = 10
ADDED = (U_OUT, U_MO)


def projection_plan():
    plan, last, flip, eva, evd = {}, {}, 0, 0, 0
    for u in sorted(STEPS):
        pieces = STEPS[u][2]
        if len(pieces) == 1:
            banks = [[2 * (flip % 2) + t] for t in range(NT)]
            flip += 1
        else:
            banks = [[2 * t, 2 * t + 1] for t in range(NT)]
        before = max([last.get(b, -1) for row in banks for b in row])
        added = any(b <= u < b + 3 for b in ADDED)
        eva += not added
        evd += not (added and any(u == b + 2 for b in ADDED))
        plan[u] = (banks, before, eva, evd)
        for row in banks:
            for b in row:
                last[b] = u
    return plan


ROUNDS = [("op_attn", 4), ("kcvc", 2), ("hx", 1), ("q1", 4), ("kcmp", 1), ("k1", 4), ("pc0", 4), ("pc1", 4), ("nsa", 2 * H1),
          ("op_f1", 4), ("r_f1", 1), ("op_kv", 4), ("op_bq", 4), ("op_ckv", 1), ("op_qa", 2), ("k2", 4),
          ("kpe", 2), ("q2", 4), ("qpe", 2), ("mla", H2), ("op_f2", 4), ("r_f2", 1), ("op_f3", 4), ("r_f3", 1), ("op_conv", 4), ("r_conv", 1), ("op_f4", 4), ("r_f4", 1),
          ("op_f5", 4), ("r_f5", 1), ("op_qkv", 4), ("q3", 4), ("k3", 4), ("diff", 2 * H3), ("op_wo", 4), ("op_f6", 4), ("r_f6", 1)]
RD, _at = {}, 0
for _n, _w in ROUNDS:
    RD[_n] = _at
    _at += _w
RSTD = {n: i for i, n in enumerate(
    ["n0", "qk1", "kcmp", "n1", "n2", "ckv", "qan", "k2n", "q2n", "n3", "n4", "post0", "n5", "post1", "n6", "post2",
     "n7", "post3", "n8", "subln", "post4", "n9", "post5"])}
ITEM0 = {"nsa": 0, "mla": 2 * H1, "diff": 2 * H1 + H2}
NITEM = {"nsa": 2 * H1, "mla": H2, "diff": 2 * H3}
LAG = 3
QK3 = {3: ("q3", 0), 4: ("q3", 2), 6: ("k3", 0), 7: ("k3", 2)}
PW1 = [[0, 1, 2], [3, 4, 5], [6, 7, 8], [9, 10, 11], [12, 13], [14, 15]]


OPN, _at = {}, 0
for _n, _w in ROUNDS:
    if _n.startswith("op_"):
        OPN[_n] = _at
        _at += _w
FUNITS = [U_F1, U_F2, U_F3, U_F4, U_F5, U_F6]


def item_blocks(kind, i):
    if kind == "nsa":
        return [(b, k) for b in range(2) for k in range(i % 2 + 1)]
    if kind == "mla":
        return [(0, 0), (1, 0), (1, 1)]
    return [(0, 0), (0, 1)]


def build(nc, stream, cols_d, rows_d, wide_d, x_d, const_d, out_d):
    ctx = ExitStack()
    with ctx:
        def sb(name, shape, dt=F32):
            return ctx.enter_context(nc.sbuf_tensor(name, shape, dt))

        def sem(name):
            return ctx.enter_context(nc.semaphore(name))

        raw = sb("raw", [P, 2, UNIT])
        whi = sb("whi", [P, 2, UNIT], F32R)
        wlo = sb("wlo", [P, 2, UNIT], F32R)
        x = sb("x", [P, NT, D])
        xn = sb("xn", [P, NT, D])
        hthi = sb("hthi", [P, DC, T], F32R)
        htlo = sb("htlo", [P, DC, T], F32R)
        proj = sb("proj", [P, 7168])
        tr = sb("tr", [P, 8192])
        att = sb("att", [P, 3072])
        hidhi = sb("hidhi", [P, 2, T], F32R)
        hidlo = sb("hidlo", [P, 2, T], F32R)
        wide = sb("wide", [P, 2, D])
        cols = sb("cols", [P, NCOLS])
        rows = sb("rows", [P, NROWS])
        const = sb("const", [P, NKEEP])
        gates = sb("gates", [P, NT, 48])
        ss = sb("ss", [P, 64])
        std = sb("std", [P, 64])
        rs = sb("rs", [P, 64])
        nmax = sb("nmax", [P, 2, 16])
        lsum = sb("lsum", [P, 2, 16])
        pw = sb("pw", [P, 2, 16])
        vcmp = sb("vcmp", [GJ, DH])
        kcd = sb("kcd", [GJ, 2, DH])
        kcz = sb("kcz", [P, 2, GJ])
        cst = sb("cst", [P, 4, H1])
        lam = sb("lam", [P, 8])
        lamt = sb("lamt", [P, 128])
        sgain = sb("sgain", [P, 1])
        rb = sb("rb", [P, T])

        bank = [ctx.enter_context(nc.psum_tensor(f"bank{i}", [P, 512], F32)) for i in range(8)]
        acc, tp, gub = bank[0:4], bank[4:6], bank[6:8]

        ident = const[:, KO["ident"]:KO["ident"] + P]
        ones = const[:, KO["ones"]:KO["ones"] + P]

        def col(name, i=0):
            return cols[:, CO[name] + i:CO[name] + i + 1]

        biasc = wide[:, :, :].rearrange("p a n -> p (a n)")[:, 0:NCONST - NKEEP]
        p1 = proj[:, 0:NT * IN_W].rearrange("p (t n) -> p t n", t=NT)
        kv = proj[:, 0:4096].rearrange("p (t h n) -> p t h n", t=NT, h=H2)
        q2 = proj[:, 4096:7168].rearrange("p (t h n) -> p t h n", t=NT, h=H2)
        p3 = proj[:, 0:6144].rearrange("p (t n) -> p t n", t=NT)
        m_out = proj[:, 0:NT * D].rearrange("p (t n) -> p t n", t=NT)
        conv_u = proj[:, 0:8 * (T + 2 * PAD)].rearrange("p (c n) -> p c n", c=8)
        conv_c = proj[:, 2304:4352].rearrange("p (c n) -> p c n", c=8)
        conv_s = proj[:, 4352:6400].rearrange("p (c n) -> p c n", c=8)
        conv_r = proj[:, 6400:6912].rearrange("p (c n) -> p c n", c=2)
        diag = [v.rearrange("p (k n) -> p k n", n=P) for v in (tr[:, 2048:8192], att[:, :], proj[:, 3584:6400])]
        diag_runs, left = [], [v.shape[1] for v in diag]
        for c in range(CONV_DVE, 8):
            k = 0
            while k < TAPS:
                part = [room > 0 for room in left].index(True)
                cnt = min(TAPS - k, left[part])
                diag_runs.append((c, k, cnt, part, diag[part].shape[1] - left[part]))
                left[part] -= cnt
                k += cnt
        diag_shared = xn[:, :, :].rearrange("p t n -> p (t n)").rearrange("p (k n) -> p k n", n=P)
        diff_o = proj[:, 0:NT * D].rearrange("p (t n) -> p t n", t=NT)

        qT = tr[:, 0:2048].rearrange("p (c n) -> p c n", c=8)
        kz = tr[:, 2048:6144].rearrange("p (m g n) -> p m g n", m=2, g=8)
        sq1 = att[:, 0:NT * 24 * 64].rearrange("p (t n) -> p t n", t=NT)
        blk = tr[:, 6144:6144 + 1920]
        kd = tr[:, 6144:8192].rearrange("p (t g d n) -> p t g d n", t=NT, g=8, d=2)
        pct = [xn[0:GJ, :, :].rearrange("p t n -> p (t n)").rearrange("p (h n) -> p h n", h=H1),
               tr[0:GJ, 6144:8192].rearrange("p (h n) -> p h n", h=H1)]
        kc2 = xn[:, :, :].rearrange("p t n -> p (t n)").rearrange("p (v a b n) -> p v a b n", v=2, a=2, b=2)
        hx = att[0:GJ, 1024:1536]
        sc_cmp = [att[:, 0:H1 * GJ], proj[:, NT * IN_W:NT * IN_W + H1 * GJ]]
        pr_cmp = [att[:, 1024:1024 + H1 * GJ], att[:, 2048:2048 + H1 * GJ]]
        xflat = xn[:, :, :].rearrange("p t n -> p (t n)")
        blkhi = hthi[:, :, :].rearrange("p c n -> p (c n)")[:, 0:1920]
        blklo = htlo[:, :, :].rearrange("p c n -> p (c n)")[:, 0:1920]
        kT2 = tr[:, 2048:4096].rearrange("p (c n) -> p c n", c=8)
        qpe = att[:, 0:1024].rearrange("p (t h n) -> p t h n", t=NT, h=H2)
        qpT = tr[:, 4096:5120].rearrange("p (c n) -> p c n", c=4)
        kpT = tr[:, 5120:6144].rearrange("p (c n) -> p c n", c=4)
        kva = att[:, 0:640].rearrange("p (t n) -> p t n", t=NT)
        qa = att[:, 640:1408].rearrange("p (t n) -> p t n", t=NT)
        kpe = att[:, 1408:2432].rearrange("p (t h n) -> p t h n", t=NT, h=H2)
        kr = att[:, 2432:2560].rearrange("p (t n) -> p t n", t=NT)
        rope_q = att[:, 2560:2816].rearrange("p (q t n) -> p q t n", q=4, t=NT)
        rope_p = att[:, 2816:3072].rearrange("p (q t n) -> p q t n", q=4, t=NT)
        sg = tr[:, 0:512].rearrange("p (c n) -> p c n", c=2)
        hidf = tr[:, 512:1024].rearrange("p (c n) -> p c n", c=2)
        gu = tr[:, 1024:2048].rearrange("p (c n) -> p c n", c=2)
        gate_up_bank = [b[:, :].rearrange("p (h n) -> p h n", h=2) for b in gub]

        s_sc = att[:, 0:1024].rearrange("p (i b n) -> p i b n", i=2, b=2)
        s_pr = att[:, 1024:2048].rearrange("p (i b n) -> p i b n", i=2, b=2)
        s_pt = att[:, 2048:3072].rearrange("p (i n) -> p i n", i=2)

        s_ldx, s_ldc, s_ldk, s_ldr = sem("x_loaded"), sem("cols_loaded"), sem("const_loaded"), sem("rows_loaded")
        s_ldi, s_ldbc = sem("identity_loaded"), sem("compressed_bias_loaded")
        s_lda = [sem("piece_a_loaded_0"), sem("piece_a_loaded_1")]
        s_ldb = [sem("piece_b_loaded_0"), sem("piece_b_loaded_1")]
        s_ldw = [sem("wide_loaded_0"), sem("wide_loaded_1")]
        s_hia, s_hib = sem("hi_a_done"), sem("hi_b_done")
        s_loa, s_lob = sem("lo_a_done"), sem("lo_b_done")
        s_usea, s_useb = sem("piece_a_used"), sem("piece_b_used")
        s_act, s_dve = sem("act_own"), sem("dve_own")
        s_x = sem("x_updated")
        s_std, s_rs = sem("std_done"), sem("rstd_done")
        s_gu, s_cgu = sem("gate_up_scaled"), sem("pw1_scaled")
        s_fin = sem("ffn_bank_finished")
        s_tr = sem("transposed")
        s_tf = [sem("transpose_bank_taken_0"), sem("transpose_bank_taken_1")]
        s_thi = sem("operand_hi_done")
        s_eva, s_evd = sem("step_taken_by_act"), sem("step_taken_by_dve")
        s_silu, s_hf, s_hh, s_hid = sem("silu_done"), sem("hidden_full"), sem("hidden_hi"), sem("hidden_done")
        s_wu = sem("wide_used")
        s_sco, s_bia, s_exp, s_prob = sem("scores_done"), sem("scores_biased"), sem("exp_done"), sem("probs_done")
        s_pv = sem("values_summed")
        s_oh, s_ol, s_od = sem("output_hi_done"), sem("output_lo_done"), sem("output_taken")
        s_pss, s_phs = sem("post_squares_summed"), sem("post_halves_added")
        s_pw, s_sig, s_glu = sem("pw1_gate_done"), sem("sigmoid_done"), sem("glu_done")
        s_out = sem("stored")
        ev = {name: sem(name) for name in (
            "blk_ready", "sq1_ready", "ss1_ready", "qn_ready", "kd_ready",
            "hx_ready", "gelu_in", "gelu_sig", "gelu_ready", "w2_done", "kcd_ready",
            "gates_ready", "cs0", "cs1", "cm0", "cm1", "ce0", "ce1", "cp0", "cp1", "kz_zeroed",
            "ckv_ready", "qa_ready", "k2_sq", "k2_ss", "q2_sq", "q2_ss", "k2n_ready", "q2n_ready", "kpe_ready",
            "diagonals_ready", "conv_summed", "conv_early", "sum_ready",
            "qpe_ready", "conv_ready", "mean_done", "centred", "sq_ready", "var_done",
            "conv_std", "lny_ready", "conv_hi", "conv_lo",
            "lam_sum", "lam_exp", "sub_ready")}

        plan = projection_plan()
        block = ctx.enter_context(nc.Block())

        def pw1_ready(eng, u, m, c):
            if m == 0:
                eng.wait_ge(s_pw, sum(1 for w in PW1 for mm, q in enumerate(w) if mm == 0 and q % 2 and q <= 2 * c + 1))
            elif m == 1:
                eng.wait_ge(s_usea, u + 1)
            else:
                eng.wait_ge(s_useb, u + 1)

        @block.sync
        def _(sp):
            sp.dma_start(const[:, 0:P], const_d[:, 0:P]).then_inc(s_ldi, 16)
            sp.dma_start(x[:, :, :], x_d.rearrange("(t p) n -> p t n", p=P)).then_inc(s_ldx, 16)
            sp.dma_start(raw[:, 0, 0:UA], stream[0, :, 0:UA]).then_inc(s_lda[0], 16)
            sp.dma_start(cols[:, :], cols_d).then_inc(s_ldc, 16)
            sp.dma_start(raw[:, 0, UA:UNIT], stream[0, :, UA:UNIT]).then_inc(s_ldb[0], 16)
            sp.dma_start(raw[:, 1, 0:UA], stream[1, :, 0:UA]).then_inc(s_lda[1], 16)
            sp.dma_start(raw[:, 1, UA:UNIT], stream[1, :, UA:UNIT]).then_inc(s_ldb[1], 16)
            sp.dma_start(const[:, P:], const_d[:, P:NKEEP]).then_inc(s_ldk, 16)
            sp.dma_start(rows[:, :], rows_d[0].partition_broadcast(P)).then_inc(s_ldr, 16)
            sp.dma_start(biasc, const_d[:, NKEEP:NCONST]).then_inc(s_ldbc, 16)
            with sp.Fori(1, UNITS // 2) as i:
                for j in range(2):
                    sp.wait_ge(s_loa, i * 2 + (j - 1))
                    sp.dma_start(raw[:, j, 0:UA], stream[i * 2 + j, :, 0:UA]).then_inc(s_lda[j], 16)
                    sp.wait_ge(s_lob, i * 2 + (j - 1))
                    sp.dma_start(raw[:, j, UA:UNIT], stream[i * 2 + j, :, UA:UNIT]).then_inc(s_ldb[j], 16)
            for j in range(2):
                sp.wait_ge(s_lda[j], 16 * (UNITS // 2))
                sp.wait_ge(s_ldb[j], 16 * (UNITS // 2))
            for j in range(2):
                sp.wait_ge(s_x, 4 * UPDATES - 2 + 2 * j)
                sl = slice(j * 512, (j + 1) * 512)
                sp.dma_start(out_d.rearrange("(t p) n -> p t n", p=P)[:, :, sl], x[:, :, sl]).then_inc(s_out, 16)
            sp.wait_ge(s_out, 32)

        @block.gpsimd
        def _(pool):
            def zero_halves():
                nc.gpsimd.memset(kz[64:128, 0, :, :], 0.0)
                return nc.gpsimd.memset(kz[0:64, 1, :, :], 0.0)

            nc.gpsimd.memset(kcz[64:128, 0, :], 0.0)
            nc.gpsimd.memset(kcz[0:64, 1, :], 0.0)
            zero_halves().then_inc(ev["kz_zeroed"], 1)
            for n in range(7):
                if n == 0:
                    pool.wait_ge(ev["cm1"], 1)
                if n == 2:
                    pool.wait_ge(s_ldi, 16)
                    pool.wait_ge(s_ldc, 16)
                    pool.wait_ge(s_ol, 16)
                    pool.wait_ge(s_x, 12)
                    dw = cols[:, CO["w_dw"]:CO["w_dw"] + 8 * TAPS].rearrange("p (k c) -> p c k", c=8)
                    for c, k, cnt, part, at in diag_runs:
                        ins = nc.gpsimd.tensor_tensor(
                            diag[part][:, at:at + cnt, :], ident.unsqueeze(1).to_broadcast([P, cnt, P]),
                            dw[:, c, k:k + cnt].unsqueeze(2).to_broadcast([P, cnt, P]), ALU.mult)
                    ins.then_inc(ev["diagonals_ready"], 1)
                    pool.wait_ge(s_rs, RSTD["n5"] + 1)
                    cnt = TAPS - SPLIT
                    nc.gpsimd.tensor_tensor(
                        diag_shared[:, 0:cnt, :], ident.unsqueeze(1).to_broadcast([P, cnt, P]),
                        dw[:, SHARED, SPLIT:TAPS].unsqueeze(2).to_broadcast([P, cnt, P]), ALU.mult)\
                        .then_inc(ev["diagonals_ready"], 1)
                if n >= 2:
                    pool.wait_ge(s_wu, n - 1)
                if n == 4:
                    zero_halves().then_inc(ev["kz_zeroed"], 1)
                pool.dma_start(wide[:, n % 2, :], wide_d[n].partition_broadcast(P)).then_inc(s_ldw[n % 2], 16)

        @block.scalar
        def _(act):
            n = dict(own=0, thi=0)

            def own(ins):
                n["own"] += 1
                ins.then_inc(s_act, 1)
                act.wait_ge(s_act, n["own"])

            def hi_a(u, i=0):
                s = u % 2
                act.wait_ge(s_lda[s], i * 16 + 16 * (u // 2 + 1))
                if u >= 2:
                    act.wait_ge(s_usea, i * 2 + (u - 1))
                nc.scalar.activation(whi[:, s, 0:UA], raw[:, s, 0:UA], ACT.Copy).then_inc(s_hia, 1)

            def hi_b(u, i=0):
                s = u % 2
                act.wait_ge(s_ldb[s], i * 16 + 16 * (u // 2 + 1))
                if u >= 2:
                    act.wait_ge(s_useb, i * 2 + (u - 1))
                nc.scalar.activation(whi[:, s, UA:UNIT], raw[:, s, UA:UNIT], ACT.Copy).then_inc(s_hib, 1)

            def step(u, dst=None, m=None, first=False):
                hi_b(u)
                hi_a(u + 1)
                if first:
                    norm(m)
                if dst is not None:
                    banks = plan[u][0]
                    act.wait_ge(s_useb, u + 1)
                    if m is not None:
                        act.wait_ge(s_rs, RSTD[f"n{m}"] + 1)
                    for j, (c, w) in enumerate(STEPS[u][2]):
                        ins = nc.scalar.activation(dst(0, u, c, w), acc[banks[0][j]][:, 0:w], ACT.Copy,
                                                   scale=1.0 if m is None else rs[:, NORM:NORM + 1])
                    ins.then_inc(s_eva, 1)

            def sqrt_table():
                nc.scalar.activation(lam[:, 6:7], ident[:, 0:1], ACT.Sqrt)

            def sqrt(name, cnt, dim, eps, at=0):
                if RSTD[name] >= 1:
                    act.wait_ge(s_rs, RSTD[name])
                r = vcmp.shape[0] if name == "kcmp" else P
                nc.scalar.activation(std[0:r, at:at + cnt], ss[0:r, at:at + cnt], ACT.Sqrt,
                                     scale=1.0 / dim, bias=eps).then_inc(s_std, 1)

            def norm(m):
                for t in range(NT):
                    if m == 0:
                        act.wait_ge(s_ldx, 16)
                    else:
                        act.wait_ge(s_x, 4 * m + t - 1)
                    ins = nc.scalar.activation(xn[:, t, :], x[:, t, :], ACT.Square, accum_out=ss[:, NORM + t:NORM + t + 1])
                own(ins)
                sqrt(f"n{m}", 2, D, EPS, NORM)

            def operand(name, chunks, free):
                if free:
                    act.wait_ge(s_useb, free)
                for a in range(0, len(chunks), 2):
                    r = RD[name] + a // 2
                    act.wait_ge(s_tr, r + 1)
                    for j, (dst, gain) in enumerate(chunks[a:a + 2]):
                        ins = nc.scalar.activation(hthi[:, dst, :], tp[r % 2][:, j * T:(j + 1) * T], ACT.Copy,
                                                   scale=1.0 if gain is None else gain)
                    ins.then_inc(s_thi, 1)

            def ffn(fi, m):
                f = FUNITS[fi]

                def chunk(j, i=0, first=False):
                    hi_a(f + j + 1, i)
                    if first:
                        norm(m)
                    act.wait_ge(s_gu, i * 2 + (FC * fi + j + 1))
                    nc.scalar.activation(sg[:, j, :], gu[:, j, 0:T], ACT.Silu).then_inc(s_silu, 1)
                    hi_b(f + j, i)

                chunk(0, first=True)
                chunk(1)
                with act.Fori(1, FC // 2) as i:
                    chunk(0, i)
                    chunk(1, i)

            def post_ffn(k, f):
                sqrt_table()
                for n_, q in enumerate((0, 2, 1, 3)):
                    if n_ < 3:
                        act.wait_ge(s_fin, 3 * FUNITS.index(f) + n_ + 1)
                    else:
                        act.wait_ge(s_useb, f + FC)
                    ins = nc.scalar.activation(xn[:, q // 2, (q % 2) * 512:(q % 2 + 1) * 512], acc[q][:, :],
                                               ACT.Square, accum_out=ss[:, 8 + q:9 + q])
                ins.then_inc(s_pss, 1)
                act.wait_ge(s_phs, k + 1)
                sqrt(f"post{k}", 2, D, EPS)

            def mixer_out(first):
                for w in range(3):
                    u = first + w
                    hi_b(u)
                    hi_a(u + 1)
                    if w == 2:
                        sqrt_table()
                    act.wait_ge(s_evd, plan[u][3])
                    sl = slice(w * PITCH, w * PITCH + STEPS[u][2][0][1])
                    for t in range(NT):
                        at = 8 + 3 * t + w
                        ins = nc.scalar.activation(xn[:, t, sl], m_out[:, t, sl], ACT.Square, accum_out=ss[:, at:at + 1])
                    ins.then_inc(s_eva, 1)

            def post_mixer(k):
                act.wait_ge(s_phs, k + 1)
                sqrt(f"post{k}", 2, D, EPS)

            def attention(kind):
                base, cnt = ITEM0[kind], NITEM[kind]

                def post(i):
                    g = base + i
                    if kind == "nsa" and i % 4 == 3:
                        act.wait_ge(s_pv, g + 1)
                        nc.scalar.activation(hthi[:, i // 4, :], gub[(i // 4) % 2][:, 0:T], ACT.Copy).then_inc(s_oh, 1)
                    if kind == "mla":
                        act.wait_ge(s_pv, g + 1)
                        nc.scalar.activation(hthi[:, i, :], gub[i % 2][:, 0:T], ACT.Copy).then_inc(s_oh, 1)
                    if kind == "diff":
                        act.wait_ge(s_pv, g + 1)
                        nc.scalar.activation(diff_o[:, i % 2, (i // 2) * P:(i // 2 + 1) * P], gub[g % 2][:, 0:P], ACT.Copy)
                        at = (i % 2) * H3 + i // 2
                        nc.scalar.activation(xflat[:, i * P:(i + 1) * P], gub[g % 2][:, 0:P], ACT.Square, accum_out=ss[:, at:at + 1])\
                            .then_inc(s_od, 1)
                        if i == cnt - 2:
                            sqrt_table()

                for i in range(cnt + LAG):
                    if i >= LAG:
                        post(i - LAG)
                    g = base + i
                    if i < cnt:
                        act.wait_ge(s_bia, g + 1)
                        act.wait_ge(s_tr, RD[kind] + max(i - 1, 0))
                        nk = P * (i % 2 + 1) if kind == "nsa" else T
                        for b in range(2):
                            ins = nc.scalar.activation(s_pr[:, g % 2, b, 0:nk], s_sc[:, g % 2, b, 0:nk], ACT.Exp,
                                                       bias=nmax[:, g % 2, b:b + 1],
                                                       accum_out=lsum[:, g % 2, b:b + 1])
                        ins.then_inc(s_exp, 1)
                    if 1 <= i <= cnt:
                        g, r = base + i - 1, RD[kind] + i - 1
                        w = P * len(item_blocks(kind, i - 1))
                        act.wait_ge(s_tr, r + 1)
                        if g >= 2:
                            act.wait_ge(s_pv, g - 1)
                        nc.scalar.activation(s_pt[:, g % 2, 0:w], tp[r % 2][:, 0:w], ACT.Copy).then_inc(s_tf[r % 2], 1)

            hi_a(0)
            act.wait_ge(s_ldc, 16)
            act.wait_ge(s_ldi, 16)
            operand("op_attn", [(c, col("attn_norm", c)) for c in range(DC)], 0)
            for u in range(U_IN, U_IN + 7):
                step(u, lambda t, u, c, w: p1[:, t, (u - U_IN) * PITCH + c:(u - U_IN) * PITCH + c + w], 0, u == U_IN)
                if u == U_IN + 4:
                    r = RD["kcvc"] + 1
                    act.wait_ge(s_tr, r + 1)
                    for b in range(2):
                        src = tp[r % 2][64 * b:64 * b + 64, :].rearrange("p (a n) -> p a n", a=2)
                        nc.scalar.activation(kc2[0:64, 1, :, b, :], src, ACT.Copy)
                        ins = nc.scalar.activation(kc2[64:128, 1, :, b, 0:T - 1], src[:, :, 1:T], ACT.Copy)
                    ins.then_inc(s_tf[r % 2], 1)
            hi_b(U_CMP)
            hi_a(U_CMP + 1)
            act.wait_ge(s_evd, plan[U_IN + 6][3])
            act.wait_ge(s_eva, plan[U_IN + 6][2])
            for t in range(NT):
                nc.scalar.activation(sq1[:, t, 0:1024], p1[:, t, 0:1024], ACT.Square)
                ins = nc.scalar.activation(
                    sq1[:, t, 1024:1536].rearrange("p (a n) -> p a n", a=2),
                    p1[:, t, COL_KS:COL_KS + 1024].rearrange("p (a n) -> p a n", a=2)[:, :, 0:256], ACT.Square)
            ins.then_inc(ev["sq1_ready"], 1)
            hi_b(U_CMP + 1)
            hi_a(U_CMP + 2)
            hi_b(U_CMP + 2)
            for v in range(2):
                act.wait_ge(s_usea, U_CMP + 2 + v)
                act.wait_ge(ev["ss1_ready"], 1)
                ins = nc.scalar.activation(hx[:, v * T:(v + 1) * T], acc[2 + v][0:GJ, 0:CMP_HIDDEN], ACT.Copy)
            ins.then_inc(ev["hx_ready"], 1)
            sqrt("qk1", 48, DH, EPS)
            r = RD["hx"]
            act.wait_ge(s_tr, r + 1)
            for q in range(4):
                ins = nc.scalar.activation(att[:, q * GJ:(q + 1) * GJ], tp[r % 2][:, q * GJ:(q + 1) * GJ], ACT.Identity,
                                           bias=col("b1", q))
            ins.then_inc(s_tf[r % 2], 1)
            act.wait_ge(ev["gelu_in"], 1)
            nc.scalar.activation(att[:, 480:720], att[:, 240:480], ACT.Sigmoid, scale=2 * 0.7978845608028654)\
                .then_inc(ev["gelu_sig"], 1)
            nc.scalar.activation(gates[:, :, :], p1[:, :, COL_G:COL_G + 48], ACT.Sigmoid).then_inc(ev["gates_ready"], 1)
            sqrt_table()
            hi_a(U_CMP + 3)
            act.wait_ge(ev["w2_done"], 1)
            own(nc.scalar.activation(att[0:GJ, 960:1024], gub[0][0:GJ, 0:DH], ACT.Square, accum_out=ss[0:GJ, 0:1]))
            sqrt("kcmp", 1, DH, EPS)
            r = RD["kcmp"]
            act.wait_ge(s_tr, r + 1)
            for m in range(2):
                ins = nc.scalar.activation(kcz[m * 64:(m + 1) * 64, m, :], tp[r % 2][m * 64:(m + 1) * 64, 0:GJ], ACT.Copy,
                                           scale=cols[m * 64:(m + 1) * 64, CO["kcmp_norm"]:CO["kcmp_norm"] + 1])
            ins.then_inc(s_tf[r % 2], 1)
            def k1_copy(r):
                rr = RD["k1"] + r
                act.wait_ge(s_tr, rr + 1)
                if r == 0:
                    act.wait_ge(ev["kz_zeroed"], 1)
                g0 = 2 * r
                name = "kslc_norm" if r < 2 else "kwin_norm"
                for m in range(2):
                    ins = nc.scalar.activation(
                        kz[m * 64:(m + 1) * 64, m, g0:g0 + 2, :],
                        tp[rr % 2][m * 64:(m + 1) * 64, :].rearrange("p (a n) -> p a n", a=2), ACT.Copy,
                        scale=cols[m * 64:(m + 1) * 64, CO[name]:CO[name] + 1])
                ins.then_inc(s_tf[rr % 2], 1)

            k1_copy(0)
            for t in range(NT):
                act.wait_ge(ev[f"cm{t}"], 1)
                nc.scalar.activation(pr_cmp[t], sc_cmp[t], ACT.Exp).then_inc(ev[f"ce{t}"], 1)
                k1_copy(t + 1)
            k1_copy(3)
            for t in range(NT):
                for q in range(4):
                    r = RD[f"pc{t}"] + q
                    act.wait_ge(s_tr, r + 1)
                    nc.scalar.activation(pct[t][:, 4 * q:4 * q + 4, :],
                                         tp[r % 2][0:GJ, :].rearrange("p (h n) -> p h n", h=4), ACT.Copy)\
                        .then_inc(s_tf[r % 2], 1)
            attention("nsa")
            for u in range(U_OUT, U_OUT + 3):
                step(u)
            operand("op_f1", [(c, col("ffn_norm", c)) for c in range(DC)], U_F1)
            ffn(0, 1)
            operand("op_kv", [(c, col("kv_norm", c)) for c in range(DC)], U_KVA)
            step(U_KVA, lambda t, u, c, w: kva[:, t, c:c + w], 2, True)
            operand("op_bq", [(c, col("b_attn_norm", c)) for c in range(DC)], U_KVA + 1)
            act.wait_ge(s_evd, plan[U_KVA][3])
            act.wait_ge(s_eva, plan[U_KVA][2])
            for t in range(NT):
                nc.scalar.activation(xn[:, t, 0:KVL], kva[:, t, 0:KVL], ACT.Square, accum_out=ss[:, t:t + 1])
                ins = nc.scalar.activation(xn[:, t, KVL:KVL + ROPE], kva[:, t, KVL:KVL + ROPE], ACT.Square,
                                           accum_out=ss[:, 40 + t:41 + t])
            own(ins)
            sqrt("ckv", 2, KVL, EPS)
            step(U_QA, lambda t, u, c, w: qa[:, t, c:c + w], 2)
            act.wait_ge(s_evd, plan[U_QA][3])
            act.wait_ge(s_eva, plan[U_QA][2])
            for t in range(NT):
                ins = nc.scalar.activation(xn[:, t, 0:QL], qa[:, t, :], ACT.Square, accum_out=ss[:, t:t + 1])
            own(ins)
            sqrt("qan", 2, QL, EPS)
            operand("op_ckv", [(c, col("kv_c_norm", c)) for c in range(2)], U_QA + 1)
            operand("op_qa", [(2 + c, col("q_a_norm", c)) for c in range(3)], U_QA + 1)
            for u in (U_KVB, U_KVB + 1):
                step(u, lambda t, u, c, w: kv[:, t, 4 * (u - U_KVB) + c // 256:4 * (u - U_KVB) + (c + w) // 256, :])
            act.wait_ge(s_evd, plan[U_KVB + 1][3])
            act.wait_ge(s_eva, plan[U_KVB + 1][2])
            for t in range(NT):
                ins = nc.scalar.activation(tr[:, 3072 + t * 1024:3072 + (t + 1) * 1024].rearrange("p (h n) -> p h n", h=H2),
                                           kv[:, t, :, 0:NOPE], ACT.Square)
            ins.then_inc(ev["k2_sq"], 1)

            def q2_out(t, u, c, w):
                return q2[:, t, 4 * (u - U_QB) + c // QK:4 * (u - U_QB) + (c + w) // QK, :]

            step(U_QB, q2_out)
            act.wait_ge(ev["k2_ss"], 1)
            sqrt("k2n", 16, QK, EPS)
            step(U_QB + 1, q2_out)
            act.wait_ge(s_evd, plan[U_QB + 1][3])
            act.wait_ge(s_eva, plan[U_QB + 1][2])
            for t in range(NT):
                nc.scalar.activation(tr[:, t * 1536:(t + 1) * 1536].rearrange("p (h n) -> p h n", h=H2),
                                     q2[:, t, :, :], ACT.Square).then_inc(ev["q2_sq"], 1)
            act.wait_ge(ev["q2_ss"], 1)
            sqrt("q2n", 16, QK, EPS, 16)
            for r in range(4):
                rr = RD["k2"] + r
                act.wait_ge(s_tr, rr + 1)
                nc.scalar.activation(kT2[:, 2 * r:2 * r + 2, :], tp[rr % 2][:, :].rearrange("p (a n) -> p a n", a=2),
                                     ACT.Copy, scale=col("knope")).then_inc(s_tf[rr % 2], 1)
            for r in range(2):
                rr = RD["kpe"] + r
                act.wait_ge(s_tr, rr + 1)
                nc.scalar.activation(kpT[:, 2 * r:2 * r + 2, :], tp[rr % 2][:, :].rearrange("p (a n) -> p a n", a=2),
                                     ACT.Copy).then_inc(s_tf[rr % 2], 1)
            attention("mla")
            for u in range(U_MO, U_MO + 3):
                step(u)
            operand("op_f2", [(c, col("ffn_norm", 8 + c)) for c in range(DC)], U_F2)
            ffn(1, 3)
            operand("op_f3", [(c, col("ffn_pre", c)) for c in range(DC)], U_F3)
            ffn(2, 4)
            post_ffn(0, U_F3)
            operand("op_conv", [(c, col("mix_pre", c)) for c in range(DC)], U_PW1)
            for w, chunks in enumerate(PW1):
                u = U_PW1 + w
                hi_b(u)
                hi_a(u + 1)
                if w == 0:
                    norm(5)
                for q in chunks:
                    if q % 2:
                        c = q // 2
                        act.wait_ge(s_cgu, c + 1)
                        nc.scalar.activation(sg[:, c % 2, :], gu[:, c % 2, T:2 * T], ACT.Sigmoid,
                                             bias=col("b_pw1", 8 + c)).then_inc(s_sig, 1)
            act.wait_ge(ev["conv_summed"], 1)
            for c in range(CONV_PE):
                ins = nc.scalar.activation(conv_c[:, CONV_DVE + c, :], acc[2 + c // 2][:, (c % 2) * T:(c % 2 + 1) * T],
                                           ACT.Identity, bias=col("b_dw", CONV_DVE + c))
            ins.then_inc(ev["sum_ready"], 1)
            for q in range(2):
                act.wait_ge(ev["centred"], q + 1)
                h = slice(4 * q, 4 * q + 4)
                nc.scalar.activation(conv_s[:, h, :], conv_c[:, h, :], ACT.Square).then_inc(ev["sq_ready"], 1)
            act.wait_ge(ev["var_done"], 1)
            nc.scalar.activation(conv_r[:, 0, :], acc[1][:, 0:T], ACT.Sqrt, bias=LN_EPS)\
                .then_inc(ev["conv_std"], 1)
            act.wait_ge(s_useb, U_PW2)
            for q in range(4):
                act.wait_ge(ev["lny_ready"], q + 1)
                for c in (2 * q, 2 * q + 1):
                    ins = nc.scalar.activation(conv_s[:, c, :], conv_c[:, c, :], ACT.Silu, scale=col("ln_g", c),
                                               bias=col("ln_b", c))
                own(ins)
                h = slice(2 * q, 2 * q + 2)
                nc.scalar.activation(hthi[:, h, :], conv_s[:, h, :], ACT.Copy).then_inc(ev["conv_hi"], 1)
            mixer_out(U_PW2)
            post_mixer(1)
            operand("op_f4", [(c, col("ffn_pre", 8 + c)) for c in range(DC)], U_F4)
            ffn(3, 6)
            post_ffn(2, U_F4)
            operand("op_f5", [(c, col("ffn_pre", 16 + c)) for c in range(DC)], U_F5)
            ffn(4, 7)
            post_ffn(3, U_F5)
            operand("op_qkv", [(c, col("mix_pre", 8 + c)) for c in range(DC)], U_QKV)
            def k3_copies(first):
                act.wait_ge(ev["kz_zeroed"], 2)
                for r in (first, first + 1):
                    rr = RD["k3"] + r
                    act.wait_ge(s_tr, rr + 1)
                    for m in range(2):
                        ins = nc.scalar.activation(
                            kz[m * 64:(m + 1) * 64, m, 2 * r:2 * r + 2, :],
                            tp[rr % 2][m * 64:(m + 1) * 64, :].rearrange("p (a n) -> p a n", a=2), ACT.Copy)
                    ins.then_inc(s_tf[rr % 2], 1)

            for u in range(U_QKV, U_QKV + 8):
                step(u, lambda t, u, c, w: p3[:, t, (u - U_QKV) * PITCH + c:(u - U_QKV) * PITCH + c + w], 8, u == U_QKV)
                if QK3.get(u - U_QKV, ("",))[0] == "k3":
                    k3_copies(QK3[u - U_QKV][1])
            act.wait_ge(ev["lam_sum"], 1)
            nc.scalar.activation(lam[:, 2:4], lam[:, 0:2], ACT.Exp).then_inc(ev["lam_exp"], 1)
            attention("diff")
            act.wait_ge(s_od, 2 * H3)
            sqrt("subln", 16, 2 * DH, SUBLN_EPS)
            operand("op_wo", [(c, sgain[:, 0:1]) for c in range(DC)], U_WO)
            mixer_out(U_WO)
            post_mixer(4)
            operand("op_f6", [(c, col("ffn_pre", 24 + c)) for c in range(DC)], U_F6)
            ffn(5, 9)
            post_ffn(5, U_F6)

        @block.tensor
        def _(pe):
            def mm3(out, whi_, wlo_, mhi, mlo, start, stop):
                nc.tensor.matmul(out, whi_, mhi, start=start, stop=False)
                nc.tensor.matmul(out, whi_, mlo, start=False, stop=False)
                return nc.tensor.matmul(out, wlo_, mhi, start=False, stop=stop)

            def bank_free(r):
                if r >= 2:
                    pe.wait_ge(s_tf[r % 2], r // 2)

            def rounds(name, cnt, per, blocks, first=0):
                for q in range(cnt):
                    r = RD[name] + first + q
                    bank_free(r)
                    for j, (rows_out, width, src) in enumerate(blocks(q)):
                        ins = nc.tensor.transpose(tp[r % 2][0:rows_out, j * per:j * per + width], src,
                                                  const[0:width, KO["ident"]:KO["ident"] + width])
                    ins.then_inc(s_tr, 1)

            def operand(name, src, nchunks):
                rounds(name, (nchunks + 1) // 2, P,
                       lambda q: [(P, P, src(t, 2 * q + j)) for j in range(min(2, nchunks - 2 * q)) for t in range(NT)])

            def operand_ahead(name, src, there):
                def one(q):
                    if q % 2 == 0:
                        there(q)
                    rounds(name, 1, P, lambda _: [(P, P, src(t, c)) for c in (2 * q, 2 * q + 1) for t in range(NT)], q)

                def ready(k):
                    if k % 2 == 0 and k < 4:
                        one(k // 2 + 2)
                    elif k % 2 == 0:
                        r = RD[name] + k // 2
                        pe.wait_ge(s_tf[r % 2], r // 2 + 1)

                one(0)
                one(1)
                return ready

            def x_operand(name, m):
                def there(q):
                    pe.wait_ge(s_x, 4 * m - 2 + q) if m else pe.wait_ge(s_ldx, 16)
                return operand_ahead(name, lambda t, c: x[:, t, c * P:(c + 1) * P], there)

            def norm_rows(name, m):
                r = RD[name]
                pe.wait_ge(s_rs, RSTD[f"n{m}"] + 1)
                bank_free(r)
                for t in range(NT):
                    ins = nc.tensor.matmul(tp[r % 2][:, t * P:(t + 1) * P],
                                           rs[:, NORM + t:NORM + t + 1].to_broadcast([P, P]), ident, start=True, stop=True)
                ins.then_inc(s_tr, 1)

            def taken(name, cnt):
                last = RD[name] + cnt - 1
                for r in (last - 1, last):
                    pe.wait_ge(s_tf[r % 2], r // 2 + 1)

            def step(u, k0=0, ready=None):
                kk, pitch, pieces = STEPS[u]
                s, end = u % 2, pieces[-1][0] + pieces[-1][1]
                banks, before, _, _ = plan[u]
                if before >= 0:
                    pe.wait_ge(s_eva, plan[before][2])
                    pe.wait_ge(s_evd, plan[before][3])
                pe.wait_ge(s_loa, u + 1)
                used_a = b_ready = False
                for k in range(kk):
                    if ready is not None:
                        ready(k)
                    if k * pitch + end > UA and not b_ready:
                        pe.wait_ge(s_lob, u + 1)
                        b_ready = True
                    for t in range(NT):
                        for j, (c, w) in enumerate(pieces):
                            sl = slice(k * pitch + c, k * pitch + c + w)
                            lhs = slice(t * P, (t + 1) * P)
                            ins = mm3(acc[banks[t][j]][:, 0:w], hthi[:, k0 + k, lhs], htlo[:, k0 + k, lhs],
                                      whi[:, s, sl], wlo[:, s, sl], k == 0, k == kk - 1)
                    if (k + 1) * pitch >= UA and not used_a:
                        ins.then_inc(s_usea, 1)
                        used_a = True
                ins.then_inc(s_useb, 1)

            def gate_up(f, c, i=0, ready=None):
                s, b = (f + c) % 2, c % 2
                pe.wait_ge(s_loa, i * 2 + (f + c + 1))
                for half in range(2):
                    for k in range(DC):
                        if ready is not None and half == 0:
                            ready(k)
                        at = half * 1024 + k * P
                        ins = mm3(gub[b][:, half * T:(half + 1) * T], whi[:, s, at:at + P], wlo[:, s, at:at + P],
                                  hthi[:, k, :], htlo[:, k, :], k == 0, k == DC - 1)
                ins.then_inc(s_usea, 1)

            def down(f, fi, c, i=0, start=False, stop=False):
                s, b = (f + c) % 2, c % 2
                pe.wait_ge(s_lob, i * 2 + (f + c + 1))
                pe.wait_ge(s_hid, i * 2 + (FC * fi + c + 1))
                for j in range(2):
                    for t in range(NT):
                        lhs, sl = slice(t * P, (t + 1) * P), slice(UA + j * 512, UA + (j + 1) * 512)
                        nc.tensor.matmul(acc[2 * t + j][:, :], hidhi[:, b, lhs], whi[:, s, sl], start=start, stop=False,
                                         skip_group_check=True)
                        nc.tensor.matmul(acc[2 * t + j][:, :], hidhi[:, b, lhs], wlo[:, s, sl], start=False, stop=False,
                                         skip_group_check=True)
                        ins = nc.tensor.matmul(acc[2 * t + j][:, :], hidlo[:, b, lhs], whi[:, s, sl], start=False,
                                               stop=stop, skip_group_check=True)
                        if stop and j + t < 2:
                            ins.then_inc(s_fin, 1)
                ins.then_inc(s_useb, 1)

            def ffn(fi, m):
                f = FUNITS[fi]
                gate_up(f, 0, ready=x_operand(f"op_f{fi + 1}", m))
                norm_rows(f"r_f{fi + 1}", m)
                gate_up(f, 1)
                down(f, fi, 0, start=True)
                with pe.Fori(1, FC // 2) as i:
                    for j in range(2):
                        pe.wait_ge(s_hid, i * 2 + (FC * fi + j - 1))
                        gate_up(f, j, i)
                        down(f, fi, j - 1, i) if j else down_prev(f, fi, i)
                down(f, fi, FC - 1, stop=True)

            def down_prev(f, fi, i):
                s = (f + 1) % 2
                pe.wait_ge(s_lob, i * 2 + f)
                pe.wait_ge(s_hid, i * 2 + FC * fi)
                for t in range(NT):
                    for j in range(2):
                        lhs, sl = slice(t * P, (t + 1) * P), slice(UA + j * 512, UA + (j + 1) * 512)
                        for a, w in ((hidhi, whi), (hidhi, wlo), (hidlo, whi)):
                            ins = nc.tensor.matmul(acc[2 * t + j][:, :], a[:, 1, lhs], w[:, s, sl], start=False, stop=False,
                                                   skip_group_check=True)
                ins.then_inc(s_useb, 1)

            def attention(kind):
                base, cnt = ITEM0[kind], NITEM[kind]

                def scores(i):
                    g = base + i
                    if g >= 4:
                        pe.wait_ge(s_bia, g - 3)
                    b = acc[g % 4]
                    if kind == "nsa":
                        h, t = i // 2, i % 2
                        nk = P * (t + 1)
                        for br in range(2):
                            ins = nc.tensor.matmul(b[:, br * T:br * T + nk], qT[:, h // 2, t * P:(t + 1) * P],
                                                   kz[:, h % 2, br * G1 + h // 4, 0:nk], start=True, stop=True)
                    elif kind == "mla":
                        o = (i % 2) * ROPE
                        for t in range(NT):
                            nc.tensor.matmul(b[:, t * T:(t + 1) * T], qT[:, i, t * P:(t + 1) * P], kT2[:, i, :],
                                             start=True, stop=False)
                            ins = nc.tensor.matmul(b[:, t * T:(t + 1) * T], qpT[o:o + ROPE, i // 2, t * P:(t + 1) * P],
                                                   kpT[o:o + ROPE, i // 2, :], start=False, stop=True)
                    else:
                        h, t = i // 2, i % 2
                        for m in range(2):
                            ins = nc.tensor.matmul(b[:, m * T:(m + 1) * T], qT[:, h, t * P:(t + 1) * P], kz[:, m, h, :],
                                                   start=True, stop=True)
                    ins.then_inc(s_sco, 1)

                def transposes(i):
                    g, r = base + i, RD[kind] + i
                    pe.wait_ge(s_prob, g + 1)
                    bank_free(r)
                    for j, (br, k) in enumerate(item_blocks(kind, i)):
                        ins = nc.tensor.transpose(tp[r % 2][:, j * P:(j + 1) * P], s_pr[:, g % 2, br, k * P:(k + 1) * P],
                                                  ident)
                    ins.then_inc(s_tr, 1)

                def values(i):
                    g, r = base + i, RD[kind] + i
                    pe.wait_ge(s_tf[r % 2], r // 2 + 1)
                    blocks = item_blocks(kind, i)

                    def pt(j):
                        return s_pt[:, g % 2, j * P:(j + 1) * P]

                    if kind == "nsa":
                        h, t = i // 2, i % 2
                        if i % 4 == 0 and i >= 8:
                            pe.wait_ge(s_ol, i // 4 - 1)
                        out = gub[(h // 2) % 2][(h % 2) * 64:(h % 2 + 1) * 64, t * P:(t + 1) * P]
                        nc.tensor.matmul(out, vcmp[:, :], pct[t][:, h, :], start=True, stop=False)
                        for j, (br, k) in enumerate(blocks):
                            c = (COL_VS, COL_VW)[br] + (h // 4) * DH
                            ins = nc.tensor.matmul(out, p1[:, k, c:c + DH], pt(j), start=False, stop=j == len(blocks) - 1)
                    elif kind == "mla":
                        pe.wait_ge(s_ol, 8 + i - 1)
                        out = gub[i % 2]
                        nc.tensor.matmul(out[:, 0:P], kv[:, 0, i, NOPE:], pt(0), start=True, stop=True)
                        nc.tensor.matmul(out[:, P:T], kv[:, 0, i, NOPE:], pt(1), start=True, stop=False)
                        ins = nc.tensor.matmul(out[:, P:T], kv[:, 1, i, NOPE:], pt(2), start=False, stop=True)
                    else:
                        h = i // 2
                        if i >= 2:
                            pe.wait_ge(s_od, i - 1)
                        for k in range(NT):
                            ins = nc.tensor.matmul(gub[g % 2][:, 0:P], pt(k), p3[:, k, 2048 + h * P:2048 + (h + 1) * P],
                                                   start=k == 0, stop=k == NT - 1)
                    ins.then_inc(s_pv, 1)

                scores(0)
                scores(1)
                for i in range(cnt + 2):
                    if i + 2 < cnt:
                        scores(i + 2)
                    if 1 <= i <= cnt:
                        transposes(i - 1)
                    if i >= 2:
                        values(i - 2)

            pe.wait_ge(s_ldi, 16)
            step(U_IN, ready=x_operand("op_attn", 0))
            for u in range(U_IN + 1, U_IN + 5):
                step(u)
            pe.wait_ge(s_eva, plan[U_IN + 3][2])
            pe.wait_ge(s_evd, plan[U_IN + 3][3])
            rounds("kcvc", 2, P, lambda q: [(P, P, p1[:, t, COL_KC + q * T + a * P:COL_KC + q * T + (a + 1) * P])
                                            for a in range(2) for t in range(NT)])
            step(U_IN + 5)
            step(U_IN + 6)
            pe.wait_ge(s_eva, 6)
            pe.wait_ge(s_evd, 6)
            for w in range(3):
                u = U_CMP + w
                s = u % 2
                for m in range(12 if w < 2 else 8):
                    e = 12 * w + m
                    v = e // 16
                    if m == 0:
                        pe.wait_ge(s_loa, u + 1)
                    if m == 8 or e == 30:
                        pe.wait_ge(s_lob, u + 1)
                    if e % 16 == 0:
                        pe.wait_ge(ev["blk_ready"], v + 1)
                    mv = slice(e * GJ, (e + 1) * GJ)
                    at = slice(m * CMP_HIDDEN, (m + 1) * CMP_HIDDEN)
                    ins = mm3(acc[2 + v][0:GJ, 0:CMP_HIDDEN], blkhi[:, mv], blklo[:, mv], whi[:, s, at], wlo[:, s, at],
                              e % 16 == 0, e % 16 == 15)
                    if e == 30:
                        ins.then_inc(s_useb, 1)
                    if m == 7:
                        ins.then_inc(s_usea, 1)
                if w < 2:
                    ins.then_inc(s_useb, 1)
            pe.wait_ge(ev["hx_ready"], 1)
            rounds("hx", 1, GJ, lambda q: [(P, GJ, hx[:, j * P:(j + 1) * P]) for j in range(4)])
            pe.wait_ge(ev["qn_ready"], 1)
            rounds("q1", 4, P, lambda q: [(P, P, p1[:, t, c * P:(c + 1) * P]) for c in (2 * q, 2 * q + 1) for t in range(NT)])
            pe.wait_ge(ev["gelu_ready"], 1)
            for v in range(2):
                for half in range(2):
                    ins = nc.tensor.matmul(gub[0][0:GJ, v * DH:(v + 1) * DH], att[:, 720 + (2 * v + half) * GJ:720 + (2 * v + half + 1) * GJ],
                                           cols[:, CO["w2"] + (2 * v + half) * DH:CO["w2"] + (2 * v + half + 1) * DH],
                                           start=half == 0, stop=half == 1)
            ins.then_inc(ev["w2_done"], 1)
            pe.wait_ge(ev["kcd_ready"], 1)
            rounds("kcmp", 1, P, lambda q: [(P, GJ, kcd[:, :, :].rearrange("p d n -> p (d n)"))])
            taken("kcmp", 1)
            pe.wait_ge(ev["kz_zeroed"], 1)
            for t in range(NT):
                for c in range(H1 // 2):
                    at = (c % 4) * 2 * GJ
                    ins = nc.tensor.matmul(acc[2 - 2 * t + c // 4][:, at:at + 2 * GJ], qT[:, c, t * P:(t + 1) * P],
                                           kcz[:, :, :].rearrange("p m n -> p (m n)"), start=True, stop=True)
                ins.then_inc(ev[f"cs{t}"], 1)
            pe.wait_ge(ev["kd_ready"], 1)
            rounds("k1", 4, P, lambda q: [(P, P, kd[:, t, g, :, :].rearrange("p d n -> p (d n)"))
                                          for g in (2 * q, 2 * q + 1) for t in range(NT)])
            for t in range(NT):
                pe.wait_ge(ev[f"cp{t}"], 1)
                rounds(f"pc{t}", 4, P, lambda q: [(GJ, P, pr_cmp[t][:, (4 * q + j) * GJ:(4 * q + j + 1) * GJ])
                                                  for j in range(4)])
            taken("pc1", 4)
            attention("nsa")
            pe.wait_ge(s_ol, 8)
            for u in range(U_OUT, U_OUT + 3):
                step(u)
            ffn(0, 1)
            step(U_KVA, ready=x_operand("op_kv", 2))
            step(U_QA, ready=x_operand("op_bq", 2))
            pe.wait_ge(ev["ckv_ready"], 1)
            operand("op_ckv", lambda t, c: kva[:, t, c * P:(c + 1) * P], 2)
            pe.wait_ge(ev["qa_ready"], 1)
            operand("op_qa", lambda t, c: qa[:, t, c * P:(c + 1) * P], 3)
            taken("op_qa", 2)
            for u in (U_KVB, U_KVB + 1):
                step(u)
            for u in (U_QB, U_QB + 1):
                step(u, 2)
            pe.wait_ge(ev["k2n_ready"], 1)
            rounds("k2", 4, P, lambda q: [(P, P, kv[:, t, h, 0:NOPE]) for h in (2 * q, 2 * q + 1) for t in range(NT)])
            pe.wait_ge(ev["kpe_ready"], 1)
            rounds("kpe", 2, P, lambda q: [(P, P, kpe[:, t, 2 * c:2 * c + 2, :].rearrange("p a n -> p (a n)"))
                                           for c in (2 * q, 2 * q + 1) for t in range(NT)])
            pe.wait_ge(ev["q2n_ready"], 1)
            rounds("q2", 4, P, lambda q: [(P, P, q2[:, t, h, 0:NOPE]) for h in (2 * q, 2 * q + 1) for t in range(NT)])
            pe.wait_ge(ev["qpe_ready"], 1)
            rounds("qpe", 2, P, lambda q: [(P, P, qpe[:, t, 2 * c:2 * c + 2, :].rearrange("p a n -> p (a n)"))
                                           for c in (2 * q, 2 * q + 1) for t in range(NT)])
            taken("qpe", 2)
            attention("mla")
            pe.wait_ge(s_ol, 16)
            for u in range(U_MO, U_MO + 3):
                step(u)
            ffn(1, 3)
            ffn(2, 4)
            ready = x_operand("op_conv", 5)
            for w, chunks in enumerate(PW1):
                u = U_PW1 + w
                s = u % 2
                pe.wait_ge(s_loa, u + 1)
                for m, q in enumerate(chunks):
                    if m == 2:
                        pe.wait_ge(s_lob, u + 1)
                    if q % 2 == 0 and q >= 4:
                        pe.wait_ge(s_cgu, q // 2 - 1)
                    for k in range(DC):
                        if q == 0:
                            ready(k)
                        at = m * 1024 + k * P
                        ins = mm3(gub[(q // 2) % 2][:, (q % 2) * T:(q % 2 + 1) * T], whi[:, s, at:at + P],
                                  wlo[:, s, at:at + P], hthi[:, k, :], htlo[:, k, :], k == 0, k == DC - 1)
                        if len(chunks) == 2 and m == 1 and k == 0:
                            pe.wait_ge(s_lob, u + 1)
                            ins.then_inc(s_useb, 1)
                    if m == 0 and q % 2:
                        ins.then_inc(s_pw, 1)
                    if m == 1:
                        ins.then_inc(s_usea, 1)
                    if m == 2:
                        ins.then_inc(s_useb, 1)
                    if q == 2:
                        norm_rows("r_conv", 5)
            pe.wait_ge(ev["diagonals_ready"], 1)
            pe.wait_ge(s_glu, 8)
            for c, k0, cnt, part, at in diag_runs:
                b = c - CONV_DVE
                for k in range(k0, k0 + cnt):
                    ins = nc.tensor.matmul(acc[2 + b // 2][:, (b % 2) * T:(b % 2 + 1) * T], diag[part][:, at + k - k0, :],
                                           conv_u[:, c, k:k + T], start=k == 0, stop=k == TAPS - 1)
            ins.then_inc(ev["conv_summed"], 1)
            pe.wait_ge(ev["diagonals_ready"], 2)
            for k in range(SPLIT, TAPS):
                ins = nc.tensor.matmul(acc[1][:, 0:T], diag_shared[:, k - SPLIT, :], conv_u[:, SHARED, k:k + T],
                                       start=k == SPLIT, stop=k == TAPS - 1)
            ins.then_inc(ev["conv_summed"], 1)
            pe.wait_ge(ev["conv_early"], 1)
            for c in (0, 1):
                nc.tensor.matmul(acc[0][:, 0:T], ones, conv_c[:, c, :], start=c == 0, stop=False)
            pe.wait_ge(ev["sum_ready"], 1)
            for c in range(CONV_DVE, 8):
                nc.tensor.matmul(acc[0][:, 0:T], ones, conv_c[:, c, :], start=False, stop=False)
            pe.wait_ge(ev["conv_ready"], 1)
            for c in range(2, CONV_DVE):
                ins = nc.tensor.matmul(acc[0][:, 0:T], ones, conv_c[:, c, :], start=False, stop=c == CONV_DVE - 1)
            ins.then_inc(ev["mean_done"], 1)
            for c in range(8):
                if c % 4 == 0:
                    pe.wait_ge(ev["sq_ready"], c // 4 + 1)
                ins = nc.tensor.matmul(acc[1][:, 0:T], ones, conv_s[:, c, :], start=c == 0, stop=c == 7)
            ins.then_inc(ev["var_done"], 1)
            step(U_PW2, ready=lambda k: pe.wait_ge(ev["conv_lo"], k // 2 + 1) if k % 2 == 0 else None)
            for u in range(U_PW2 + 1, U_PW2 + 3):
                step(u)
            ffn(3, 6)
            ffn(4, 7)
            step(U_QKV, ready=x_operand("op_qkv", 8))
            for u in range(U_QKV + 1, U_QKV + 8):
                step(u)
                if u - U_QKV in QK3:
                    name, first = QK3[u - U_QKV]
                    at = 0 if name == "q3" else 1024
                    pe.wait_ge(s_eva, plan[u - 1][2])
                    pe.wait_ge(s_evd, plan[u - 1][3])
                    rounds(name, 2, P, lambda q: [(P, P, p3[:, t, at + c * P:at + (c + 1) * P])
                                                  for c in (2 * (q + first), 2 * (q + first) + 1) for t in range(NT)], first)
            pe.wait_ge(s_eva, plan[U_QKV + 7][2])
            pe.wait_ge(s_evd, plan[U_QKV + 7][3])
            attention("diff")
            step(U_WO, ready=operand_ahead("op_wo", lambda t, c: diff_o[:, t, c * P:(c + 1) * P],
                                           lambda q: pe.wait_ge(ev["sub_ready"], q // 2 + 1)))
            for u in (U_WO + 1, U_WO + 2):
                step(u)
            ffn(5, 9)

        @block.vector
        def _(dve):
            n = dict(own=0)
            V = nc.vector

            def own(ins):
                n["own"] += 1
                ins.then_inc(s_dve, 1)
                dve.wait_ge(s_dve, n["own"])

            def lo_a(u, i=0):
                s = u % 2
                dve.wait_ge(s_hia, i * 2 + (u + 1))
                V.tensor_tensor(wlo[:, s, 0:UA], raw[:, s, 0:UA], whi[:, s, 0:UA].bitcast(F32), ALU.subtract)\
                    .then_inc(s_loa, 1)

            def lo_b(u, i=0):
                s = u % 2
                dve.wait_ge(s_hib, i * 2 + (u + 1))
                V.tensor_tensor(wlo[:, s, UA:UNIT], raw[:, s, UA:UNIT], whi[:, s, UA:UNIT].bitcast(F32), ALU.subtract)\
                    .then_inc(s_lob, 1)

            def step(u, dst=None, m=None, first=False, between=None):
                lo_b(u)
                lo_a(u + 1)
                if between is not None:
                    between()
                if first:
                    rstd(f"n{m}", 2, at=NORM)
                banks = plan[u][0]
                dve.wait_ge(s_useb, u + 1)
                if dst is not None:
                    for j, (c, w) in enumerate(STEPS[u][2]):
                        src = acc[banks[1][j]][:, 0:w]
                        out = dst(1, u, c, w)
                        if m is None:
                            ins = V.tensor_copy(out, src)
                        else:
                            ins = V.tensor_scalar(out, src, rs[:, NORM + 1:NORM + 2], None, ALU.mult)
                    ins.then_inc(s_evd, 1)

            def add_steps(first):
                for u in range(first, first + 3):
                    step(u)
                    a, w = (u - first) * PITCH, STEPS[u][2][0][1]
                    for t in range(NT):
                        ins = V.tensor_tensor(x[:, t, a:a + w], x[:, t, a:a + w], acc[plan[u][0][t][0]][:, 0:w], ALU.add)
                        if u == first + 2:
                            ins.then_inc(s_x, 2)
                    if u < first + 2:
                        ins.then_inc(s_evd, 1)

            def rstd(name, cnt, r=P, at=0):
                dve.wait_ge(s_std, RSTD[name] + 1)
                V.reciprocal(rs[0:r, at:at + cnt], std[0:r, at:at + cnt]).then_inc(s_rs, 1)
                dve.wait_ge(s_rs, RSTD[name] + 1)

            def norm_rows(name, m):
                rstd(f"n{m}", 2, at=NORM)
                r = RD[name]
                dve.wait_ge(s_tr, r + 1)
                V.tensor_copy(rb[:, :], tp[r % 2][:, 0:T]).then_inc(s_tf[r % 2], 1)
                dve.wait_ge(s_tf[r % 2], r // 2 + 1)

            def operand(name, chunks):
                for a in range(0, len(chunks), 2):
                    r = RD[name] + a // 2
                    dve.wait_ge(s_thi, OPN[name] + a // 2 + 1)
                    for j, (dst, gain) in enumerate(chunks[a:a + 2]):
                        ins = V.scalar_tensor_tensor(out=htlo[:, dst, :], in0=tp[r % 2][:, j * T:(j + 1) * T],
                                                     scalar=gain, in1=hthi[:, dst, :].bitcast(F32),
                                                     op0=ALU.mult, op1=ALU.subtract)
                    ins.then_inc(s_tf[r % 2], 1)

            both = rb[:, :].unsqueeze(1).to_broadcast([P, 2, T])

            def ffn(fi, m):
                f = FUNITS[fi]

                def chunk(j, i=0, first=False):
                    lo_a(f + j + 1, i)
                    if first:
                        norm_rows(f"r_f{fi + 1}", m)
                    dve.wait_ge(s_usea, i * 2 + (f + j + 1))
                    V.tensor_tensor(gu[:, j, :].rearrange("p (h n) -> p h n", h=2), gate_up_bank[j], both, ALU.mult)\
                        .then_inc(s_gu, 1)
                    dve.wait_ge(s_silu, i * 2 + (FC * fi + j + 1))
                    V.tensor_tensor(hidf[:, j, :], sg[:, j, :], gu[:, j, T:2 * T], ALU.mult).then_inc(s_hf, 1)
                    dve.wait_ge(s_hf, i * 2 + (FC * fi + j + 1))
                    dve.wait_ge(s_useb, i * 2 + (f + j - 1))
                    V.tensor_copy(hidhi[:, j, :], hidf[:, j, :]).then_inc(s_hh, 1)
                    dve.wait_ge(s_hh, i * 2 + (FC * fi + j + 1))
                    V.tensor_tensor(hidlo[:, j, :], hidf[:, j, :], hidhi[:, j, :].bitcast(F32), ALU.subtract)\
                        .then_inc(s_hid, 1)
                    lo_b(f + j, i)

                chunk(0, first=True)
                chunk(1)
                with dve.Fori(1, FC // 2) as i:
                    chunk(0, i)
                    chunk(1, i)

            def add_ffn(f):
                for j in range(2):
                    for t in range(NT):
                        if j + t < 2:
                            dve.wait_ge(s_fin, 3 * FUNITS.index(f) + 2 * j + t + 1)
                        else:
                            dve.wait_ge(s_useb, f + FC)
                        sl = slice(j * 512, (j + 1) * 512)
                        V.tensor_tensor(x[:, t, sl], x[:, t, sl], acc[2 * t + j][:, :], ALU.add).then_inc(s_x, 1)

            def post_ffn(k, row):
                dve.wait_ge(s_pss, [0, None, 1, 2, None, 3][k] + 1)
                V.tensor_tensor(ss[:, 0:2], ss[:, 8:12].rearrange("p (t j) -> p t j", j=2)[:, :, 0],
                                ss[:, 8:12].rearrange("p (t j) -> p t j", j=2)[:, :, 1], ALU.add).then_inc(s_phs, 1)
                rstd(f"post{k}", 2)
                dve.wait_ge(s_ldw[row % 2], 16 * (row // 2 + 1))
                for j in range(2):
                    sl = slice(j * 512, (j + 1) * 512)
                    for t in range(NT):
                        ins = V.scalar_tensor_tensor(out=xn[:, t, sl], in0=acc[2 * t + j][:, :], scalar=rs[:, t:t + 1],
                                                     in1=wide[:, row % 2, sl], op0=ALU.mult, op1=ALU.mult)
                    if j == 0:
                        own(ins)
                    else:
                        ins.then_inc(s_wu, 1)
                        dve.wait_ge(s_wu, row + 1)
                    for t in range(NT):
                        V.scalar_tensor_tensor(out=x[:, t, sl], in0=xn[:, t, sl], scalar=0.5, in1=x[:, t, sl],
                                               op0=ALU.mult, op1=ALU.add).then_inc(s_x, 1)

            def mixer_out(first, bias=None):
                for w in range(3):
                    u = first + w
                    lo_b(u)
                    lo_a(u + 1)
                    dve.wait_ge(s_useb, u + 1)
                    n_ = STEPS[u][2][0][1]
                    sl = slice(w * PITCH, w * PITCH + n_)
                    for t in range(NT):
                        src = acc[plan[u][0][t][0]][:, 0:n_]
                        if bias is None:
                            ins = V.tensor_copy(m_out[:, t, sl], src)
                        else:
                            ins = V.tensor_tensor(m_out[:, t, sl], src, bias(sl), ALU.add)
                    ins.then_inc(s_evd, 1)

            def post_mixer(k, row, first):
                dve.wait_ge(s_eva, plan[first + 2][2])
                V.tensor_reduce(ss[:, 0:2], ss[:, 8:14].rearrange("p (t j) -> p t j", t=NT), AX, ALU.add).then_inc(s_phs, 1)
                rstd(f"post{k}", 2)
                dve.wait_ge(s_ldw[row % 2], 16 * (row // 2 + 1))
                for j in range(2):
                    sl = slice(j * 512, (j + 1) * 512)
                    for t in range(NT):
                        ins = V.scalar_tensor_tensor(out=xn[:, t, sl], in0=m_out[:, t, sl], scalar=rs[:, t:t + 1],
                                                     in1=wide[:, row % 2, sl], op0=ALU.mult, op1=ALU.mult)
                        if k == 1 and j == t == 0:
                            ins.then_inc(s_wu, 1)
                    if j == 0:
                        own(ins)
                    else:
                        ins.then_inc(s_wu, 1)
                        dve.wait_ge(s_wu, row + 1)
                    for t in range(NT):
                        V.tensor_tensor(x[:, t, sl], x[:, t, sl], xn[:, t, sl], ALU.add).then_inc(s_x, 1)

            def attention(kind):
                base, cnt = ITEM0[kind], NITEM[kind]

                def bias(i):
                    g, t = base + i, i % 2
                    dve.wait_ge(s_sco, g + 1)
                    if g >= 2:
                        dve.wait_ge(s_exp, g - 1)
                    nk = P * (t + 1) if kind == "nsa" else T
                    src = acc[g % 4][:, :].rearrange("p (b n) -> p b n", b=2)[:, :, 0:nk]
                    out = s_sc[:, g % 2, :, 0:nk]
                    if kind == "mla":
                        own(V.scalar_tensor_tensor(out=out, in0=src, scalar=float(QK) ** -0.5,
                                                   in1=const[:, KO["mask"]:KO["mask"] + 512].rearrange("p (t n) -> p t n", t=2),
                                                   op0=ALU.mult, op1=ALU.add))
                    else:
                        k = KO["causal" if kind == "nsa" else "dist"] + t * T
                        slope = SLOPES1[i // 2] if kind == "nsa" else -SLOPES3[i // 2]
                        own(V.scalar_tensor_tensor(out=out, in0=const[:, k:k + nk].unsqueeze(1).to_broadcast([P, 2, nk]),
                                                   scalar=slope, in1=src, op0=ALU.mult, op1=ALU.add))
                    V.tensor_reduce(nmax[:, g % 2, 0:2], out, AX, ALU.max, negate=True).then_inc(s_bia, 1)

                def probs(i):
                    g, t = base + i, i % 2
                    s = g % 2
                    nk = P * (t + 1) if kind == "nsa" else T
                    dve.wait_ge(s_exp, g + 1)
                    own(V.reciprocal(pw[:, s, 0:2], lsum[:, s, 0:2]))
                    if kind == "nsa":
                        h = i // 2
                        own(V.tensor_tensor(pw[:, s, 2:4], pw[:, s, 0:2], gates[:, t, 3 * h + 1:3 * h + 3], ALU.mult))
                        for b in range(2):
                            ins = V.tensor_scalar(s_pr[:, s, b, 0:nk], s_pr[:, s, b, 0:nk], pw[:, s, 2 + b:3 + b], None, ALU.mult)
                    elif kind == "mla":
                        for b in range(2):
                            ins = V.tensor_scalar(s_pr[:, s, b, :], s_pr[:, s, b, :], pw[:, s, b:b + 1], None, ALU.mult)
                    else:
                        V.tensor_scalar(pw[:, s, 2:3], pw[:, s, 1:2], lam[:, 4:5], None, ALU.mult)
                        own(V.tensor_scalar(s_pr[:, s, 0, :], s_pr[:, s, 0, :], pw[:, s, 0:1], None, ALU.mult))
                        ins = V.scalar_tensor_tensor(out=s_pr[:, s, 0, :], in0=s_pr[:, s, 1, :], scalar=pw[:, s, 2:3],
                                                     in1=s_pr[:, s, 0, :], op0=ALU.mult, op1=ALU.add)
                    ins.then_inc(s_prob, 1)

                def post(i):
                    if kind == "nsa" and i % 4 == 3:
                        c = i // 4
                        dve.wait_ge(s_oh, c + 1)
                        V.tensor_tensor(htlo[:, c, :], gub[c % 2][:, 0:T], hthi[:, c, :].bitcast(F32), ALU.subtract)\
                            .then_inc(s_ol, 1)
                    if kind == "mla":
                        dve.wait_ge(s_oh, 8 + i + 1)
                        V.tensor_tensor(htlo[:, i, :], gub[i % 2][:, 0:T], hthi[:, i, :].bitcast(F32), ALU.subtract)\
                            .then_inc(s_ol, 1)

                for i in range(cnt + LAG):
                    if i < cnt:
                        bias(i)
                    if 1 <= i <= cnt:
                        probs(i - 1)
                    if i >= LAG:
                        post(i - LAG)

            lo_a(0)
            dve.wait_ge(s_ldc, 16)
            operand("op_attn", [(c, col("attn_norm", c)) for c in range(DC)])
            def blocks():
                dve.wait_ge(s_tf[(RD["kcvc"] + 1) % 2], (RD["kcvc"] + 1) // 2 + 1)
                for v in range(2):
                    for half in range(2):
                        src = kc2[:, v, :, :, :].rearrange("p a b n -> p (a b) n").rearrange("p g (j c r) -> p g j c r", c=8, r=2)
                        src = src[:, :, half:half + NCMP, :, 0].rearrange("p g j c -> p c g j")
                        at = (v * 16 + half * 8) * GJ
                        pos = cols[:, CO["pos"] + v * 16 + half * 8:CO["pos"] + v * 16 + half * 8 + 8]
                        ins = V.tensor_tensor(blk[:, at:at + 8 * GJ].rearrange("p (c g j) -> p c g j", c=8, g=G1), src,
                                              pos.unsqueeze(2).unsqueeze(3).to_broadcast([P, 8, G1, NCMP]), ALU.add)
                own(ins)

            for u in range(U_IN, U_IN + 7):
                step(u, lambda t, u, c, w: p1[:, t, (u - U_IN) * PITCH + c:(u - U_IN) * PITCH + c + w], 0, u == U_IN,
                     blocks if u == U_IN + 5 else None)
                if u == U_IN + 4:
                    r = RD["kcvc"]
                    dve.wait_ge(s_tr, r + 1)
                    for b in range(2):
                        src = tp[r % 2][64 * b:64 * b + 64, :].rearrange("p (a n) -> p a n", a=2)
                        V.tensor_copy(kc2[0:64, 0, :, b, :], src)
                        ins = V.tensor_copy(kc2[64:128, 0, :, b, 0:T - 1], src[:, :, 1:T])
                    ins.then_inc(s_tf[r % 2], 1)
                    dve.wait_ge(s_tf[r % 2], r // 2 + 1)
            for v in range(2):
                h = slice(v * 16 * GJ, (v + 1) * 16 * GJ)
                own(V.tensor_copy(blkhi[:, h], blk[:, h]))
                V.tensor_tensor(blklo[:, h], blk[:, h], blkhi[:, h].bitcast(F32), ALU.subtract).then_inc(ev["blk_ready"], 1)
                if v == 0:
                    lo_b(U_CMP)
            lo_a(U_CMP + 1)
            lo_b(U_CMP + 1)
            lo_a(U_CMP + 2)
            lo_b(U_CMP + 2)
            dve.wait_ge(ev["sq1_ready"], 1)
            V.tensor_reduce(ss[:, 0:48], att[:, 0:3072].rearrange("p (a n) -> p a n", n=DH), AX, ALU.add)\
                .then_inc(ev["ss1_ready"], 1)
            dve.wait_ge(ev["ss1_ready"], 1)
            rstd("qk1", 48)
            dve.wait_ge(ev["blk_ready"], 2)
            for t in range(NT):
                qv = p1[:, t, 0:1024].rearrange("p (h n) -> p h n", h=H1)
                ins = V.tensor_tensor(qv, qv, rs[:, 24 * t:24 * t + 16].unsqueeze(2).to_broadcast([P, H1, DH]), ALU.mult)
            ins.then_inc(ev["qn_ready"], 1)
            r = RD["hx"]
            dve.wait_ge(s_tf[r % 2], r // 2 + 1)
            own(V.tensor_tensor(att[:, 240:480], att[:, 0:240], att[:, 0:240], ALU.mult))
            own(V.tensor_scalar(att[:, 240:480], att[:, 240:480], 0.044715, 1.0, ALU.mult, ALU.add))
            V.tensor_tensor(att[:, 240:480], att[:, 240:480], att[:, 0:240], ALU.mult).then_inc(ev["gelu_in"], 1)
            for r in range(4):
                rr = RD["q1"] + r
                dve.wait_ge(s_tr, rr + 1)
                V.tensor_scalar(qT[:, 2 * r:2 * r + 2, :], tp[rr % 2][:, :].rearrange("p (a n) -> p a n", a=2),
                                col("q_norm"), DH ** -0.5, ALU.mult, ALU.mult).then_inc(s_tf[rr % 2], 1)
            dve.wait_ge(ev["gelu_sig"], 1)
            V.tensor_tensor(att[:, 720:960], att[:, 480:720], att[:, 0:240], ALU.mult).then_inc(ev["gelu_ready"], 1)
            for t in range(NT):
                for b in range(2):
                    c = (COL_KS, COL_KW)[b]
                    src = p1[:, t, c:c + 256].rearrange("p (g n) -> p g n", g=G1)
                    r = rs[:, 24 * t + 16 + 4 * b:24 * t + 20 + 4 * b].unsqueeze(2).to_broadcast([P, G1, DH])
                    for d in range(2):
                        ins = V.tensor_tensor(kd[:, t, 4 * b:4 * b + 4, d, :], src, r, ALU.mult)
            ins.then_inc(ev["kd_ready"], 1)
            rstd("kcmp", 1, GJ)
            V.tensor_copy(vcmp[:, :], gub[0][0:GJ, DH:2 * DH])
            for d in range(2):
                ins = V.tensor_scalar(kcd[:, d, :], gub[0][0:GJ, 0:DH], rs[0:GJ, 0:1], None, ALU.mult)
            ins.then_inc(ev["kcd_ready"], 1)
            lo_a(U_CMP + 3)
            dve.wait_ge(ev["gates_ready"], 1)
            dve.wait_ge(s_ldbc, 16)
            dve.wait_ge(s_ldk, 16)
            for t in range(NT):
                dve.wait_ge(ev[f"cs{t}"], 1)
                for b in range(2):
                    w = 8 * GJ
                    k = (2 * t + b) * w
                    ins = V.tensor_tensor(sc_cmp[t][:, b * w:(b + 1) * w], biasc[:, k:k + w], acc[2 - 2 * t + b][:, 0:w], ALU.add)
                own(ins)
                sv = sc_cmp[t].rearrange("p (h n) -> p h n", h=H1)
                own(V.tensor_reduce(cst[:, 0, :], sv, AX, ALU.max))
                V.tensor_tensor(sv, sv, cst[:, 0, :].unsqueeze(2).to_broadcast([P, H1, GJ]), ALU.subtract)\
                    .then_inc(ev[f"cm{t}"], 1)
                dve.wait_ge(ev[f"cm{t}"], 1)
            for t in range(NT):
                pv = pr_cmp[t].rearrange("p (h n) -> p h n", h=H1)
                dve.wait_ge(ev[f"ce{t}"], 1)
                own(V.tensor_reduce(cst[:, 1, :], pv, AX, ALU.add))
                own(V.reciprocal(cst[:, 2, :], cst[:, 1, :]))
                own(V.scalar_tensor_tensor(out=cst[:, 3, :], in0=cst[:, 2, :],
                                           scalar=const[:, KO["valid"] + t:KO["valid"] + t + 1],
                                           in1=gates[:, t, :].rearrange("p (h n) -> p h n", n=3)[:, :, 0],
                                           op0=ALU.mult, op1=ALU.mult))
                V.tensor_tensor(pv, pv, cst[:, 3, :].unsqueeze(2).to_broadcast([P, H1, GJ]), ALU.mult)\
                    .then_inc(ev[f"cp{t}"], 1)
            attention("nsa")
            add_steps(U_OUT)
            operand("op_f1", [(c, col("ffn_norm", c)) for c in range(DC)])
            ffn(0, 1)
            add_ffn(U_F1)
            operand("op_kv", [(c, col("kv_norm", c)) for c in range(DC)])
            step(U_KVA, lambda t, u, c, w: kva[:, t, c:c + w], 2, True)
            operand("op_bq", [(c, col("b_attn_norm", c)) for c in range(DC)])
            rstd("ckv", 2)
            for t in range(NT):
                ins = V.tensor_scalar(kva[:, t, 0:KVL], kva[:, t, 0:KVL], rs[:, t:t + 1], None, ALU.mult)
            ins.then_inc(ev["ckv_ready"], 1)
            step(U_QA, lambda t, u, c, w: qa[:, t, c:c + w], 2)
            rstd("qan", 2)
            for t in range(NT):
                ins = V.tensor_scalar(qa[:, t, :], qa[:, t, :], rs[:, t:t + 1], None, ALU.mult)
            ins.then_inc(ev["qa_ready"], 1)
            operand("op_ckv", [(c, col("kv_c_norm", c)) for c in range(2)])
            operand("op_qa", [(2 + c, col("q_a_norm", c)) for c in range(3)])
            hr = ROPE // 2
            cos, sin = (const[:, KO[n_]:KO[n_] + ROPE].rearrange("p (t n) -> p t n", t=NT) for n_ in ("cos", "sin"))

            def gain_row(name, half, w=hr):
                return rows[:, RO[name] + half * hr:RO[name] + half * hr + w].unsqueeze(1).to_broadcast([P, NT, w])

            dve.wait_ge(s_ldr, 16)
            for q, (table, half) in enumerate(((cos, 0), (sin, 1), (sin, 0), (cos, 1))):
                V.tensor_tensor(rope_q[:, q, :, :], table, gain_row("qpe", half), ALU.mult)
            own(V.tensor_tensor(kr, kva[:, :, KVL:KVL + ROPE], gain_row("kpe", 0, ROPE), ALU.mult))
            for q, (half, table) in enumerate(((0, cos), (1, sin), (0, sin), (1, cos))):
                ins = V.tensor_tensor(rope_p[:, q, :, :], kr[:, :, half * hr:(half + 1) * hr], table, ALU.mult)
            own(ins)
            V.tensor_tensor(kr[:, :, 0:hr], rope_p[:, 0, :, :], rope_p[:, 1, :, :], ALU.subtract)
            own(V.tensor_tensor(kr[:, :, hr:ROPE], rope_p[:, 2, :, :], rope_p[:, 3, :, :], ALU.add))

            def per_head(r0, w):
                return rs[:, r0:r0 + H2].unsqueeze(2).to_broadcast([P, H2, w])

            def on_heads(k, w):
                return k.unsqueeze(1).to_broadcast([P, H2, w])

            def q2_out(t, u, c, w):
                return q2[:, t, 4 * (u - U_QB) + c // QK:4 * (u - U_QB) + (c + w) // QK, :]

            def k_sums():
                dve.wait_ge(ev["k2_sq"], 1)
                own(V.tensor_reduce(ss[:, 0:16], tr[:, 3072:5120].rearrange("p (a n) -> p a n", n=NOPE), AX, ALU.add))
                for t in range(NT):
                    ins = V.tensor_scalar(ss[:, 8 * t:8 * t + 8], ss[:, 8 * t:8 * t + 8], ss[:, 40 + t:41 + t], None, ALU.add)
                ins.then_inc(ev["k2_ss"], 1)

            def k_scaled():
                for t in range(NT):
                    ins = V.tensor_tensor(kv[:, t, :, 0:NOPE], kv[:, t, :, 0:NOPE], per_head(8 * t, NOPE), ALU.mult)
                ins.then_inc(ev["k2n_ready"], 1)
                for t in range(NT):
                    ins = V.tensor_tensor(kpe[:, t, :, :], on_heads(kr[:, t, :], ROPE), per_head(8 * t, ROPE), ALU.mult)
                ins.then_inc(ev["kpe_ready"], 1)

            for u in (U_KVB, U_KVB + 1):
                step(u, lambda t, u, c, w: kv[:, t, 4 * (u - U_KVB) + c // 256:4 * (u - U_KVB) + (c + w) // 256, :])
            step(U_QB, q2_out, between=k_sums)
            rstd("k2n", 16)
            step(U_QB + 1, q2_out)
            k_scaled()
            for t in range(NT):
                dve.wait_ge(ev["q2_sq"], t + 1)
                ins = V.tensor_reduce(ss[:, 16 + 8 * t:24 + 8 * t], tr[:, t * 1536:(t + 1) * 1536].rearrange("p (a n) -> p a n", n=QK),
                                      AX, ALU.add)
            ins.then_inc(ev["q2_ss"], 1)
            rstd("q2n", 16, at=16)
            for t in range(NT):
                ins = V.tensor_tensor(q2[:, t, :, :], q2[:, t, :, :], per_head(16 + 8 * t, QK), ALU.mult)
            ins.then_inc(ev["q2n_ready"], 1)
            dve.wait_ge(ev["q2n_ready"], 1)
            pr = [[xflat[:, (4 * t + q) * 256:(4 * t + q + 1) * 256].rearrange("p (h n) -> p h n", h=H2)
                   for q in range(4)] for t in range(NT)]
            for t in range(NT):
                for q in range(4):
                    src = q2[:, t, :, NOPE + (q % 2) * hr:NOPE + (q % 2 + 1) * hr]
                    ins = V.tensor_tensor(pr[t][q], src, on_heads(rope_q[:, q, t, :], hr), ALU.mult)
            own(ins)
            for t in range(NT):
                V.tensor_tensor(qpe[:, t, :, 0:hr], pr[t][0], pr[t][1], ALU.subtract)
                ins = V.tensor_tensor(qpe[:, t, :, hr:ROPE], pr[t][2], pr[t][3], ALU.add)
            ins.then_inc(ev["qpe_ready"], 1)
            for r in range(4):
                rr = RD["q2"] + r
                dve.wait_ge(s_tr, rr + 1)
                V.tensor_scalar(qT[:, 2 * r:2 * r + 2, :], tp[rr % 2][:, :].rearrange("p (a n) -> p a n", a=2),
                                col("qnope"), None, ALU.mult).then_inc(s_tf[rr % 2], 1)
            for r in range(2):
                rr = RD["qpe"] + r
                dve.wait_ge(s_tr, rr + 1)
                V.tensor_copy(qpT[:, 2 * r:2 * r + 2, :], tp[rr % 2][:, :].rearrange("p (a n) -> p a n", a=2))\
                    .then_inc(s_tf[rr % 2], 1)
            attention("mla")
            add_steps(U_MO)
            operand("op_f2", [(c, col("ffn_norm", 8 + c)) for c in range(DC)])
            ffn(1, 3)
            add_ffn(U_F2)
            operand("op_f3", [(c, col("ffn_pre", c)) for c in range(DC)])
            ffn(2, 4)
            post_ffn(0, 0)
            V.memset(conv_u[:, :, 0:PAD], 0.0)
            V.memset(conv_u[:, :, PAD + T:], 0.0)
            operand("op_conv", [(c, col("mix_pre", c)) for c in range(DC)])
            def conv_taps(chunks_, k0, k1, ready=None):
                for k in range(k0, k1):
                    for c in chunks_:
                        w = col("w_dw", k * 8 + c)
                        if k == 0:
                            ins = V.tensor_scalar(conv_c[:, c, :], conv_u[:, c, 0:T], w, col("b_dw", c), ALU.mult, ALU.add)
                        else:
                            ins = V.scalar_tensor_tensor(out=conv_c[:, c, :], in0=conv_u[:, c, k:k + T], scalar=w,
                                                         in1=conv_c[:, c, :], op0=ALU.mult, op1=ALU.add)
                    if k < k1 - 1 or ready is None:
                        own(ins)
                if ready is not None:
                    ins.then_inc(ready, 1)

            for w, chunks in enumerate(PW1):
                u = U_PW1 + w
                lo_b(u)
                lo_a(u + 1)
                if w == 0:
                    norm_rows("r_conv", 5)
                for m, q in enumerate(chunks):
                    if q % 2:
                        c = q // 2
                        pw1_ready(dve, u, m, c)
                        V.tensor_tensor(gu[:, c % 2, :].rearrange("p (h n) -> p h n", h=2), gate_up_bank[c % 2], both, ALU.mult)\
                            .then_inc(s_cgu, 1)
                        if 2 <= c < 7:
                            dve.wait_ge(s_glu, 2)
                            conv_taps((0, 1), EARLY * (c - 2), EARLY * (c - 1))
                        dve.wait_ge(s_sig, c + 1)
                        V.scalar_tensor_tensor(out=conv_u[:, c, PAD:PAD + T], in0=gu[:, c % 2, 0:T], scalar=col("b_pw1", c),
                                               in1=sg[:, c % 2, :], op0=ALU.add, op1=ALU.mult).then_inc(s_glu, 1)
            dve.wait_ge(s_glu, 8)
            conv_taps((0, 1), 5 * EARLY, TAPS, ready=ev["conv_early"])
            conv_taps(range(2, CONV_DVE), 0, SPLIT)
            conv_taps(range(2, SHARED), SPLIT, TAPS)
            dve.wait_ge(ev["conv_summed"], 2)
            V.tensor_tensor(conv_c[:, SHARED, :], conv_c[:, SHARED, :], acc[1][:, 0:T], ALU.add).then_inc(ev["conv_ready"], 1)
            dve.wait_ge(ev["mean_done"], 1)
            mean = acc[0][:, 0:T].unsqueeze(1).to_broadcast([P, 4, T])
            for q in range(2):
                h = slice(4 * q, 4 * q + 4)
                V.tensor_tensor(conv_c[:, h, :], conv_c[:, h, :], mean, ALU.subtract).then_inc(ev["centred"], 1)
            dve.wait_ge(ev["conv_std"], 1)
            own(V.reciprocal(conv_r[:, 1, :], conv_r[:, 0, :]))
            dve.wait_ge(ev["centred"], 2)
            for q in range(5):
                if q < 4:
                    h = slice(2 * q, 2 * q + 2)
                    V.tensor_tensor(conv_c[:, h, :], conv_c[:, h, :], conv_r[:, 1, :].unsqueeze(1).to_broadcast([P, 2, T]),
                                    ALU.mult).then_inc(ev["lny_ready"], 1)
                if q >= 1:
                    h = slice(2 * q - 2, 2 * q)
                    dve.wait_ge(ev["conv_hi"], q)
                    V.tensor_tensor(htlo[:, h, :], conv_s[:, h, :], hthi[:, h, :].bitcast(F32), ALU.subtract)\
                        .then_inc(ev["conv_lo"], 1)
            dve.wait_ge(s_ldw[1], 16)
            mixer_out(U_PW2, lambda sl: wide[:, 1, sl])
            post_mixer(1, 2, U_PW2)
            operand("op_f4", [(c, col("ffn_pre", 8 + c)) for c in range(DC)])
            ffn(3, 6)
            post_ffn(2, 3)
            operand("op_f5", [(c, col("ffn_pre", 16 + c)) for c in range(DC)])
            ffn(4, 7)
            post_ffn(3, 4)
            lv = rows[:, RO["lambda"]:RO["lambda"] + 256].rearrange("p (a b n) -> p a b n", a=2, b=2)
            own(V.tensor_tensor(lamt[:, :].rearrange("p (a n) -> p a n", a=2), lv[:, :, 0, :], lv[:, :, 1, :], ALU.mult))
            V.tensor_reduce(lam[:, 0:2], lamt[:, :].rearrange("p (a n) -> p a n", a=2), AX, ALU.add).then_inc(ev["lam_sum"], 1)
            operand("op_qkv", [(c, col("mix_pre", 8 + c)) for c in range(DC)])
            def q3_copies(first):
                for r in (first, first + 1):
                    rr = RD["q3"] + r
                    dve.wait_ge(s_tr, rr + 1)
                    V.tensor_scalar(qT[:, 2 * r:2 * r + 2, :], tp[rr % 2][:, :].rearrange("p (a n) -> p a n", a=2),
                                    DH ** -0.5, None, ALU.mult).then_inc(s_tf[rr % 2], 1)

            for u in range(U_QKV, U_QKV + 8):
                step(u, lambda t, u, c, w: p3[:, t, (u - U_QKV) * PITCH + c:(u - U_QKV) * PITCH + c + w], 8, u == U_QKV)
                if QK3.get(u - U_QKV, ("",))[0] == "q3":
                    q3_copies(QK3[u - U_QKV][1])
            dve.wait_ge(ev["lam_exp"], 1)
            own(V.tensor_tensor(lam[:, 5:6], lam[:, 3:4], lam[:, 2:3], ALU.subtract))
            own(V.tensor_scalar(lam[:, 4:5], lam[:, 5:6], -LAMBDA_INIT, None, ALU.add))
            V.tensor_scalar(sgain[:, :], col("subln"), 1.0 - LAMBDA_INIT, None, ALU.mult)
            attention("diff")
            rstd("subln", 16)
            ov = proj[:, 0:2048].rearrange("p (t h n) -> p t h n", t=NT, h=H3)
            rv = rs[:, 0:16].rearrange("p (t h) -> p t h", t=NT)
            for h in range(2):
                hs = slice(4 * h, 4 * h + 4)
                V.tensor_tensor(ov[:, :, hs, :], ov[:, :, hs, :], rv[:, :, hs].unsqueeze(3).to_broadcast([P, NT, 4, P]), ALU.mult)\
                    .then_inc(ev["sub_ready"], 1)
            operand("op_wo", [(c, sgain[:, 0:1]) for c in range(DC)])
            mixer_out(U_WO)
            post_mixer(4, 5, U_WO)
            operand("op_f6", [(c, col("ffn_pre", 24 + c)) for c in range(DC)])
            ffn(5, 9)
            post_ffn(5, 6)


def chunks(w, pitch=None):
    k, n = w.shape
    pitch = pitch or n
    out = np.zeros((P, k // P, pitch), w.dtype)
    out[:, :, :n] = w.reshape(k // P, P, n).transpose(1, 0, 2)
    return out


def lay_stream(a):
    s = np.zeros((UNITS, P, UNIT), np.float32)

    def projection(u0, w, width=PITCH):
        for i in range(-(-w.shape[1] // width)):
            part = w[:, i * width:(i + 1) * width]
            pitch = STEPS[u0 + i][1]
            rows_ = part.shape[0] // P
            for k in range(rows_):
                s[u0 + i, :, k * pitch:k * pitch + part.shape[1]] = part[k * P:(k + 1) * P]

    def ffn(u0, gate, up, down):
        for c in range(FC):
            sl = slice(c * P, (c + 1) * P)
            s[u0 + c, :, 0:1024] = chunks(gate[:, sl]).reshape(P, 1024)
            s[u0 + c, :, 1024:2048] = chunks(up[:, sl]).reshape(P, 1024)
            s[u0 + c, :, 2048:] = down[sl]

    projection(U_IN, a["a_w_in"][0])
    w1 = np.concatenate([chunks(a["a_cmp_k_w1"][0]), chunks(a["a_cmp_v_w1"][0])], 1).reshape(P, -1)
    for i in range(3):
        part = w1[:, i * UNIT:(i + 1) * UNIT]
        s[U_CMP + i, :, :part.shape[1]] = part
    projection(U_OUT, a["a_w_out"][0])
    for i in range(2):
        ffn((U_F1, U_F2)[i], a["ffn_w_gate_up"][i][:, :FF], a["ffn_w_gate_up"][i][:, FF:], a["ffn_w_down"][i])
    projection(U_KVA, a["kv_w_a"])
    projection(U_QA, a["b_w_q_a"][0])
    projection(U_KVB, a["kv_w_b"], 1024)
    projection(U_QB, a["b_w_q_b"][0], 768)
    projection(U_MO, a["b_w_out"][0])
    for i, u in enumerate((U_F3, U_F4, U_F5, U_F6)):
        ffn(u, a["ffn_w_gate_2"][i // 2, i % 2], a["ffn_w_up_2"][i // 2, i % 2], a["ffn_w_down_2"][i // 2, i % 2])
    pw1 = a["conv_w_pw1_2"][0]
    for w, qs in enumerate(PW1):
        for m, q in enumerate(qs):
            c0 = (q % 2) * D + (q // 2) * P
            s[U_PW1 + w, :, m * 1024:(m + 1) * 1024] = chunks(pw1[:, c0:c0 + P]).reshape(P, 1024)
    projection(U_PW2, a["conv_w_pw2_2"][0])
    projection(U_QKV, a["attn_w_qkv_2"][0])
    projection(U_WO, a["attn_w_o_2"][0])
    return s


def lay_cols(a):
    def v(x):
        return x.reshape(-1, P).T

    def twice(x):
        return np.concatenate([x, x])[:, None]

    parts = {
        "attn_norm": v(a["a_attn_norm"]), "kv_norm": v(a["kv_norm"]), "b_attn_norm": v(a["b_attn_norm"]),
        "ffn_norm": v(a["ffn_norm"]), "ffn_pre": v(a["ffn_norm_pre_2"]), "mix_pre": v(a["mix_norm_pre_2"]),
        "q_norm": twice(a["a_q_norm"][0]), "kcmp_norm": twice(a["a_kcmp_norm"][0]),
        "kslc_norm": twice(a["a_kslc_norm"][0]), "kwin_norm": twice(a["a_kwin_norm"][0]),
        "b1": np.concatenate([v(a["a_cmp_k_b1"]), v(a["a_cmp_v_b1"])], 1),
        "pos": np.concatenate([v(a["a_cmp_pos_k"]), v(a["a_cmp_pos_v"])], 1),
        "w2": np.concatenate([chunks(a["a_cmp_k_w2"][0]).reshape(P, -1), chunks(a["a_cmp_v_w2"][0]).reshape(P, -1)], 1),
        "kv_c_norm": v(a["kv_c_norm"]), "q_a_norm": v(a["b_q_a_norm"]),
        "knope": a["kv_k_norm"][:NOPE, None], "qnope": a["b_q_norm"][0, :NOPE, None],
        "b_pw1": v(a["conv_b_pw1_2"]), "ln_g": v(a["conv_ln_g_2"]), "ln_b": v(a["conv_ln_b_2"]),
        "b_dw": v(a["conv_b_dw_2"]), "w_dw": v(a["conv_w_dw_2"]), "subln": v(a["attn_subln_g_2"]),
    }
    return np.ascontiguousarray(np.concatenate([parts[n] for n, _ in COLS], 1))


def lay_rows(a):
    return np.concatenate([a["kv_k_norm"][NOPE:], a["b_q_norm"][0, NOPE:], a["attn_lambda_q1_2"][0], a["attn_lambda_k1_2"][0],
                           a["attn_lambda_q2_2"][0], a["attn_lambda_k2_2"][0]])[None]


def lay_wide(a):
    post, mix = a["ffn_norm_post_2"], a["mix_norm_post_2"]
    return np.stack([post[0, 0], a["conv_b_pw2_2"][0], mix[0], post[0, 1], post[1, 0], mix[1], post[1, 1]])


def shape_constants():
    f = np.float32
    tok, key = np.arange(T), np.arange(T)
    allowed = key[None, :] <= tok[:, None]
    dist = (key[None, :] - tok[:, None]).astype(f)

    def tiles(m):
        return m.reshape(NT, P, -1).transpose(1, 0, 2).reshape(P, -1).astype(f)

    j = np.arange(NCMP)
    end, mid = j * CMP_STRIDE + CMP_BLOCK - 1, (j * CMP_STRIDE).astype(f) + f(0.5 * (CMP_BLOCK - 1))
    biasc = np.full((T, H1, G1, NCMP), f(-1e30))
    for h in range(H1):
        b = -f(SLOPES1[h]) * (tok.astype(f)[:, None] - mid[None, :])
        biasc[:, h, h // (H1 // G1)] = np.where(end[None, :] <= tok[:, None], b, f(-1e30))
    inv = f(10000.0) ** (-np.arange(0, ROPE, 2, dtype=f) / f(ROPE))
    ang = tok.astype(f)[:, None] * inv[None, :]
    parts = {
        "ident": np.eye(P, dtype=f), "ones": np.full((P, P), f(1.0 / D)),
        "causal": tiles(np.where(allowed, dist, f(-1e32))), "mask": tiles(np.where(allowed, f(0), f(-1e30))),
        "dist": tiles(np.abs(dist)), "biasc": tiles(biasc.reshape(T, -1)),
        "valid": tiles((tok >= CMP_BLOCK - 1).astype(f)[:, None]), "cos": tiles(np.cos(ang)), "sin": tiles(np.sin(ang)),
    }
    out = np.zeros((P, NCONST), f)
    for name, m in parts.items():
        out[:, KO[name]:KO[name] + m.shape[1]] = m
    return out


def kernel(**inputs):
    import concourse.bacc as bacc
    from concourse.bass_utils import run_bass_kernel_spmd

    a = {k: np.asarray(v) for k, v in inputs.items()}
    arrays = {
        "in_stream": lay_stream(a), "in_cols": lay_cols(a), "in_rows": lay_rows(a), "in_wide": lay_wide(a),
        "in_x": np.ascontiguousarray(a["x"][0]), "in_const": shape_constants(),
    }
    nc = bacc.Bacc("TRN2", target_bir_lowering=False, num_devices=1)
    args = [nc.dram_tensor(k, v.shape, mybir.dt.from_np(v.dtype), kind="ExternalInput").ap() for k, v in arrays.items()]
    args.append(nc.dram_tensor("out_0", (T, D), F32, kind="ExternalOutput").ap())
    build(nc, *args)
    r = run_bass_kernel_spmd(nc, [arrays], core_ids=[0])
    return r.results[0]["out_0"].reshape(1, T, D)
```
